# Optimizing a Trainium2 kernel written in Bass

```python
import jax, jax.numpy as jnp
from jax import lax
import numpy as np
import math

D_MODEL = 1024
BATCH = 1
SEQ = 512
DEPTH = 2

N_MIXERS = 2
PLE_DIM = 256
ATT_HEADS = 16
ATT_HEAD_DIM = 64
ATT_WIDTH = ATT_HEADS * ATT_HEAD_DIM
QUERY_BLOCK = 128
REC_HEADS = 8
REC_KEY_DIM = 128
REC_VAL_DIM = 128
REC_WIDTH = REC_HEADS * REC_KEY_DIM
REC_VWIDTH = REC_HEADS * REC_VAL_DIM
CHUNK = 64
N_ATT_LAYERS = (DEPTH + 1) // 2
N_REC_LAYERS = DEPTH // 2
EPS = 1e-6


def rms_norm(x, gain):
    xf = x.astype(jnp.float32)
    y = xf * lax.rsqrt(jnp.mean(xf * xf, axis=-1, keepdims=True) + EPS)
    return (y * gain.astype(jnp.float32)).astype(x.dtype)

def fox_attention(q, k, v, c):
    B, H, S, hd = q.shape
    scale = hd ** -0.5
    kpos = jnp.arange(S)

    def block(i):
        start = i * QUERY_BLOCK
        qb = lax.dynamic_slice_in_dim(q, start, QUERY_BLOCK, axis=2)
        cb = lax.dynamic_slice_in_dim(c, start, QUERY_BLOCK, axis=2)
        s = jnp.einsum('bhqd,bhkd->bhqk', qb, k).astype(jnp.float32) * scale
        s = s + (cb[..., :, None] - c[..., None, :])
        qpos = start + jnp.arange(QUERY_BLOCK)
        s = jnp.where(kpos[None, :] <= qpos[:, None], s, -jnp.inf)
        w = jax.nn.softmax(s, axis=-1)
        return jnp.einsum('bhqk,bhkd->bhqd', w.astype(v.dtype), v)

    out = lax.map(block, jnp.arange(S // QUERY_BLOCK))
    return out.transpose(1, 0, 3, 2, 4).reshape(B, S, H * hd)

def fox_mixer(u, w_in, b_f, w_out):
    B, S, _ = u.shape
    proj = u @ w_in
    q, k, v, g, fl = jnp.split(proj, [ATT_WIDTH, 2 * ATT_WIDTH, 3 * ATT_WIDTH, 4 * ATT_WIDTH], axis=-1)
    heads = lambda t: t.reshape(B, S, ATT_HEADS, ATT_HEAD_DIM).transpose(0, 2, 1, 3)
    log_f = jax.nn.log_sigmoid(fl.astype(jnp.float32) + b_f.astype(jnp.float32))
    c = jnp.cumsum(log_f, axis=1).transpose(0, 2, 1)
    attn = fox_attention(heads(q), heads(k), heads(v), c)
    return (attn * jax.nn.silu(g)) @ w_out

def hgrn2_mixer(u, w_in, lb, out_gain, w_out):
    B, S, _ = u.shape
    proj = u @ w_in
    q, fl, inp, g = jnp.split(proj, [REC_WIDTH, 2 * REC_WIDTH, 2 * REC_WIDTH + REC_VWIDTH], axis=-1)
    lbf = lb.astype(jnp.float32)
    log_f = jnp.logaddexp(jnp.log(lbf), jnp.log1p(-lbf) + jax.nn.log_sigmoid(fl.astype(jnp.float32)))
    k = -jnp.expm1(log_f)

    def chunks(t, dh):
        return t.astype(jnp.float32).reshape(B, S // CHUNK, CHUNK, REC_HEADS, dh).transpose(1, 0, 3, 2, 4)

    qc, kc, gc = chunks(q, REC_KEY_DIM), chunks(k, REC_KEY_DIM), chunks(log_f, REC_KEY_DIM)
    ic = chunks(inp, REC_VAL_DIM)
    causal = jnp.tril(jnp.ones((CHUNK, CHUNK), dtype=bool))

    def step(state, xs):
        qb, kb, gb, ib = xs
        b = jnp.cumsum(gb, axis=-2)
        diff = b[..., :, None, :] - b[..., None, :, :]
        decay = jnp.exp(jnp.where(causal[:, :, None], diff, -jnp.inf))
        scores = jnp.einsum('bhtd,bhsd,bhtsd->bhts', qb, kb, decay)
        o = scores @ ib + jnp.einsum('bhtd,bhdv->bhtv', qb * jnp.exp(b), state)
        b_last = b[..., -1:, :]
        state = jnp.exp(b_last[..., 0, :])[..., None] * state + \
            jnp.einsum('bhsd,bhsv->bhdv', kb * jnp.exp(b_last - b), ib)
        return state, o

    state0 = jnp.zeros((B, REC_HEADS, REC_KEY_DIM, REC_VAL_DIM), jnp.float32)
    _, o = lax.scan(step, state0, (qc, kc, gc, ic))
    o = o.transpose(1, 0, 3, 2, 4).reshape(B, S, REC_HEADS, REC_VAL_DIM)
    o = o * lax.rsqrt(jnp.mean(o * o, axis=-1, keepdims=True) + EPS) * out_gain.astype(jnp.float32)
    gh = g.astype(jnp.float32).reshape(B, S, REC_HEADS, REC_VAL_DIM)
    y = (o * jax.nn.silu(gh)).reshape(B, S, REC_VWIDTH).astype(u.dtype)
    return y @ w_out

def first_inputs(seed: int = 0) -> dict:
    key = jax.random.key(seed)
    ks = jax.random.split(key, 14)
    nrm = jax.random.normal
    D = D_MODEL
    return {
        "x": nrm(ks[0], (BATCH, SEQ, D), jnp.float32),
        "p": nrm(ks[1], (DEPTH, BATCH, SEQ, PLE_DIM), jnp.float32),
        "norm_pre": 1.0 + 0.05 * nrm(ks[2], (DEPTH, D), jnp.float32),
        "norm_post": 1.0 + 0.05 * nrm(ks[3], (DEPTH, D), jnp.float32),
        "att_w_in": nrm(ks[4], (N_ATT_LAYERS, D, 4 * ATT_WIDTH + ATT_HEADS), jnp.float32) * D ** -0.5,
        "att_b_f": jax.random.uniform(ks[5], (N_ATT_LAYERS, ATT_HEADS), jnp.float32, 1.0, 6.0),
        "att_w_out": nrm(ks[6], (N_ATT_LAYERS, ATT_WIDTH, D), jnp.float32) * ATT_WIDTH ** -0.5,
        "rec_w_in": nrm(ks[7], (N_REC_LAYERS, D, 2 * REC_WIDTH + 2 * REC_VWIDTH), jnp.float32) * D ** -0.5,
        "rec_lb": 1.0 + 0.1 * nrm(ks[8], (DEPTH, REC_WIDTH), jnp.float32),
        "rec_out_norm": 1.0 + 0.05 * nrm(ks[9], (N_REC_LAYERS, REC_VAL_DIM), jnp.float32),
        "rec_w_out": nrm(ks[10], (N_REC_LAYERS, REC_VWIDTH, D), jnp.float32) * REC_VWIDTH ** -0.5,
        "ple_w_proj": nrm(ks[11], (DEPTH, PLE_DIM, D), jnp.float32) * PLE_DIM ** -0.5,
        "ple_w_gate": nrm(ks[12], (DEPTH, D, D), jnp.float32) * D ** -0.5,
    }

def first_block(x, p, norm_pre, norm_post, att_w_in, att_b_f, att_w_out, rec_w_in, rec_lb,
              rec_out_norm, rec_w_out, ple_w_proj, ple_w_gate):
    sm = jax.nn.softmax(rec_lb.astype(jnp.float32), axis=0)
    lower_bounds = jnp.cumsum(sm, axis=0) - sm[0:1]
    h = x
    for layer in range(DEPTH):
        u = rms_norm(h, norm_pre[layer])
        j = layer // N_MIXERS
        if layer % N_MIXERS == 0:
            y = fox_mixer(u, att_w_in[j], att_b_f[j], att_w_out[j])
        else:
            y = hgrn2_mixer(u, rec_w_in[j], lower_bounds[layer], rec_out_norm[j], rec_w_out[j])
        h = h + rms_norm(y, norm_post[layer])
        gate = jax.nn.sigmoid((h @ ple_w_gate[layer]).astype(jnp.float32)).astype(h.dtype)
        h = h + (p[layer] @ ple_w_proj[layer]) * gate
    return h


DEPTH_2 = 1

HEAD_DIM = 64
N_HEADS_A = 8
N_HEADS_B = 8
WIDTH_A = N_HEADS_A * HEAD_DIM
WIDTH_B = N_HEADS_B * HEAD_DIM
ROPE_DIM = HEAD_DIM // 4
ROPE_THETA = 500000.0
IDX_HEADS = 8
IDX_DIM = 64
TOPK_MAX = 256
BLOCK_Q = 128
D_FF = 4 * D_MODEL
IN_SPLITS = (WIDTH_A, WIDTH_A, WIDTH_A,
             WIDTH_B, WIDTH_B, WIDTH_B,
             IDX_HEADS * IDX_DIM, IDX_DIM,
             IDX_HEADS,
             D_MODEL, D_MODEL)
IN_COLS = sum(IN_SPLITS)


def rmsnorm(x, g):
    x32 = x.astype(jnp.float32)
    y = x32 * lax.rsqrt(jnp.mean(x32 * x32, axis=-1, keepdims=True) + EPS)
    return (y * g.astype(jnp.float32)).astype(x.dtype)

def rope_tables(seq_len):
    pos = jnp.arange(seq_len, dtype=jnp.float32)
    inv_freq = ROPE_THETA ** (-jnp.arange(0, ROPE_DIM, 2, dtype=jnp.float32) / ROPE_DIM)
    ang = pos[:, None] * inv_freq[None, :]
    return jnp.cos(ang), jnp.sin(ang)

def partial_rope(x, cos, sin):
    half = ROPE_DIM // 2
    x1 = x[..., :half]
    x2 = x[..., half:ROPE_DIM]
    cos = cos.astype(x.dtype)
    sin = sin.astype(x.dtype)
    return jnp.concatenate([x1 * cos - x2 * sin, x2 * cos + x1 * sin, x[..., ROPE_DIM:]], axis=-1)

def to_blocks(a, nblk):
    return a.reshape((a.shape[0], nblk, BLOCK_Q) + a.shape[2:]).swapaxes(0, 1)

def from_blocks(a):
    a = a.swapaxes(0, 1)
    return a.reshape((a.shape[0], a.shape[1] * a.shape[2]) + a.shape[3:])

def token_mixers(q_a, k_a, v_a, q_b, k_b, v_b, q_i, k_i, w_i):
    L = q_a.shape[1]
    nblk = L // BLOCK_Q
    topk = min(TOPK_MAX, L // 4)
    f32 = jnp.float32
    key_pos = jnp.arange(L, dtype=jnp.int32)
    scale = HEAD_DIM ** -0.5
    idx_scale = (IDX_DIM ** -0.5) * (IDX_HEADS ** -0.5)

    def block_fn(args):
        qa, qi, wi, qb, t0 = args
        t = t0 + jnp.arange(BLOCK_Q, dtype=jnp.int32)
        rel = jax.nn.relu(jnp.einsum('bqhd,bsd->bqhs', qi, k_i).astype(f32))
        isc = jnp.einsum('bqhs,bqh->bqs', rel, wi.astype(f32)) * idx_scale
        causal = key_pos[None, :] <= t[:, None]
        isc = jnp.where(causal[None], isc, -jnp.inf)
        _, sel = lax.top_k(isc, topk)
        valid = sel <= t[None, :, None]
        kg = jax.vmap(lambda kb, ib: kb[ib])(k_a, sel)
        vg = jax.vmap(lambda vb, ib: vb[ib])(v_a, sel)
        logit = jnp.einsum('bqhd,bqkhd->bqhk', qa, kg).astype(f32) * scale
        logit = jnp.where(valid[:, :, None, :], logit, -jnp.inf)
        p = jax.nn.softmax(logit, axis=-1).astype(vg.dtype)
        oa = jnp.einsum('bqhk,bqkhd->bqhd', p, vg)
        z = jnp.einsum('bqhd,bshd->bhqs', qb, k_b).astype(f32) * scale
        strict = (key_pos[None, :] < t[:, None])[None, None]
        log_1mb = jnp.where(strict, jax.nn.log_sigmoid(-z), 0.0)
        after = lax.cumsum(log_1mb, axis=3, reverse=True) - log_1mb
        att = jnp.where(strict, jnp.exp(jax.nn.log_sigmoid(z) + after), 0.0)
        ob = jnp.einsum('bhqs,bshd->bqhd', att.astype(v_b.dtype), v_b)
        return oa, ob

    starts = jnp.arange(nblk, dtype=jnp.int32) * BLOCK_Q
    oa, ob = lax.map(block_fn, (to_blocks(q_a, nblk), to_blocks(q_i, nblk),
                                to_blocks(w_i, nblk), to_blocks(q_b, nblk), starts))
    return from_blocks(oa), from_blocks(ob)

def second_inputs(seed: int = 0) -> dict:
    key = jax.random.key(seed)
    ks = jax.random.split(key, 16)
    f32 = jnp.float32
    nrm = lambda k, shape, fan_in: jax.random.normal(k, shape, f32) * (fan_in ** -0.5)
    gain = lambda k: 1.0 + 0.05 * jax.random.normal(k, (DEPTH_2, D_MODEL), f32)
    return {
        "x": jax.random.normal(ks[0], (BATCH, SEQ, D_MODEL), f32),
        "c": jax.random.normal(ks[1], (BATCH, D_MODEL), f32),
        "w_ada": nrm(ks[2], (DEPTH_2, D_MODEL, 6 * D_MODEL), D_MODEL),
        "b_ada": 0.01 * jax.random.normal(ks[3], (DEPTH_2, 6 * D_MODEL), f32),
        "g_pre_mix": gain(ks[4]),
        "w_in": nrm(ks[5], (DEPTH_2, D_MODEL, IN_COLS), D_MODEL),
        "w_up_a": nrm(ks[6], (DEPTH_2, WIDTH_A, D_MODEL), WIDTH_A),
        "w_up_b": nrm(ks[7], (DEPTH_2, WIDTH_B, D_MODEL), WIDTH_B),
        "w_out": nrm(ks[8], (DEPTH_2, D_MODEL, D_MODEL), D_MODEL),
        "g_post_mix": gain(ks[9]),
        "g_pre_ffn": gain(ks[10]),
        "w_ff1": nrm(ks[11], (DEPTH_2, D_MODEL, D_FF), D_MODEL),
        "w_ff2": nrm(ks[12], (DEPTH_2, D_FF, D_MODEL), D_FF),
        "g_post_ffn": gain(ks[13]),
    }

def second_block(x, c, w_ada, b_ada, g_pre_mix, w_in, w_up_a, w_up_b, w_out, g_post_mix,
              g_pre_ffn, w_ff1, w_ff2, g_post_ffn):
    B, L, D = x.shape
    cos, sin = rope_tables(L)
    cos_h, sin_h = cos[:, None, :], sin[:, None, :]
    split_at = list(np.cumsum(IN_SPLITS)[:-1])
    for l in range(DEPTH_2):
        mod = jax.nn.silu(c) @ w_ada[l] + b_ada[l]
        sh1, sc1, ga1, sh2, sc2, ga2 = [m[:, None, :] for m in jnp.split(mod, 6, axis=-1)]

        h = rmsnorm(x, g_pre_mix[l]) * (1.0 + sc1) + sh1
        proj = h @ w_in[l]
        qa, ka, va, qb, kb, vb, qi, ki, wi, gate_a, gate_b = jnp.split(proj, split_at, axis=-1)
        heads = lambda t, n: t.reshape(B, L, n, HEAD_DIM)
        qa = partial_rope(heads(qa, N_HEADS_A), cos_h, sin_h)
        ka = partial_rope(heads(ka, N_HEADS_A), cos_h, sin_h)
        va = heads(va, N_HEADS_A)
        qb, kb, vb = heads(qb, N_HEADS_B), heads(kb, N_HEADS_B), heads(vb, N_HEADS_B)
        qi = partial_rope(qi.reshape(B, L, IDX_HEADS, IDX_DIM), cos_h, sin_h)
        ki = partial_rope(ki, cos, sin)
        oa, ob = token_mixers(qa, ka, va, qb, kb, vb, qi, ki, wi)
        ya = oa.reshape(B, L, WIDTH_A) @ w_up_a[l]
        yb = ob.reshape(B, L, WIDTH_B) @ w_up_b[l]
        merged = jax.nn.sigmoid(gate_a) * ya + jax.nn.sigmoid(gate_b) * yb
        y = merged @ w_out[l]
        x = x + ga1 * rmsnorm(y, g_post_mix[l])

        h = rmsnorm(x, g_pre_ffn[l]) * (1.0 + sc2) + sh2
        u = jax.nn.relu(h @ w_ff1[l])
        y = (u * u) @ w_ff2[l]
        x = x + ga2 * rmsnorm(y, g_post_ffn[l])
    return x


def setup_inputs(seed=0):
    out = dict(first_inputs(seed))
    for name, value in second_inputs(seed + 1).items():
        if name != "x":
            out[name + "_2"] = value
    return out


def reference(
    x, p, norm_pre, norm_post, att_w_in, att_b_f, att_w_out, rec_w_in, rec_lb, rec_out_norm,
    rec_w_out, ple_w_proj, ple_w_gate, c_2, w_ada_2, b_ada_2, g_pre_mix_2, w_in_2, w_up_a_2,
    w_up_b_2, w_out_2, g_post_mix_2, g_pre_ffn_2, w_ff1_2, w_ff2_2, g_post_ffn_2,
):
    x = first_block(
        x, p, norm_pre, norm_post, att_w_in, att_b_f, att_w_out, rec_w_in, rec_lb, rec_out_norm,
        rec_w_out, ple_w_proj, ple_w_gate,
    )
    return second_block(
        x, c_2, w_ada_2, b_ada_2, g_pre_mix_2, w_in_2, w_up_a_2, w_up_b_2, w_out_2,
        g_post_mix_2, g_pre_ffn_2, w_ff1_2, w_ff2_2, g_post_ffn_2,
    )


_drawn_inputs = setup_inputs


def setup_inputs(seed=0):
    import zlib

    import numpy as np

    out = dict(_drawn_inputs(seed))
    spreads = {}
    factors = {'b_ada_2': 4.807, 'g_post_mix_2': 3.677, 'g_pre_ffn_2': 3.712, 'g_post_ffn_2': 3.82}
    for name, (base, spread) in spreads.items():
        noise = np.random.default_rng([zlib.crc32(name.encode()), seed]).standard_normal(out[name].shape)
        drawn = base * np.exp(spread * noise) if base else spread * noise
        out[name] = __import__('jax').numpy.asarray(drawn.astype(out[name].dtype))
    for name, factor in factors.items():
        out[name] = (out[name] * factor).astype(out[name].dtype)
    return out
```

```python
from contextlib import ExitStack

import numpy as np

import concourse.bass as bass
from concourse import mybir

P = 128
T = 512
TT = T // P
D = 1024
KT = D // P
G = 512
HD = 64
NEG = -3.0e38
EPS = 1e-6
TOPK = min(256, T // 4)
ISCALE = (64 ** -0.5) * (8 ** -0.5)
KOFF = [0, 128, 384, 768]
F32 = mybir.dt.float32
F32R = mybir.dt.float32r
I32 = mybir.dt.int32
ALU = mybir.AluOpType
ACT = mybir.ActivationFunctionType
AX = mybir.AxisListType

STAGES = [
    ("norm0", 8, 0, 8, 8), ("qkv0", 24, 12, 0, 0), ("g0", 8, 4, 8, 8), ("out0", 8, 4, 0, 0),
    ("ht0", 8, 0, 8, 8), ("pt0", 2, 0, 2, 2), ("ple0", 16, 6, 8, 0),
    ("norm1", 8, 0, 8, 8), ("qfi1", 24, 12, 8, 0), ("on1", 8, 0, 0, 0), ("g1", 8, 4, 8, 8),
    ("out1", 8, 4, 0, 0), ("ht1", 8, 0, 8, 8), ("pt1", 2, 0, 2, 2), ("ple1", 16, 6, 8, 0),
    ("norm2", 8, 0, 8, 8), ("qi2", 8, 2, 4, 0), ("qka2", 16, 4, 8, 0), ("va2", 4, 2, 0, 0),
    ("b2", 12, 6, 0, 0), ("merge2", 32, 12, 16, 8), ("out2", 8, 4, 0, 0), ("ga2_0", 2, 0, 0, 0),
    ("norm3", 8, 0, 8, 8), ("ffn", 96, 32, 96, 32), ("ga2_1", 2, 0, 0, 0),
]
BASE, _at = {}, [0, 0, 0, 0]
for _name, *_use in STAGES:
    BASE[_name] = tuple(_at)
    _at = [a + b for a, b in zip(_at, _use)]
CHUNKS = _at[1]


class Chain:

    def __init__(self, eng, sem):
        self.eng, self.sem, self.n, self.turn = eng, sem, 0, None

    def mark(self, ins):
        self.n += 1
        ins.then_inc(self.sem, 1)

    def wait(self):
        self.eng.wait_ge(self.sem, self.n if self.turn is None else self.turn + self.n)

    def after(self, ins):
        self.mark(ins)
        self.wait()

    def enter(self, i, per):
        self.start, self.per, self.turn = self.n, per, i * per

    def leave(self, turns):
        assert self.n == self.start + self.per, (self.n - self.start, self.per)
        self.n, self.turn = self.start + self.per * turns, None


def build(nc, a):
    ctx = ExitStack()
    with ctx:
        def sb(name, shape, dt=F32):
            return ctx.enter_context(nc.sbuf_tensor(name, shape, dt))

        def sem(name):
            return ctx.enter_context(nc.semaphore(name))

        h = sb("h", [P, TT, D])
        slot = {x: sb(f"slot_{x}", [P, 4096]) for x in "ABC"}
        d_at = nc.sbuf_base
        slot["D"] = sb("slot_D", [P, 4096])
        feat = {x: slot[x][:, :].rearrange("p (k t) -> p k t", k=KT) for x in "ABCD"}
        tok = {x: slot[x][:, :].rearrange("p (t d) -> p t d", t=TT) for x in "ABCD"}
        xh, xl = sb("xh", [P, KT, T], F32R), sb("xl", [P, KT, T], F32R)
        y_at = nc.sbuf_base
        yh = sb("yh", [P, KT, T], F32R)
        yl_at = nc.sbuf_base
        yl = sb("yl", [P, KT, T], F32R)
        wk = nc.alloc_sbuf_tensor_at("work_hi", [P, KT, T], F32, offset=y_at)
        wl = nc.alloc_sbuf_tensor_at("work_lo", [P, KT, T], F32, offset=yl_at)
        raw = [sb(f"w_raw{s}", [P, 4, G]) for s in range(2)]
        wh = [sb(f"w_hi{s}", [P, 4, G], F32R) for s in range(2)]
        wlo = [sb(f"w_lo{s}", [P, 4, G], F32R) for s in range(2)]
        ev = sb("ev", [P, 4, T])
        grow = sb("gain_row", [P, D])
        mask = sb("causal_mask", [P, T])
        ident = sb("ident", [P, P])
        gcol = sb("gain_cols", [P, 4, KT])
        modc = sb("mod_cols", [P, 48])
        ocol = sb("out_norm_col", [P, 1])
        lbc = sb("lb_cols", [P, 6, KT])
        stat = sb("stat", [P, 64])
        stat2 = sb("stat2", [P, 32])
        bfc = sb("b_f_col", [P, 1])
        sel = sb("head_select", [P, 16])
        m8 = sb("max8", [P, 8])
        zero = sb("zero", [P, 1])

        perm = slot["D"][:, 3072:3200]
        rope = [slot["D"][:, 2048:2560], slot["D"][:, 2560:3072]]
        rope_t = slot["D"][:, 3200:3264].rearrange("p (a t f) -> p a t f", a=2, t=TT)
        wsm = slot["D"][:, 0:576].rearrange("p (k n) -> p k n", k=KT)
        wsm_h = nc.alloc_sbuf_tensor_at("w_small_hi", [P, KT, 72], F32R, offset=d_at + 4 * 576)
        wsm_l = nc.alloc_sbuf_tensor_at("w_small_lo", [P, KT, 72], F32R, offset=d_at + 4 * 1152)
        tok_p = slot["C"][:, 0:1024].rearrange("p (t d) -> p t d", t=TT)
        tri, ones, strict, strict_neg = (grow[:, j * P:j * P + P] for j in range(4))
        z_t = slot["A"][:, 0:2048].rearrange("p (j t) -> p j t", j=TT)
        sp_t = slot["A"][:, 2048:4096].rearrange("p (j t) -> p j t", j=TT)
        at_t = slot["B"][:, 0:2048].rearrange("p (j t) -> p j t", j=TT)
        ln_t = slot["B"][:, 2048:4096].rearrange("p (j t) -> p j t", j=TT)
        isc = slot["A"][:, 2048:3328]
        level = ev[:, 0:2, :].rearrange("p a (l s) -> p (a l) s", l=4).bitcast(I32)

        ps = ctx.enter_context(nc.psum_tensor("banks", [P, 8, 512], F32))

        w_landed = [sem(f"w_landed{s}") for s in range(2)]
        w_split, w_ready, w_free = sem("w_split"), sem("w_ready"), sem("w_free")
        bank_full, bank_free = sem("bank_full"), sem("bank_free")
        ev_free, hi_done = sem("ev_free"), sem("hi_done")
        const_in, late_in = sem("const_in"), sem("late_in")
        dve_self, act_self = sem("dve_self"), sem("act_self")
        stored = sem("stored")
        apart = sem("apart")
        S = {}

        def sg(name):
            if name not in S:
                S[name] = sem(name)
            return S[name]

        def cols(w, c0, n=G, k0=0, kn=4):
            return w[k0 * P:(k0 + kn) * P, c0:c0 + n].rearrange("(k p) n -> p k n", p=P)

        win0, wout0 = a["att_w_in"][0], a["att_w_out"][0]
        win1, wout1 = a["rec_w_in"][0], a["rec_w_out"][0]
        win2, wout2 = a["w_in_2"][0], a["w_out_2"][0]
        wada = a["w_ada_2"][0]
        wff1, wff2 = a["w_ff1_2"][0], a["w_ff2_2"][0]

        ctx.enter_context(nc.allow_non_contiguous_dma(reason="small columns of gains"))
        block = ctx.enter_context(nc.Block())

        CONSTS = 15

        @block.sync
        def _(sp):
            for dst, src in (
                (ident[:, :], a["c_ident"]), (mask[:, :], a["c_mask"]), (sel[:, :], a["c_sel"]),
                (gcol[:, 0, :], a["norm_pre"][0].rearrange("(k p) -> p k", p=P)),
                (gcol[:, 1, :], a["norm_pre"][1].rearrange("(k p) -> p k", p=P)),
                (gcol[:, 2, :], a["g_pre_mix_2"][0].rearrange("(k p) -> p k", p=P)),
                (gcol[:, 3, :], a["g_pre_ffn_2"][0].rearrange("(k p) -> p k", p=P)),
                (modc[:, :], a["b_ada_2"][0].rearrange("(k p) -> p k", p=P)),
                (ocol[:, :], a["rec_out_norm"][0].rearrange("(p a) -> p a", a=1)),
                (lbc[:, 0:2, :], a["rec_lb"].rearrange("l (k p) -> p l k", p=P)),
                (stat[:, 32:40], a["c_2"][0].rearrange("(k p) -> p k", p=P)),
                (bfc[0:16, :], a["att_b_f"][0].rearrange("(p a) -> p a", a=1)),
                (bfc[32:48, :], a["att_b_f"][0].rearrange("(p a) -> p a", a=1)),
                (bfc[64:80, :], a["att_b_f"][0].rearrange("(p a) -> p a", a=1)),
                (bfc[96:112, :], a["att_b_f"][0].rearrange("(p a) -> p a", a=1)),
            ):
                sp.dma_start(dst, src).then_inc(const_in, 16)
            sp.dma_start(h[:, :, :], a["x"][0].rearrange("(t p) d -> p t d", p=P)).then_inc(sg("x_in"), 16)

            for c in range(24):
                if c >= 4:
                    sp.wait_ge(sg("ada_used"), c - 3)
                buf = slot["CD"[c % 4 // 2]][:, (c % 2) * 2048:(c % 2) * 2048 + 2048]
                sp.dma_start(buf.rearrange("p (k n) -> p k n", k=4), cols(wada, c // 2 * G, k0=4 * (c % 2)))\
                  .then_inc(sg(f"ada_landed{c % 4}"), 16)

            count = [0]

            def load(src, kn=4):
                c = count[0]
                sp.wait_ge(w_ready, c + 1)
                sp.dma_start(raw[c % 2][:, 0:kn, :], src).then_inc(w_landed[c % 2], 16)
                count[0] += 1

            def load_groups(w, n, c0=0):
                if n < 4:
                    for g in range(n):
                        load(cols(w, c0 + g * G))
                        load(cols(w, c0 + g * G, k0=4))
                    return
                first = count[0]
                with sp.Fori(0, n) as g:
                    for half in range(2):
                        sp.wait_ge(w_ready, 2 * g + (first + half + 1))
                        src = w[half * 4 * P:(half + 1) * 4 * P, bass.ds(g * G + c0, G)]
                        sp.dma_start(raw[half][:, :, :], src.rearrange("(k p) n -> p k n", p=P))\
                          .then_inc(w_landed[half], 16)
                count[0] += 2 * n

            def load_ple(l):
                for n in range(2):
                    load(cols(a["ple_w_gate"][l], n * G))
                    load(cols(a["ple_w_gate"][l], n * G, k0=4))
                    load(cols(a["ple_w_proj"][l], n * G, kn=2), kn=2)

            load_groups(win0, 6)
            load_groups(win0, 2, 3 * D)
            load_groups(wout0, 2)
            load_ple(0)
            load_groups(win1, 6)
            load_groups(win1, 2, 3 * D)
            load_groups(wout1, 2)
            load_ple(1)
            load_groups(win2, 1, 6 * G)
            load_groups(win2, 3)
            load_groups(win2, 3, 3 * G)
            for n in range(2):
                for gate, up in ((3656, a["w_up_a_2"][0]), (4680, a["w_up_b_2"][0])):
                    load(cols(win2, gate + n * G))
                    load(cols(win2, gate + n * G, k0=4))
                    load(cols(up, n * G))
            load_groups(wout2, 2)
            for i in range(9):
                if i < 8:
                    load(cols(wff1, i * G))
                    load(cols(wff1, i * G, k0=4))
                if i > 0:
                    load(cols(wff2, 0, k0=4 * (i - 1)))
                    load(cols(wff2, G, k0=4 * (i - 1)))
            assert count[0] == CHUNKS, (count[0], CHUNKS)
            sp.wait_ge(sg("final"), TT)
            sp.dma_start(a["out"][0].rearrange("(t p) d -> p t d", p=P), h[:, :, :]).then_inc(stored, 16)
            sp.wait_ge(stored, 16)

        @block.gpsimd
        def _(pool):
            pool.sem_inc(w_ready, 2)
            pool.memset(zero[:, :], 0.0).then_inc(w_split, 1)
            pool.wait_ge(w_split, 1)
            nothing = zero[:, :].unsqueeze(2).broadcast_to([P, 4, G])
            with pool.Fori(0, CHUNKS // 2) as i:
                for s in range(2):
                    pool.wait_ge(w_landed[s], 16 * i + 16)
                    pool.wait_ge(w_free, 2 * i + (s + 1))
                    pool.tensor_tensor(wh[s][:, :, :], raw[s][:, :, :], nothing, ALU.add).then_inc(w_split, 1)
                    pool.wait_ge(w_split, 2 * i + (s + 2))
                    pool.tensor_tensor(wlo[s][:, :, :], raw[s][:, :, :], wh[s][:, :, :].bitcast(F32), ALU.subtract)\
                        .then_inc(w_ready, 1)

        @block.tensor
        def _(pe):
            pe.sem_inc(w_free, 2)

            def bank(n):
                return ps[:, n % 8, :]

            def three(out, s, k, act_h, act_l, ak, m, feature_major, start, stop):
                cut = slice(m * P, m * P + P)
                if feature_major:
                    w_h, w_l, x_h, x_l = wh[s][:, k, cut], wlo[s][:, k, cut], act_h[:, ak, :], act_l[:, ak, :]
                    pe.matmul(out, w_h, x_h, start=start, stop=False)
                    pe.matmul(out, w_h, x_l, start=False, stop=False)
                    return pe.matmul(out, w_l, x_h, start=False, stop=stop)
                w_h, w_l, x_h, x_l = wh[s][:, k, :], wlo[s][:, k, :], act_h[:, ak, cut], act_l[:, ak, cut]
                pe.matmul(out, x_h, w_h, start=start, stop=False)
                pe.matmul(out, x_h, w_l, start=False, stop=False)
                return pe.matmul(out, x_l, w_h, start=False, stop=stop)

            def group(n, c, feature_major, act_h=xh, act_l=xl, a0=0, chunks=2, kn=4, static=0):
                n8, c2 = static
                for ch in range(chunks):
                    pe.wait_ge(w_ready, c + (ch + 3))
                    for m in range(4):
                        if ch == 0:
                            pe.wait_ge(bank_free, n + (m + 1))
                        for k in range(kn):
                            mm = three(ps[:, (n8 + m) % 8, :], (c2 + ch) % 2, k, act_h, act_l, a0 + 4 * ch + k, m,
                                       feature_major, ch == 0 and k == 0, ch == chunks - 1 and k == kn - 1)
                        if ch == chunks - 1:
                            mm.then_inc(bank_full, 1)
                            if m == 3:
                                pe.drain().then_inc(w_free, 1)
                        elif m == 3:
                            mm.then_inc(w_free, 1)

            def groups(name, count, kinds, skip=0, **kw):
                n0, c0 = BASE[name][0] + 4 * skip, BASE[name][1] + 2 * skip
                static = (n0 % 8, c0 % 2)
                if count >= 4:
                    with pe.Fori(0, count // 2) as i:
                        for half in range(2):
                            group(8 * i + (n0 + 4 * half), 4 * i + (c0 + 2 * half), kinds,
                                  static=((n0 + 4 * half) % 8, c0 % 2), **kw)
                else:
                    for g in range(count):
                        group(n0 + 4 * g, c0 + 2 * g, kinds, static=((n0 + 4 * g) % 8, c0 % 2), **kw)

            def transposes(name, src, ready, tiles=KT, skip=0):
                n0 = BASE[name][0]
                pe.wait_ge(*ready)
                for k in range(tiles):
                    n = n0 + k
                    pe.wait_ge(bank_free, n + 1)
                    for t in range(TT):
                        tr = pe.transpose(bank(n)[:, t * P:t * P + P], src[:, t, k * P:k * P + P], ident[:, :])
                    tr.then_inc(bank_full, 1)

            def all_banks_free(name):
                pe.wait_ge(bank_free, BASE[name][0] + 8)

            def attention(x, pairs, qs, ks, vs, lh, rb, ss, pt):
                pe.sem_inc(sg(x + "_turned"), 2)
                pe.sem_inc(sg(x + "_summed"), 2)
                with pe.Fori(0, pairs) as i:
                    pe.wait_ge(sg(x + "_staged"), i + 1)
                    for t in range(10):
                        if t < 8:
                            r, q = t // 4, t % 4
                            hs, kw = slice(HD * r, HD * r + HD), (q + 1) * P
                            pe.wait_ge(sg(x + "_max"), 8 * i + (t + 1))
                            mm = pe.matmul(ps[:, t % 2, 0:kw], qs[hs, q * P:q * P + P], ks[hs, 0:kw],
                                           start=True, stop=lh is None)
                            if lh is not None:
                                mm = pe.matmul(ps[:, t % 2, 0:kw], lh[r][hs, q * P:q * P + P], rb[hs, 0:kw],
                                               start=False, stop=True)
                            mm.then_inc(sg(x + "_scores"), 1)
                        if 1 <= t < 9:
                            b = t - 1
                            pe.wait_ge(sg(x + "_probs"), 8 * i + (b + 1))
                            pe.wait_ge(sg(x + "_evac"), 8 * i + (b + 1))
                            for j in range(b % 4 + 1):
                                mm = pe.transpose(ps[:, 2 + b % 2, j * P:j * P + P], ss[b % 2][:, j * P:j * P + P],
                                                  ident[:, :])
                            mm.then_inc(sg(x + "_turned"), 1)
                        if t >= 2:
                            b = t - 2
                            r, q = b // 4, b % 4
                            pe.wait_ge(sg(x + "_evac"), 8 * i + (b + 3))
                            for j in range(q + 1):
                                mm = pe.matmul(ps[HD * r:HD * r + HD, 4, q * P:q * P + P], vs[:, j, HD * r:HD * r + HD],
                                               pt[b % 2][:, j * P:j * P + P], start=j == 0, stop=j == q)
                            mm.then_inc(sg(x + "_summed"), 1)
                pe.wait_ge(sg(x + "_out"), pairs)

            pe.wait_ge(const_in, 16 * CONSTS)
            pe.wait_ge(sg("ones"), 1)
            for n in range(12):
                pe.wait_ge(sg("ada_acc"), n + 1)
                for c in range(4):
                    mm = pe.matmul(ps[:, 7, 4 * n + c:4 * n + c + 1], ev[:, n % 2, c * P:c * P + P],
                                   wk[:, 0, 0:1], start=True, stop=True)
                mm.then_inc(sg("ada_sum"), 1)
            pe.wait_ge(sg("mod_done"), 1)

            transposes("norm0", tok["D"], (sg("norm0_xn"), TT))
            pe.wait_ge(ev_free, BASE["qkv0"][2] + 4)
            groups("qkv0", 4, True)
            groups("qkv0", 2, False, skip=4)
            all_banks_free("g0")
            pe.wait_ge(sg("fl_split"), 1)
            for t in range(TT):
                for k in range(KT):
                    cut = slice(t * P, t * P + P)
                    pe.matmul(ps[:, 0, 16 * t:16 * t + 16], xh[:, k, cut], wsm_h[:, k, 0:16], start=k == 0, stop=False)
                    pe.matmul(ps[:, 0, 16 * t:16 * t + 16], xh[:, k, cut], wsm_l[:, k, 0:16], start=False, stop=False)
                    mm = pe.matmul(ps[:, 0, 16 * t:16 * t + 16], xl[:, k, cut], wsm_h[:, k, 0:16], start=False, stop=k == KT - 1)
            mm.then_inc(sg("fl_full"), 1)
            pe.wait_ge(sg("fl_rows"), 1)
            for t in range(TT):
                mm = pe.transpose(ps[:, 1, t * P:t * P + P], ev[:, 0, t * P:t * P + P], ident[:, :])
            mm.then_inc(sg("fl_turned"), 1)
            dt_ = feat["D"]
            attention("fox", 8, dt_[:, 0, :], dt_[:, 1, :], dt_[:, 2, :].rearrange("p (t d) -> p t d", t=TT),
                      [dt_[:, 3, :], dt_[:, 4, :]], dt_[:, 6, :], [ev[:, 0, :], ev[:, 1, :]], [ev[:, 2, :], ev[:, 3, :]])
            groups("g0", 2, True)
            pe.wait_ge(ev_free, BASE["out0"][2] + 4)
            groups("out0", 2, False, act_h=yh, act_l=yl)

            def ple(l):
                transposes(f"ht{l}", h, (sg(f"post{l}"), TT))
                transposes(f"pt{l}", tok_p, (sg(f"p_in{l}"), 16), tiles=2)
                n0, c0, u0, _ = BASE[f"ple{l}"]
                pe.wait_ge(ev_free, u0 + 4)
                for n in range(2):
                    group(n0 + 8 * n, c0 + 3 * n, False, static=((n0 + 8 * n) % 8, (c0 + 3 * n) % 2))
                    group(n0 + 8 * n + 4, c0 + 3 * n + 2, False, act_h=yh, act_l=yl, chunks=1, kn=2,
                          static=((n0 + 8 * n + 4) % 8, (c0 + 3 * n + 2) % 2))

            ple(0)

            transposes("norm1", tok["D"], (sg("norm1_xn"), TT))
            pe.wait_ge(ev_free, BASE["qfi1"][2] + 4)
            groups("qfi1", 4, True)
            groups("qfi1", 2, False, skip=4)
            all_banks_free("on1")
            pe.sem_inc(sg("lev_used"), 2)
            pe.sem_inc(sg("rec_full"), 1)
            with pe.Fori(0, 8) as i:
                for l in range(8):
                    pe.wait_ge(sg("lev_qk"), 8 * i + (l + 1))
                    pe.wait_ge(sg("lev_kept"), 8 * i + (l + 1))
                    for j in range(TT):
                        mm = pe.matmul(ps[:, l % 2, j * P:j * P + P], wk[:, 4 + l % 2, j * P:j * P + P],
                                       wk[:, 2 + l % 2, j * P:j * P + P], start=True, stop=True)
                    mm.then_inc(sg("lev_used"), 1)
                pe.wait_ge(sg("kd_ready"), i + 1)
                for j in range(TT - 1):
                    mm = pe.transpose(ps[:, 2, j * P:j * P + P], wl[:, 1, j * P:j * P + P], ident[:, :])
                mm.then_inc(sg("kd_turned"), 1)
                pe.wait_ge(sg("lev_kept"), 8 * i + 10)
                pe.wait_ge(sg("inp_staged"), i + 1)
                pe.wait_ge(sg("kd_copied"), i + 1)
                for j in range(TT):
                    cut = slice(j * P, j * P + P)
                    if j < TT - 1:
                        pe.matmul(ps[:, 4 + j, cut], wl[:, 2, cut], wl[:, 3, cut], start=True, stop=True)\
                            .then_inc(sg("state_add"), 1)
                    mm = pe.matmul(ps[:, 3, cut], wk[:, 6, cut], wl[:, 3, cut], start=True, stop=j == 0)
                    if j > 0:
                        pe.wait_ge(sg("state"), 3 * i + j)
                        mm = pe.matmul(ps[:, 3, cut], wl[:, 0, cut], wl[:, 4, (j % 2) * P:(j % 2) * P + P],
                                       start=False, stop=True)
                mm.then_inc(sg("rec_full"), 1)
            pe.wait_ge(sg("rec_out"), 9)
            transposes("on1", tok["D"], (sg("o_normed"), 1))
            groups("g1", 2, True)
            pe.wait_ge(ev_free, BASE["out1"][2] + 4)
            groups("out1", 2, False, act_h=yh, act_l=yl)
            ple(1)

            transposes("norm2", tok["D"], (sg("norm2_xn"), TT))
            pe.wait_ge(ev_free, BASE["qi2"][2] + 4)

            def rope_group(n, c, u, static):
                group(n, c, True, static=static)
                for m in range(4):
                    pe.wait_ge(bank_free, n + (m + 9))
                    pe.matmul(ps[:, (static[0] + 4 + m) % 8, :], perm[:, :], ev[:, m, :], start=True, stop=True)\
                        .then_inc(bank_full, 1)

            n0, c0, u0, _ = BASE["qi2"]
            pe.wait_ge(sg("rope_in"), 64)
            rope_group(n0, c0, u0, (n0 % 8, c0 % 2))
            n0, c0, u0, _ = BASE["qka2"]
            for g in range(2):
                rope_group(n0 + 8 * g, c0 + 2 * g, u0 + 4 * g, (n0 % 8, c0 % 2))
            n0, c0, _, _ = BASE["va2"]
            group(n0, c0, False, static=(n0 % 8, c0 % 2))
            all_banks_free("b2")
            pe.wait_ge(sg("ki_split"), 1)
            for t in range(TT):
                for k in range(KT):
                    cut = slice(t * P, t * P + P)
                    o = ps[:, 0, 72 * t:72 * t + 72]
                    pe.matmul(o, xh[:, k, cut], wsm_h[:, k, :], start=k == 0, stop=False)
                    pe.matmul(o, xh[:, k, cut], wsm_l[:, k, :], start=False, stop=False)
                    mm = pe.matmul(o, xl[:, k, cut], wsm_h[:, k, :], start=False, stop=k == KT - 1)
            mm.then_inc(sg("ki_full"), 1)
            pe.wait_ge(sg("ki_rows"), 1)
            for t in range(TT):
                mm = pe.transpose(ps[:, 1, t * P:t * P + P], ev[:, 1, t * P:t * P + P], ident[:, :])
            mm.then_inc(sg("ki_turned"), 1)
            pe.wait_ge(sg("ki_ready"), 1)
            for q in range(TT):
                kw = (q + 1) * P
                for hh in range(8):
                    b = 8 * q + hh
                    hs = slice(HD * (hh % 2), HD * (hh % 2) + HD)
                    if b >= 2:
                        pe.wait_ge(sg("idx_relu"), b - 1)
                    pe.matmul(ps[:, 2 + b % 2, 0:kw], feat["A"][hs, hh // 2, q * P:q * P + P], ev[hs, 2, 0:kw],
                              start=True, stop=True).then_inc(sg("idx_full"), 1)
            pe.wait_ge(sg("idx_relu"), 32)
            n0, c0, _, _ = BASE["b2"]
            for g in range(3):
                group(n0 + 4 * g, c0 + 2 * g, g < 2, static=((n0 + 4 * g) % 8, c0 % 2))
            all_banks_free("merge2")
            attention("top", 4, wk[:, 4, :], wk[:, 5, :], wk[:, 6, :].rearrange("p (t d) -> p t d", t=TT),
                      None, None, [wk[:, 7, :], wl[:, 4, :]], [wl[:, 5, :], wl[:, 6, :]])

            qs, ks, vs = ev[:, 0, :], ev[:, 1, :], ev[:, 2, :].rearrange("p (t d) -> p t d", t=TT)
            pe.wait_ge(sg("tri_in"), 16)
            with pe.Fori(0, 4) as i:
                pe.wait_ge(sg("stk_staged"), i + 1)
                for r in range(2):
                    hs = slice(HD * r, HD * r + HD)
                    for j in reversed(range(TT)):
                        pe.matmul(ps[:, j, j * P:T], ks[hs, j * P:j * P + P], qs[hs, j * P:T], start=True, stop=True)\
                            .then_inc(sg("stk_z"), 1)
                    for j in reversed(range(TT)):
                        pe.wait_ge(sg("stk_sp"), 8 * i + (4 * r + 4 - j))
                        pe.wait_ge(sg("stk_zc"), 8 * i + (4 * r + 4 - j))
                        for j2 in range(j, TT):
                            mm = pe.matmul(ps[:, j, j2 * P:T], tri if j2 == j else ones,
                                           sp_t[:, j2, j2 * P:T], start=j2 == j, stop=j2 == TT - 1)
                        mm.then_inc(sg("stk_r"), 1)
                    for j in range(TT):
                        if j == 0:
                            pe.wait_ge(sg("stk_att"), 8 * i + (4 * r + 4))
                        mm = pe.matmul(ps[hs, 4, j * P:T], vs[:, j, hs], at_t[:, j, j * P:T], start=j == 0, stop=j == TT - 1)
                    mm.then_inc(sg("stk_o"), 1)
            pe.wait_ge(sg("stk_out"), 4)

            n0, c0, _, _ = BASE["merge2"]
            for n in range(2):
                for b in range(2):
                    ni, ci = n0 + 16 * n + 8 * b, c0 + 6 * n + 3 * b
                    group(ni, ci, True, static=(ni % 8, ci % 2))
                    group(ni + 4, ci + 2, True, act_h=yh, act_l=yl, a0=4 * b, chunks=1,
                          static=((ni + 4) % 8, (ci + 2) % 2))
            pe.wait_ge(sg("merged"), KT)
            groups("out2", 2, False)

            def rows_of(name, col):
                n0 = BASE[name][0]
                for b in range(2):
                    pe.wait_ge(bank_free, n0 + b + 1)
                    for k in range(4):
                        c = modc[:, col + 4 * b + k:col + 4 * b + k + 1]
                        mm = pe.matmul(bank(n0 + b)[:, k * P:k * P + P], c.broadcast_to([P, P]), ident[:, :],
                                       start=True, stop=True)
                    mm.then_inc(bank_full, 1)

            rows_of("ga2_0", 16)
            transposes("norm3", tok["D"], (sg("norm3_xn"), TT))
            n0, c0, u0, _ = BASE["ffn"]
            pe.wait_ge(ev_free, u0 + 4)

            def ff1(n, c, st):
                group(n, c, True, static=st)

            def ff2(n, c, u, st, half):
                pe.wait_ge(ev_free, u)
                for g in range(2):
                    group(n + 4 * g, c + g, False, act_h=yh, act_l=yl, a0=4 * half, chunks=1,
                          static=((st[0] + 4 * g) % 8, (st[1] + g) % 2))

            def at(dn, dc):
                return ((n0 + dn) % 8, (c0 + dc) % 2)

            ff1(n0, c0, at(0, 0))
            with pe.Fori(0, 3) as j:
                n, c, u = 24 * j + n0, 8 * j + c0, 24 * j + u0
                ff1(n + 4, c + 2, at(4, 2))
                ff2(n + 8, c + 4, u + 8, at(8, 4), 0)
                ff1(n + 16, c + 6, at(16, 6))
                ff2(n + 20, c + 8, u + 12 + 8, at(20, 8), 1)
            n, c, u = n0 + 72, c0 + 24, u0 + 72
            ff1(n + 4, c + 2, at(4, 2))
            ff2(n + 8, c + 4, u + 8, at(8, 4), 0)
            ff2(n + 16, c + 6, u + 12, at(16, 6), 1)
            rows_of("ga2_1", 40)

        @block.scalar
        def _(act):
            A = Chain(act, act_self)
            act.sem_inc(bank_free, 8)

            def empty(n, dst, func=ACT.Copy, **kw):
                act.wait_ge(bank_full, n + 1)
                act.activation(dst, ps[:, n % 8, :], func, **kw).then_inc(bank_free, 1)

            def empty_to_ev(n, u, func=ACT.Copy, **kw):
                act.wait_ge(ev_free, u + 1)
                empty(n, ev[:, u % 4, :], func, **kw)

            def squares(name, src, junk, ready):
                for t in range(TT):
                    act.wait_ge(ready[0], ready[1][t])
                    act.activation(junk[:, t, :], src[:, t, :], ACT.Square, accum_out=stat[:, t:t + 1])\
                       .then_inc(sg(name + "_ss"), 1)
                act.wait_ge(sg(name + "_var"), 1)
                act.activation(stat[:, 8:12], stat[:, 4:8], ACT.Sqrt).then_inc(sg(name + "_sd"), 1)

            def turned_with_gain(name, gains, bias=None, tiles=KT):
                n0, _, u0, _ = BASE[name]
                for k in range(tiles):
                    if gains is None:
                        empty_to_ev(n0 + k, u0 + k)
                    else:
                        empty_to_ev(n0 + k, u0 + k, ACT.Identity, scale=gains[:, k:k + 1],
                                    bias=0.0 if bias is None else bias[:, k:k + 1])

            def empty_all(name, count, dst, skip=0, **kw):
                for m in range(count):
                    empty(BASE[name][0] + skip + m, dst(m), **kw)

            def gated(name):
                for m in range(8):
                    empty_to_ev(BASE[name][0] + m, BASE[name][2] + m, ACT.Silu)

            def token_dst(x):
                return lambda m: tok[x][:, m % 4, (m // 4) * G:(m // 4) * G + G]

            def out_and_norm(name, l, gain_src):
                empty_all(name, 8, token_dst("B"))
                act.dma_start(grow[:, :], gain_src.partition_broadcast(P)).then_inc(sg(f"grow{l}"), 16)
                n_last = BASE[name][0] + 8
                squares(f"post{l}", tok["B"], tok["D"], (bank_free, [8 + n_last] * 4))

            def ple(l):
                act.dma_start(tok_p, a["p"][l, 0].rearrange("(t p) d -> p t d", p=P)).then_inc(sg(f"p_in{l}"), 16)
                turned_with_gain(f"ht{l}", None)
                turned_with_gain(f"pt{l}", None, tiles=2)
                n0, _, u0, _ = BASE[f"ple{l}"]
                for n in range(2):
                    for t in range(TT):
                        empty(n0 + 8 * n + t, tok["A"][:, t, n * G:n * G + G], ACT.Sigmoid)
                    for t in range(TT):
                        empty_to_ev(n0 + 8 * n + 4 + t, u0 + 4 * n + t)

            def attention(x, pairs, ss, pt, sm, nm):
                act.sem_inc(sg(x + "_evac"), 2)
                with act.Fori(0, pairs) as i:
                    for t in range(9):
                        if t < 8:
                            b = t
                            kw = (b % 4 + 1) * P
                            act.wait_ge(sg(x + "_max"), 8 * i + (b + 3))
                            act.activation(ss[b % 2][:, 0:kw], ss[b % 2][:, 0:kw], ACT.Exp,
                                           bias=nm[:, b % 2:b % 2 + 1], accum_out=sm[:, b % 2:b % 2 + 1])\
                               .then_inc(sg(x + "_exp"), 1)
                        if t >= 1:
                            b = t - 1
                            kw = (b % 4 + 1) * P
                            act.wait_ge(sg(x + "_turned"), 8 * i + (b + 3))
                            act.wait_ge(sg(x + "_summed"), 8 * i + (b + 1))
                            act.activation(pt[b % 2][:, 0:kw], ps[:, 2 + b % 2, 0:kw], ACT.Copy)\
                               .then_inc(sg(x + "_evac"), 1)

            act.wait_ge(const_in, 16 * CONSTS)
            act.activation(stat[:, 40:48], stat[:, 32:40], ACT.Silu).then_inc(sg("c_silu"), 1)

            act.wait_ge(sg("x_in"), 16)
            squares("norm0", h, tok["B"], (sg("x_in"), [16] * 4))
            turned_with_gain("norm0", gcol[:, 0, :])
            act.dma_start(wsm[:, :, 0:16], cols(win0, 4 * D, 16, kn=KT)).then_inc(sg("fl_in"), 16)
            empty_all("qkv0", 8, lambda m: feat["A"][:, m, :], scale=HD ** -0.5)
            empty_all("qkv0", 8, lambda m: feat["B"][:, m, :], skip=8)
            empty_all("qkv0", 8, token_dst("C"), skip=16)
            act.wait_ge(sg("fl_x"), 1)
            A.after(act.activation(feat["D"][:, 5, :], feat["D"][:, 7, :], ACT.Abs))
            act.activation(feat["D"][:, 5, :], feat["D"][:, 5, :], ACT.Exp, scale=-1.0).then_inc(act_self, 1)
            A.n += 1
            A.wait()
            act.activation(feat["D"][:, 5, :], feat["D"][:, 5, :], ACT.Ln, bias=1.0).then_inc(sg("fl_ln"), 1)
            attention("fox", 8, [ev[:, 0, :], ev[:, 1, :]], [ev[:, 2, :], ev[:, 3, :]], stat[:, 20:22], stat[:, 22:24])
            gated("g0")
            out_and_norm("out0", 0, a["norm_post"][0])
            ple(0)

            act.wait_ge(sg("lb_sub"), 1)
            act.activation(lbc[:, 3:5, :], lbc[:, 3:5, :], ACT.Exp).then_inc(sg("lb_exp"), 1)
            squares("norm1", h, tok["B"], (sg("ple0_h"), [8] * 4))
            turned_with_gain("norm1", gcol[:, 1, :])
            empty_all("qfi1", 8, lambda m: feat["A"][:, m, :])
            for m in range(8):
                empty_to_ev(BASE["qfi1"][0] + 8 + m, BASE["qfi1"][2] + m, ACT.Sigmoid)
            empty_all("qfi1", 8, token_dst("D"), skip=16)
            LT, EB, ED, IS, KTT = wl[:, 7, :], wl[:, 5, :], wl[:, 6, :], wl[:, 3, :], wl[:, 2, :]
            act.sem_inc(sg("rec_out"), 1)
            act.wait_ge(bank_free, BASE["on1"][0] + 8)
            act.wait_ge(sg("f_ready"), KT)
            act.dma_start(ev[:, 0:2, :], a["c_levels"].rearrange("p (a s) -> p a s", a=2)).then_inc(sg("level_in"), 16)
            with act.Fori(0, 8) as i:
                act.wait_ge(sg("cum_done"), i + 1)
                act.sem_inc(apart, 1)
                act.activation(LT, feat["B"][:, i, :], ACT.Ln).then_inc(sg("logs"), 1)
                act.wait_ge(sg("rec_out"), i + 1)
                act.sem_inc(apart, 1)
                act.activation(IS.rearrange("p (t d) -> p t d", t=TT), tok["D"][:, :, bass.ds(i * P, P)], ACT.Copy)\
                   .then_inc(sg("inp_staged"), 1)
                for l in range(7):
                    act.wait_ge(sg("lev_diff"), 8 * i + (l + 1))
                    act.activation(wk[:, l % 2, :], wk[:, l % 2, :], ACT.Exp).then_inc(sg("lev_exp"), 1)
                act.wait_ge(sg("lev_diff"), 8 * i + 8)
                act.activation(ED, ED, ACT.Exp)
                act.activation(EB, wk[:, 7, :], ACT.Exp).then_inc(sg("eb_ready"), 1)
                act.wait_ge(sg("kd_turned"), i + 1)
                act.activation(KTT[:, 0:384], ps[:, 2, 0:384], ACT.Copy).then_inc(sg("kd_copied"), 1)
                act.wait_ge(sg("rec_full"), i + 2)
                for j in range(TT):
                    act.activation(LT[:, 0:P], ps[:, 3, j * P:j * P + P], ACT.Square,
                                   accum_out=stat2[:, bass.ds(i * 4 + j, 1)]).then_inc(sg("junk"), 1)
                    act.wait_ge(sg("junk"), 4 * i + (j + 1))
                act.sem_inc(apart, 1)
                act.activation(tok["D"][:, :, bass.ds(i * P, P)], ps[:, 3, :].rearrange("p (t d) -> p t d", t=TT),
                               ACT.Copy).then_inc(sg("rec_out"), 1)
            act.wait_ge(sg("o_var"), 1)
            act.activation(stat2[:, 0:32], stat2[:, 0:32], ACT.Sqrt).then_inc(sg("o_sd"), 1)
            n0 = BASE["on1"][0]
            for k in range(KT):
                empty(n0 + k, feat["A"][:, k, :], ACT.Copy, scale=ocol[:, 0:1])
            gated("g1")
            out_and_norm("out1", 1, a["norm_post"][1])
            ple(1)

            squares("norm2", h, tok["B"], (sg("ple1_h"), [8] * 4))
            act.wait_ge(sg("gains2"), 2)
            turned_with_gain("norm2", gcol[:, 2, :], modc[:, 0:8])
            act.dma_start(rope[0], a["c_cos"]).then_inc(sg("rope_in"), 16)
            act.dma_start(rope[1], a["c_sin"]).then_inc(sg("rope_in"), 16)
            act.dma_start(perm, a["c_perm"]).then_inc(sg("rope_in"), 16)
            act.dma_start(slot["D"][:, 3200:3264], a["c_rope_t"]).then_inc(sg("rope_in"), 16)
            act.dma_start(wsm, cols(win2, 7 * G, 72, kn=KT)).then_inc(sg("ki_in"), 16)

            def rope_group(n, u, dst, scale):
                for m in range(4):
                    empty_to_ev(n + m, u + m, scale=scale)
                for m in range(4):
                    empty(n + 4 + m, dst(m))

            n0, _, u0, _ = BASE["qi2"]
            rope_group(n0, u0, lambda m: feat["A"][:, m, :], 1.0)
            n0, _, u0, _ = BASE["qka2"]
            rope_group(n0, u0, lambda m: feat["B"][:, m, :], HD ** -0.5)
            rope_group(n0 + 8, u0 + 4, lambda m: feat["B"][:, 4 + m, :], 1.0)
            empty_all("va2", 4, token_dst("C"))
            rt = [ev[:, 3, :], ev[:, 0, :]]
            for q in range(TT):
                for hh in range(8):
                    b = 8 * q + hh
                    if b >= 2:
                        act.wait_ge(sg("idx_acc"), b - 1)
                    act.wait_ge(sg("idx_full"), b + 1)
                    act.activation(rt[b % 2][:, 0:(q + 1) * P], ps[:, 2 + b % 2, 0:(q + 1) * P], ACT.Relu)\
                       .then_inc(sg("idx_relu"), 1)
            empty_all("b2", 4, lambda m: feat["D"][:, m, :], scale=HD ** -0.5)
            empty_all("b2", 4, lambda m: feat["D"][:, 4 + m, :], skip=4)
            empty_all("b2", 4, lambda m: tok["C"][:, m, G:D], skip=8)
            act.dma_start(grow[:, 0:512], a["c_stick"]).then_inc(sg("tri_in"), 16)
            attention("top", 4, [wk[:, 7, :], wl[:, 4, :]], [wl[:, 5, :], wl[:, 6, :]], stat[:, 20:22], stat[:, 22:24])

            act.wait_ge(sg("top_out"), 4)
            with act.Fori(0, 4) as i:
                for r in range(2):
                    for j in reversed(range(TT)):
                        z = ps[:, j, j * P:T]
                        act.wait_ge(sg("stk_z"), 8 * i + (4 * r + 4 - j))
                        act.wait_ge(sg("stk_free"), 2 * i + (r + 1))
                        act.activation(z_t[:, j, j * P:T], z, ACT.Copy).then_inc(sg("stk_zc"), 1)
                        act.activation(ln_t[:, j, j * P:T], z, ACT.Abs).then_inc(act_self, 1)
                        act.wait_ge(act_self, A.n + 16 * i + (8 * r + 2 * (TT - 1 - j) + 1))
                        act.activation(ln_t[:, j, j * P:T], ln_t[:, j, j * P:T], ACT.Exp, scale=-1.0).then_inc(act_self, 1)
                        act.wait_ge(act_self, A.n + 16 * i + (8 * r + 2 * (TT - 1 - j) + 2))
                        act.activation(ln_t[:, j, j * P:T], ln_t[:, j, j * P:T], ACT.Ln, bias=1.0).then_inc(sg("stk_ln"), 1)
                    for j in reversed(range(TT)):
                        act.wait_ge(sg("stk_arg"), 8 * i + (4 * r + 4 - j))
                        act.activation(at_t[:, j, j * P:T], z_t[:, j, j * P:T], ACT.Exp).then_inc(sg("stk_att"), 1)
            A.n += 64

            n0, _, u0, _ = BASE["merge2"]
            for n in range(2):
                for b in range(2):
                    gates = feat["BC"[b]]
                    for m in range(4):
                        empty(n0 + 16 * n + 8 * b + m, gates[:, 4 * n + m, :], ACT.Sigmoid)
                    for m in range(4):
                        empty_to_ev(n0 + 16 * n + 8 * b + 4 + m, u0 + 8 * n + 4 * b + m)

            def rows_of(name, l):
                for b in range(2):
                    empty(BASE[name][0] + b, slot["C"][:, b * G:b * G + G])

            out_and_norm("out2", 2, a["g_post_mix_2"][0])
            rows_of("ga2_0", 2)
            squares("norm3", h, tok["B"], (sg("post2"), [1, 2, 3, 4]))
            turned_with_gain("norm3", gcol[:, 3, :], modc[:, 24:32])
            n0, _, u0, _ = BASE["ffn"]
            n, u = n0, u0
            for i in range(9):
                if i < 8:
                    for m in range(4):
                        empty_to_ev(n + m, u + m, ACT.Relu)
                    n, u = n + 4, u + 4
                if i > 0:
                    for m in range(8):
                        empty_to_ev(n + m, u + m)
                    n, u = n + 8, u + 8
            act.dma_start(grow[:, :], a["g_post_ffn_2"][0].partition_broadcast(P)).then_inc(sg("grow3"), 16)
            squares("post3", tok["B"], tok["D"], (ev_free, [4 + u] * 4))
            rows_of("ga2_1", 3)

        @block.vector
        def _(dve):
            V = Chain(dve, dve_self)
            dve.sem_inc(ev_free, 4)
            X = (xh, xl)
            Y = (yh, yl)

            def split(n, u, s, dst, k):
                dve.wait_ge(bank_free, n + 9)
                split_tile(ev[:, u % 4, :], s, dst, k).then_inc(ev_free, 1)

            def split_tile(src, s, dst, k):
                dve.tensor_copy(dst[0][:, k, :], src).then_inc(hi_done, 1)
                dve.wait_ge(hi_done, s + 1)
                return dve.tensor_tensor(dst[1][:, k, :], src, dst[0][:, k, :].bitcast(F32), ALU.subtract)

            def split_all(name, dst, tiles=KT):
                n0, _, u0, s0 = BASE[name]
                for k in range(tiles):
                    split(n0 + k, u0 + k, s0 + k, dst, k)

            def rstd(name):
                dve.wait_ge(sg(name + "_ss"), TT)
                dve.tensor_scalar(stat[:, 4:8], stat[:, 0:4], 1.0 / D, EPS, ALU.mult, ALU.add).then_inc(sg(name + "_var"), 1)
                dve.wait_ge(sg(name + "_sd"), 1)
                V.after(dve.reciprocal(stat[:, 12:16], stat[:, 8:12]))

            def norm(name):
                rstd(name)
                for t in range(TT):
                    dve.tensor_scalar(tok["D"][:, t, :], h[:, t, :], stat[:, 12 + t:13 + t], None, ALU.mult)\
                       .then_inc(sg(name + "_xn"), 1)

            def post(l, last=None):
                rstd(f"post{l}")
                dve.wait_ge(sg(f"grow{l}"), 16)
                if l >= 2:
                    dve.wait_ge(bank_free, BASE[f"ga2_{l - 2}"][0] + 10)
                    V.after(dve.tensor_tensor(grow[:, :], grow[:, :], slot["C"][:, 0:D], ALU.mult))
                for t in range(TT):
                    y = tok["B"][:, t, :]
                    V.after(dve.scalar_tensor_tensor(out=y, in0=y, scalar=stat[:, 12 + t:13 + t], in1=grow[:, :],
                                                     op0=ALU.mult, op1=ALU.mult))
                    dve.tensor_tensor(h[:, t, :], h[:, t, :], y, ALU.add).then_inc(last or sg(f"post{l}"), 1)

            def gated(name):
                n0, _, u0, s0 = BASE[name]
                for m in range(8):
                    dve.wait_ge(bank_free, n0 + m + 9)
                    e = ev[:, (u0 + m) % 4, :]
                    V.after(dve.tensor_tensor(e, e, feat["A"][:, m, :], ALU.mult))
                    split_tile(e, s0 + m, Y, m).then_inc(ev_free, 1)

            def ple(l):
                dve.wait_ge(sg(f"post{l}"), TT)
                split_all(f"ht{l}", X)
                split_all(f"pt{l}", Y, tiles=2)
                n0, _, u0, _ = BASE[f"ple{l}"]
                for n in range(2):
                    for t in range(TT):
                        dve.wait_ge(bank_free, n0 + 8 * n + 4 + t + 9)
                        e = ev[:, (u0 + 4 * n + t) % 4, :]
                        hh = h[:, t, n * G:n * G + G]
                        V.after(dve.tensor_tensor(e, e, tok["A"][:, t, n * G:n * G + G], ALU.mult))
                        V.after(dve.tensor_tensor(hh, hh, e, ALU.add))
                        dve.sem_inc(ev_free, 1)
                        dve.sem_inc(sg(f"ple{l}_h"), 1)

            def attention(x, pairs, src, qs, ks, vs, lh, ss, strip, mx, nm, sm, rs, out, out_links=0):
                dve.sem_inc(sg(x + "_max"), 2)
                with dve.Fori(0, pairs) as i:
                    V.enter(i, 2 * 8 + out_links)
                    dve.sem_inc(apart, 1)
                    dve.tensor_copy(qs, src[0][:, i, :])
                    dve.tensor_copy(ks, src[1][:, i, :])
                    if lh is not None:
                        for r in range(2):
                            dve.tensor_scalar(lh[r], feat["D"][:, 7, :], sel[:, bass.ds(2 * i + r, 1)], None,
                                              ALU.mult)
                    dve.tensor_copy(vs, src[2][:, :, bass.ds(i * P, P)]).then_inc(sg(x + "_staged"), 1)
                    for t in range(9):
                        if t < 8:
                            b = t
                            o = b % 2
                            kw = (b % 4 + 1) * P
                            dve.wait_ge(sg(x + "_scores"), 8 * i + (b + 1))
                            dve.wait_ge(sg(x + "_turned"), 8 * i + (b + 1))
                            dve.sem_inc(apart, 1)
                            V.after(dve.tensor_tensor_reduce(ss[o][:, 0:kw], ps[:, o, 0:kw], strip(b % 4), 1.0,
                                                             NEG, ALU.add, ALU.max, mx[:, o:o + 1]))
                            dve.tensor_scalar(nm[:, o:o + 1], mx[:, o:o + 1], -1.0, None, ALU.mult)\
                               .then_inc(sg(x + "_max"), 1)
                        if t >= 1:
                            b = t - 1
                            o = b % 2
                            kw = (b % 4 + 1) * P
                            dve.wait_ge(sg(x + "_exp"), 8 * i + (b + 1))
                            V.after(dve.reciprocal(rs[:, o:o + 1], sm[:, o:o + 1]))
                            dve.tensor_scalar(ss[o][:, 0:kw], ss[o][:, 0:kw], rs[:, o:o + 1], None, ALU.mult)\
                               .then_inc(sg(x + "_probs"), 1)
                    dve.wait_ge(sg(x + "_summed"), 8 * i + 10)
                    dve.sem_inc(apart, 1)
                    out(i)
                V.leave(pairs)

            V.after(dve.memset(wk[:, 0, 0:1], 1.0))
            dve.sem_inc(sg("ones"), 1)
            dve.wait_ge(sg("c_silu"), 1)
            for n in range(12):
                acc = ev[:, n % 2, :]
                if n >= 2:
                    dve.wait_ge(sg("ada_sum"), n - 1)
                for c in (2 * n, 2 * n + 1):
                    dve.wait_ge(sg(f"ada_landed{c % 4}"), 16 * (c // 4 + 1))
                    buf = slot["CD"[c % 4 // 2]][:, (c % 2) * 2048:(c % 2) * 2048 + 2048]
                    for k in range(4):
                        w = buf[:, k * G:k * G + G]
                        s = stat[:, 40 + 4 * (c % 2) + k:41 + 4 * (c % 2) + k]
                        if c % 2 == 0 and k == 0:
                            V.after(dve.tensor_scalar(acc, w, s, None, ALU.mult))
                        else:
                            V.after(dve.scalar_tensor_tensor(out=acc, in0=w, scalar=s, in1=acc, op0=ALU.mult, op1=ALU.add))
                    dve.sem_inc(sg("ada_used"), 1)
                dve.sem_inc(sg("ada_acc"), 1)
            dve.wait_ge(sg("ada_sum"), 12)
            V.after(dve.tensor_tensor(modc[:, :], modc[:, :], ps[:, 7, 0:48], ALU.add))
            dve.sem_inc(sg("mod_done"), 1)
            for g, c in ((2, 8), (3, 32)):
                dve.scalar_tensor_tensor(out=gcol[:, g, :], in0=modc[:, c:c + 8], scalar=1.0, in1=gcol[:, g, :],
                                         op0=ALU.add, op1=ALU.mult).then_inc(sg("gains2"), 1)
            V.after(dve.tensor_tensor(lbc[:, 2, :], lbc[:, 0, :], lbc[:, 1, :], ALU.max))
            dve.tensor_tensor(lbc[:, 3, :], lbc[:, 0, :], lbc[:, 2, :], ALU.subtract)
            dve.tensor_tensor(lbc[:, 4, :], lbc[:, 1, :], lbc[:, 2, :], ALU.subtract).then_inc(sg("lb_sub"), 1)

            norm("norm0")
            split_all("norm0", X)
            dve.wait_ge(sg("fl_in"), 16)
            V.after(dve.tensor_copy(wsm_h[:, :, 0:16], wsm[:, :, 0:16]))
            V.after(dve.tensor_tensor(wsm_l[:, :, 0:16], wsm[:, :, 0:16], wsm_h[:, :, 0:16].bitcast(F32), ALU.subtract))
            dve.sem_inc(sg("fl_split"), 1)
            fr = ev[:, 0, :].rearrange("p (t c) -> p t c", t=TT)
            V.after(dve.memset(ev[:, 0, :], 0.0))
            dve.wait_ge(sg("fl_full"), 1)
            fp = ps[:, 0, 0:64].rearrange("p (t c) -> p t c", t=TT)
            for r in (0, 32, 64, 96):
                V.after(dve.tensor_copy(fr[:, :, r:r + 16], fp))
            dve.sem_inc(sg("fl_rows"), 1)
            dve.wait_ge(sg("fl_turned"), 1)
            C5, C6, C7 = (feat["D"][:, k, :] for k in (5, 6, 7))
            V.after(dve.memset(stat[:, 24:25], 0.0))
            for r in (0, 32, 64, 96):
                V.after(dve.tensor_copy(stat[r:r + 16, 24:25], bfc[r:r + 16, :]))
            V.after(dve.tensor_scalar(C7, ps[:, 1, :], stat[:, 24:25], None, ALU.add))
            dve.sem_inc(sg("fl_x"), 1)
            dve.wait_ge(sg("fl_ln"), 1)
            V.after(dve.tensor_scalar(C7, C7, 0.0, None, ALU.min))
            V.after(dve.tensor_tensor(C7, C7, C5, ALU.subtract))
            V.after(dve.tensor_tensor_scan(C6, C7, C7, 0.0, ALU.add, ALU.bypass))
            V.after(dve.memset(C7, 0.0))
            for r in (0, 64):
                V.after(dve.tensor_copy(C7[r:r + 16, :], C6[r:r + 16, :]))
                V.after(dve.memset(C7[r + 32:r + 64, :], -1.0))
                V.after(dve.memset(C6[r:r + 32, :], 1.0))
            DT = feat["D"]

            def fox_out(i):
                dve.tensor_copy(feat["A"][:, i, :], ps[:, 4, :]).then_inc(sg("fox_out"), 1)

            attention("fox", 8, (feat["A"], feat["B"], tok["C"]), DT[:, 0, :], DT[:, 1, :],
                      DT[:, 2, :].rearrange("p (t d) -> p t d", t=TT), [DT[:, 3, :], DT[:, 4, :]],
                      [ev[:, 0, :], ev[:, 1, :]], lambda q: mask[:, 384 - q * P:512],
                      stat[:, 16:18], stat[:, 22:24], stat[:, 20:22], stat[:, 18:20], fox_out)
            dve.wait_ge(sg("fox_out"), 8)
            gated("g0")
            post(0)
            ple(0)

            dve.wait_ge(sg("lb_exp"), 1)
            V.after(dve.tensor_tensor(lbc[:, 0, :], lbc[:, 3, :], lbc[:, 4, :], ALU.add))
            V.after(dve.reciprocal(lbc[:, 1, :], lbc[:, 0, :]))
            V.after(dve.tensor_tensor(lbc[:, 3, :], lbc[:, 3, :], lbc[:, 1, :], ALU.mult))
            V.after(dve.tensor_tensor(lbc[:, 4, :], lbc[:, 4, :], lbc[:, 1, :], ALU.mult))
            V.after(dve.tensor_tensor(lbc[:, 1, :], lbc[:, 3, :], lbc[:, 4, :], ALU.add))
            V.after(dve.tensor_tensor(lbc[:, 1, :], lbc[:, 1, :], lbc[:, 3, :], ALU.subtract))
            V.after(dve.tensor_scalar(lbc[:, 0, :], lbc[:, 1, :], -1.0, 1.0, ALU.mult, ALU.add))
            V.after(dve.tensor_scalar(lbc[:, 5, :], lbc[:, 0, :], -1.0, None, ALU.mult))
            dve.wait_ge(sg("ple0_h"), 8)
            norm("norm1")
            split_all("norm1", X)
            n0, _, u0, _ = BASE["qfi1"]
            for m in range(8):
                dve.wait_ge(bank_free, n0 + 8 + m + 9)
                e = ev[:, (u0 + m) % 4, :]
                V.after(dve.tensor_scalar(feat["B"][:, m, :], e, lbc[:, 0, m:m + 1], lbc[:, 1, m:m + 1], ALU.mult, ALU.add))
                V.after(dve.tensor_scalar(feat["B"][:, m, :], feat["B"][:, m, :], 2.0 ** -63, None, ALU.max))
                V.after(dve.tensor_scalar(feat["C"][:, m, :], e, lbc[:, 5, m:m + 1], lbc[:, 0, m:m + 1], ALU.mult, ALU.add))
                dve.sem_inc(ev_free, 1)
                dve.sem_inc(sg("f_ready"), 1)
            dve.wait_ge(sg("level_in"), 16)
            LT, EB, ED, BT, SC = wl[:, 7, :], wl[:, 5, :], wl[:, 6, :], wk[:, 7, :], wk[:, 6, :]
            ST = [wl[:, 4, 0:P], wl[:, 4, P:2 * P]]
            V.after(dve.memset(wk[:, 2:7, :], 0.0))
            dve.sem_inc(sg("cum_done"), 1)
            dve.sem_inc(sg("lev_kept"), 2)
            with dve.Fori(0, 8) as i:
                V.enter(i, 4 + 2 * 8 + 2 * 8 + 8 + 3 + 3)
                dve.wait_ge(sg("logs"), i + 1)
                for j in range(TT):
                    cut = slice(j * P, j * P + P)
                    V.mark(dve.tensor_tensor_scan(BT[:, cut], LT[:, cut], LT[:, cut], 0.0, ALU.add, ALU.bypass))
                V.wait()
                dve.sem_inc(sg("cum_done"), 1)

                def diff(l):
                    if l == 7:
                        bl = BT.rearrange("p (n c) -> p n c", c=P)
                        V.mark(dve.tensor_tensor(ED.rearrange("p (n c) -> p n c", c=P),
                                                 bl[:, :, P - 1:P].broadcast_to([P, TT, P]), bl, ALU.subtract))
                        V.mark(dve.tensor_copy(m8[:, 0:1], BT[:, 0:1]))
                    else:
                        half = 64 >> l
                        b3 = BT.rearrange("p (n c) -> p n c", c=2 * half)
                        e3 = wk[:, l % 2, :].rearrange("p (n c) -> p n c", c=2 * half)
                        mid = b3[:, :, half - 1:half].broadcast_to([P, T // (2 * half), half])
                        V.mark(dve.tensor_tensor(e3[:, :, 0:half], mid, b3[:, :, 0:half], ALU.subtract))
                        V.mark(dve.tensor_tensor(e3[:, :, half:2 * half], b3[:, :, half:2 * half], mid, ALU.subtract))
                    V.wait()
                    dve.sem_inc(sg("lev_diff"), 1)

                def decay(l):
                    o = l % 2
                    dve.wait_ge(sg("lev_used"), 8 * i + (l + 1))
                    if l == 7:
                        dve.sem_inc(apart, 1)
                        V.mark(dve.tensor_copy(wk[:, 2 + o, :], feat["A"][:, i, :]))
                        V.mark(dve.tensor_copy(wk[:, 4 + o, :], feat["C"][:, i, :]))
                    else:
                        half = 64 >> l
                        dve.wait_ge(sg("lev_exp"), 7 * i + (l + 1))
                        v = [x.rearrange("p (n c) -> p n c", c=2 * half) for x in
                             (wk[:, 2 + o, :], wk[:, 4 + o, :], wk[:, o, :], feat["A"][:, i, :], feat["C"][:, i, :])]
                        hi, lo = slice(half, 2 * half), slice(0, half)
                        V.mark(dve.tensor_tensor(v[0][:, :, hi], v[3][:, :, hi], v[2][:, :, hi], ALU.mult))
                        V.mark(dve.tensor_tensor(v[1][:, :, lo], v[4][:, :, lo], v[2][:, :, lo], ALU.mult))
                    V.wait()
                    dve.sem_inc(sg("lev_qk"), 1)

                def keep(l):
                    dve.wait_ge(sg("lev_used"), 8 * i + (l + 3))
                    if l == 0:
                        dve.wait_ge(sg("rec_full"), i + 1)
                    mk = level[:, l:l + 1, :].broadcast_to([P, TT, P])
                    dve.sem_inc(apart, 1)
                    V.after(dve.copy_predicated(SC.rearrange("p (n c) -> p n c", c=P), mk,
                                                ps[:, l % 2, :].rearrange("p (n c) -> p n c", c=P)))
                    dve.sem_inc(sg("lev_kept"), 1)

                diff(0)
                for l in range(8):
                    if l < 7:
                        diff(l + 1)
                    decay(l)
                    if l > 0:
                        keep(l - 1)
                dve.wait_ge(sg("eb_ready"), i + 1)
                V.mark(dve.tensor_tensor(wl[:, 0, :], feat["A"][:, i, :], EB, ALU.mult))
                V.mark(dve.tensor_tensor(wl[:, 1, :], feat["C"][:, i, :], ED, ALU.mult))
                V.wait()
                dve.sem_inc(sg("kd_ready"), 1)
                keep(7)
                V.mark(dve.tensor_copy(m8[:, 0:1], BT[:, 0:1]))
                for j in range(TT - 1):
                    dve.wait_ge(sg("state_add"), 3 * i + (j + 1))
                    u = ps[:, 4 + j, j * P:j * P + P]
                    if j == 0:
                        ins = dve.tensor_copy(ST[1], u)
                    else:
                        ins = dve.scalar_tensor_tensor(out=ST[(j + 1) % 2], in0=ST[j % 2],
                                                       scalar=EB[:, j * P + P - 1:j * P + P], in1=u,
                                                       op0=ALU.mult, op1=ALU.add)
                    V.after(ins)
                    dve.sem_inc(sg("state"), 1)
                V.wait()
            V.leave(8)
            dve.wait_ge(sg("rec_out"), 9)
            V.after(dve.tensor_scalar(stat2[:, 0:32], stat2[:, 0:32], 1.0 / P, EPS, ALU.mult, ALU.add))
            dve.sem_inc(sg("o_var"), 1)
            dve.wait_ge(sg("o_sd"), 1)
            V.after(dve.reciprocal(stat2[:, 0:32], stat2[:, 0:32]))
            o4 = slot["D"][:, :].rearrange("p (t h d) -> p t h d", t=TT, h=8)
            r4 = stat2[:, 0:32].rearrange("p (h t) -> p t h", t=TT)
            for t in range(TT):
                V.after(dve.tensor_tensor(o4[:, t], o4[:, t], r4[:, t, :].unsqueeze(2).broadcast_to([P, 8, P]), ALU.mult))
            dve.sem_inc(sg("o_normed"), 1)
            gated("g1")
            post(1)
            ple(1)

            dve.wait_ge(sg("ple1_h"), 8)
            norm("norm2")
            split_all("norm2", X)
            dve.wait_ge(sg("ki_in"), 16)
            V.after(dve.tensor_copy(wsm_h[:, :, :], wsm))
            V.after(dve.tensor_tensor(wsm_l[:, :, :], wsm, wsm_h[:, :, :].bitcast(F32), ALU.subtract))
            dve.sem_inc(sg("ki_split"), 1)
            dve.wait_ge(sg("rope_in"), 64)

            def rope_group(n, u, dst):
                for m in range(4):
                    dve.wait_ge(bank_free, n + 4 + m + 9)
                    e = ev[:, (u + m) % 4, :]
                    V.mark(dve.tensor_tensor(dst(m), dst(m), rope[1], ALU.mult))
                    V.mark(dve.tensor_tensor(e, e, rope[0], ALU.mult))
                    V.wait()
                    V.after(dve.tensor_tensor(dst(m), dst(m), e, ALU.add))
                    dve.sem_inc(ev_free, 1)

            n0, _, u0, _ = BASE["qi2"]
            rope_group(n0, u0, lambda m: feat["A"][:, m, :])
            n0, _, u0, _ = BASE["qka2"]
            rope_group(n0, u0, lambda m: feat["B"][:, m, :])
            rope_group(n0 + 8, u0 + 4, lambda m: feat["B"][:, 4 + m, :])
            dve.wait_ge(sg("ki_full"), 1)
            smv = ev[:, 0, 0:288].rearrange("p (t c) -> p t c", t=TT)
            kr = ev[:, 1, :].rearrange("p (t c) -> p t c", t=TT)
            tmp = ev[:, 0, 288:352].rearrange("p (a t f) -> p a t f", a=2, t=TT)
            V.after(dve.tensor_copy(smv, ps[:, 0, 0:288].rearrange("p (t c) -> p t c", t=TT)))
            V.mark(dve.tensor_scalar(stat2[:, 0:32].rearrange("p (t h) -> p t h", t=TT), smv[:, :, 64:72], ISCALE, None, ALU.mult))
            V.mark(dve.tensor_copy(kr[:, :, 0:64], smv[:, :, 0:64]))
            x1, x2, cs, sn = smv[:, :, 0:8], smv[:, :, 8:16], rope_t[:, 0], rope_t[:, 1]
            V.mark(dve.tensor_tensor(tmp[:, 0], x2, sn, ALU.mult))
            V.mark(dve.tensor_tensor(tmp[:, 1], x1, sn, ALU.mult))
            V.wait()
            V.mark(dve.tensor_tensor(kr[:, :, 0:8], x1, cs, ALU.mult))
            V.mark(dve.tensor_tensor(kr[:, :, 8:16], x2, cs, ALU.mult))
            V.wait()
            V.mark(dve.tensor_tensor(kr[:, :, 0:8], kr[:, :, 0:8], tmp[:, 0], ALU.subtract))
            V.mark(dve.tensor_tensor(kr[:, :, 8:16], kr[:, :, 8:16], tmp[:, 1], ALU.add))
            V.wait()
            V.after(dve.tensor_copy(kr[:, :, 64:128], kr[:, :, 0:64]))
            dve.sem_inc(sg("ki_rows"), 1)
            dve.wait_ge(sg("ki_turned"), 1)
            V.after(dve.tensor_copy(ev[:, 2, :], ps[:, 1, :]))
            dve.sem_inc(sg("ki_ready"), 1)
            rt = [ev[:, 3, :], ev[:, 0, :]]
            for q in range(TT):
                kw = (q + 1) * P
                strip = isc[:, KOFF[q]:KOFF[q] + kw]
                for hh in range(8):
                    b = 8 * q + hh
                    dve.wait_ge(sg("idx_relu"), b + 1)
                    V.after(dve.scalar_tensor_tensor(out=strip, in0=rt[b % 2][:, 0:kw],
                                                     scalar=stat2[:, 8 * q + hh:8 * q + hh + 1],
                                                     in1=mask[:, 384 - q * P:512] if hh == 0 else strip,
                                                     op0=ALU.mult, op1=ALU.add))
                    dve.sem_inc(sg("idx_acc"), 1)
            dve.wait_ge(sg("idx_relu"), 32)
            tw, eq = slot["A"][:, 0:512], slot["A"][:, 512:1024]
            V.after(dve.tensor_copy(isc[:, 0:P], mask[:, 384:512]))
            for q in range(1, TT):
                kw = (q + 1) * P
                strip, w, e = isc[:, KOFF[q]:KOFF[q] + kw], tw[:, 0:kw], eq[:, 0:kw]
                V.after(dve.tensor_copy(w, strip))
                for r in range(TOPK // 8):
                    V.after(dve.max(m8[:, :], w))
                    if r < TOPK // 8 - 1:
                        V.after(dve.match_replace(w, m8[:, :], w, NEG))
                V.after(dve.tensor_scalar(e, strip, m8[:, 7:8], None, ALU.is_equal))
                V.after(dve.tensor_scalar(w, strip, m8[:, 7:8], None, ALU.is_gt))
                V.after(dve.tensor_reduce(stat[:, 24:25], w, AX.X, ALU.add))
                V.after(dve.tensor_scalar(stat[:, 25:26], stat[:, 24:25], -1.0, float(TOPK), ALU.mult, ALU.add))
                V.after(dve.tensor_tensor_scan(strip, e, e, 0.0, ALU.add, ALU.bypass))
                V.after(dve.scalar_tensor_tensor(out=e, in0=strip, scalar=stat[:, 25:26], in1=e, op0=ALU.is_le, op1=ALU.mult))
                V.after(dve.tensor_tensor(w, w, e, ALU.add))
                V.after(dve.tensor_scalar(strip, w, 1.0, -NEG, ALU.subtract, ALU.mult))
            dve.wait_ge(bank_free, BASE["merge2"][0] + 8)

            def top_out(i):
                o = wl[:, 7, :]
                V.after(dve.tensor_copy(o, ps[:, 4, :]))
                V.after(dve.tensor_copy(yh[:, i, :], o))
                dve.tensor_tensor(yl[:, i, :], o, yh[:, i, :].bitcast(F32), ALU.subtract).then_inc(sg("top_out"), 1)

            attention("top", 4, (feat["B"], feat["B"][:, 4:8, :], tok["C"]), wk[:, 4, :], wk[:, 5, :],
                      wk[:, 6, :].rearrange("p (t d) -> p t d", t=TT), None,
                      [wk[:, 7, :], wl[:, 4, :]], lambda q: isc[:, KOFF[q]:KOFF[q] + (q + 1) * P],
                      stat[:, 16:18], stat[:, 22:24], stat[:, 20:22], stat[:, 18:20], top_out, out_links=2)

            dve.wait_ge(sg("tri_in"), 16)
            dve.wait_ge(sg("top_out"), 4)
            dve.sem_inc(sg("stk_free"), 1)
            with dve.Fori(0, 4) as i:
                V.enter(i, 2 * (4 * 2 + 4 * 2) + 2)
                dve.tensor_copy(ev[:, 0, :], feat["D"][:, i, :])
                dve.tensor_copy(ev[:, 1, :], feat["D"][:, i + 4, :])
                dve.tensor_copy(ev[:, 2, :].rearrange("p (t d) -> p t d", t=TT), tok["C"][:, :, bass.ds(i * P + G, P)])\
                   .then_inc(sg("stk_staged"), 1)
                for r in range(2):
                    for j in reversed(range(TT)):
                        dve.wait_ge(sg("stk_ln"), 8 * i + (4 * r + 4 - j))
                        V.after(dve.scalar_tensor_tensor(out=sp_t[:, j, j * P:T], in0=z_t[:, j, j * P:T], scalar=0.0,
                                                         in1=ln_t[:, j, j * P:T], op0=ALU.max, op1=ALU.add))
                        dg = sp_t[:, j, j * P:j * P + P]
                        V.after(dve.tensor_tensor(dg, dg, strict, ALU.mult))
                        dve.sem_inc(sg("stk_sp"), 1)
                    for j in reversed(range(TT)):
                        dve.wait_ge(sg("stk_r"), 8 * i + (4 * r + 4 - j))
                        V.after(dve.tensor_tensor(z_t[:, j, j * P:T], z_t[:, j, j * P:T], ps[:, j, j * P:T], ALU.subtract))
                        dg = z_t[:, j, j * P:j * P + P]
                        V.after(dve.tensor_tensor(dg, dg, strict_neg, ALU.add))
                        dve.sem_inc(sg("stk_arg"), 1)
                    dve.wait_ge(sg("stk_o"), 2 * i + (r + 1))
                    dve.sem_inc(sg("stk_free"), 1)
                o = ev[:, 3, :]
                V.after(dve.tensor_copy(o, ps[:, 4, :]))
                V.after(dve.tensor_copy(yh[:, i + 4, :], o))
                dve.tensor_tensor(yl[:, i + 4, :], o, yh[:, i + 4, :].bitcast(F32), ALU.subtract).then_inc(sg("stk_out"), 1)
            V.leave(4)

            n0, _, u0, s0 = BASE["merge2"]
            for n in range(2):
                for b in range(2):
                    for m in range(4):
                        dve.wait_ge(bank_free, n0 + 16 * n + 8 * b + 4 + m + 9)
                        e, am = ev[:, (u0 + 8 * n + 4 * b + m) % 4, :], feat["A"][:, 4 * n + m, :]
                        gate = feat["BC"[b]][:, 4 * n + m, :]
                        if b == 0:
                            V.after(dve.tensor_tensor(am, e, gate, ALU.mult))
                        else:
                            V.after(dve.tensor_tensor(e, e, gate, ALU.mult))
                            V.after(dve.tensor_tensor(am, am, e, ALU.add))
                        dve.sem_inc(ev_free, 1)
            for k in range(KT):
                split_tile(feat["A"][:, k, :], s0 + k, X, k).then_inc(sg("merged"), 1)
            post(2)
            dve.wait_ge(sg("post2"), TT)
            norm("norm3")
            split_all("norm3", X)
            n0, _, u0, s0 = BASE["ffn"]
            n, u, s = n0, u0, s0
            for i in range(9):
                if i < 8:
                    for m in range(4):
                        dve.wait_ge(bank_free, n + m + 9)
                        e = ev[:, (u + m) % 4, :]
                        V.after(dve.tensor_tensor(e, e, e, ALU.mult))
                        split_tile(e, s + m, Y, 4 * (i % 2) + m).then_inc(ev_free, 1)
                    n, u, s = n + 4, u + 4, s + 4
                if i > 0:
                    for m in range(8):
                        dve.wait_ge(bank_free, n + m + 9)
                        e = ev[:, (u + m) % 4, :]
                        y = tok["B"][:, m % 4, (m // 4) * G:(m // 4) * G + G]
                        if i == 1:
                            V.after(dve.tensor_copy(y, e))
                        else:
                            V.after(dve.tensor_tensor(y, y, e, ALU.add))
                        dve.sem_inc(ev_free, 1)
                    n, u = n + 8, u + 8
            post(3, last=sg("final"))


def constants():
    i = np.arange(P)
    causal = np.zeros((P, T), np.float32)
    causal[:, 384:] = np.where(i[None, :] > i[:, None], NEG, 0.0)
    sel = np.zeros((P, 16), np.float32)
    for x in range(16):
        sel[x::32, x] = 1.0
    s, t = i[:, None], i[None, :]
    levels = np.zeros((P, 8, P), np.float32)
    for l in range(7):
        half = 64 >> l
        levels[:, l] = (s // (2 * half) == t // (2 * half)) & (s % (2 * half) < half) & (t % (2 * half) >= half)
    levels[:, 7] = s == t
    stick = np.concatenate([(s >= t).astype(np.float32), np.ones((P, P), np.float32), (s < t).astype(np.float32),
                            np.where(s < t, 0.0, NEG).astype(np.float32)], axis=1)
    pos = np.arange(T, dtype=np.float32)
    freq = np.float32(500000.0) ** (-np.arange(0, 16, 2, dtype=np.float32) / np.float32(16))
    ang = pos[:, None] * freq[None, :].astype(np.float32)
    cos, sin = np.cos(ang).astype(np.float32), np.sin(ang).astype(np.float32)
    fcos, fsin, perm = np.ones((P, T), np.float32), np.zeros((P, T), np.float32), np.zeros((P, P), np.float32)
    for base in (0, 64):
        for f in range(8):
            fcos[base + f] = fcos[base + 8 + f] = cos[:, f]
            fsin[base + f], fsin[base + 8 + f] = -sin[:, f], sin[:, f]
            perm[base + 8 + f, base + f] = perm[base + f, base + 8 + f] = 1.0
    rope_t = np.stack([x.reshape(TT, P, 8).transpose(1, 0, 2) for x in (cos, sin)], axis=1).reshape(P, 64)
    return {
        "c_ident": np.eye(P, dtype=np.float32), "c_mask": causal, "c_sel": sel, "c_levels": levels.reshape(P, 8 * P),
        "c_stick": stick, "c_cos": fcos, "c_sin": fsin, "c_perm": perm, "c_rope_t": np.ascontiguousarray(rope_t),
    }


INPUTS = ["x", "p", "norm_pre", "norm_post", "att_w_in", "att_b_f", "att_w_out", "rec_w_in", "rec_lb", "rec_out_norm",
          "rec_w_out", "ple_w_proj", "ple_w_gate", "c_2", "w_ada_2", "b_ada_2", "g_pre_mix_2", "w_in_2", "w_up_a_2",
          "w_up_b_2", "w_out_2", "g_post_mix_2", "g_pre_ffn_2", "w_ff1_2", "w_ff2_2", "g_post_ffn_2"]


def kernel(**inputs):
    import concourse.bacc as bacc
    from concourse.bass_utils import run_bass_kernel_spmd

    nc = bacc.Bacc("TRN2", target_bir_lowering=False, num_devices=1)
    arrays = {name: np.ascontiguousarray(inputs[name]) for name in INPUTS}
    arrays.update(constants())
    aps = {name: nc.dram_tensor(name + "_dram", x.shape, mybir.dt.from_np(x.dtype), kind="ExternalInput").ap()
           for name, x in arrays.items()}
    aps["out"] = nc.dram_tensor("out_dram", (1, T, D), F32, kind="ExternalOutput").ap()
    build(nc, aps)
    r = run_bass_kernel_spmd(nc, [{name + "_dram": x for name, x in arrays.items()}], core_ids=[0])
    return r.results[0]["out_dram"]
```

```python
from contextlib import ExitStack

import numpy as np

import concourse.bass as bass
from concourse import mybir

P = 128
T = 512
TT = T // P
D = 1024
KT = D // P
G = 512
HD = 64
NEG = -3.0e38
EPS = 1e-6
TOPK = min(256, T // 4)
ISCALE = (64 ** -0.5) * (8 ** -0.5)
KOFF = [0, 128, 384, 768]
F32 = mybir.dt.float32
F32R = mybir.dt.float32r
I32 = mybir.dt.int32
ALU = mybir.AluOpType
ACT = mybir.ActivationFunctionType
AX = mybir.AxisListType

STAGES = [
    ("norm0", 8, 0, 8, 8), ("qkv0", 24, 12, 0, 0), ("at0", 8, 0, 0, 0), ("g0", 8, 4, 8, 8), ("out0", 8, 4, 0, 0),
    ("ht0", 8, 0, 8, 8), ("pt0", 2, 0, 2, 2), ("ple0", 16, 6, 8, 0),
    ("norm1", 8, 0, 8, 8), ("qfi1", 24, 12, 8, 0), ("on1", 8, 0, 0, 0), ("g1", 8, 4, 8, 8),
    ("out1", 8, 4, 0, 0), ("ht1", 8, 0, 8, 8), ("pt1", 2, 0, 2, 2), ("ple1", 16, 6, 8, 0),
    ("norm2", 8, 0, 8, 8), ("qi2", 8, 2, 4, 0), ("qka2", 16, 4, 8, 0), ("va2", 4, 2, 0, 0),
    ("b2", 12, 6, 0, 0), ("at2", 4, 0, 4, 4), ("merge2", 32, 12, 16, 8), ("out2", 8, 4, 0, 0), ("ga2_0", 2, 0, 0, 0),
    ("norm3", 8, 0, 8, 8), ("ffn", 96, 32, 96, 32), ("ga2_1", 2, 0, 0, 0),
]
BASE, _at = {}, [0, 0, 0, 0]
for _name, *_use in STAGES:
    BASE[_name] = tuple(_at)
    _at = [a + b for a, b in zip(_at, _use)]
CHUNKS = _at[1]


class Chain:

    def __init__(self, eng, sem):
        self.eng, self.sem, self.n, self.turn = eng, sem, 0, None

    def mark(self, ins):
        self.n += 1
        ins.then_inc(self.sem, 1)

    def wait(self):
        self.eng.wait_ge(self.sem, self.n if self.turn is None else self.turn + self.n)

    def after(self, ins):
        self.mark(ins)
        self.wait()

    def enter(self, i, per):
        self.start, self.per, self.turn = self.n, per, i * per

    def leave(self, turns):
        assert self.n == self.start + self.per, (self.n - self.start, self.per)
        self.n, self.turn = self.start + self.per * turns, None


def build(nc, a):
    ctx = ExitStack()
    with ctx:
        def sb(name, shape, dt=F32):
            return ctx.enter_context(nc.sbuf_tensor(name, shape, dt))

        def sem(name):
            return ctx.enter_context(nc.semaphore(name))

        h = sb("h", [P, TT, D])
        slot = {x: sb(f"slot_{x}", [P, 4096]) for x in "ABC"}
        d_at = nc.sbuf_base
        slot["D"] = sb("slot_D", [P, 4096])
        feat = {x: slot[x][:, :].rearrange("p (k t) -> p k t", k=KT) for x in "ABCD"}
        tok = {x: slot[x][:, :].rearrange("p (t d) -> p t d", t=TT) for x in "ABCD"}
        xh, xl = sb("xh", [P, KT, T], F32R), sb("xl", [P, KT, T], F32R)
        y_at = nc.sbuf_base
        yh = sb("yh", [P, KT, T], F32R)
        yl_at = nc.sbuf_base
        yl = sb("yl", [P, KT, T], F32R)
        wk = nc.alloc_sbuf_tensor_at("work_hi", [P, KT, T], F32, offset=y_at)
        wl = nc.alloc_sbuf_tensor_at("work_lo", [P, KT, T], F32, offset=yl_at)
        raw = [sb(f"w_raw{s}", [P, 4, G]) for s in range(2)]
        wh = [sb(f"w_hi{s}", [P, 4, G], F32R) for s in range(2)]
        wlo = [sb(f"w_lo{s}", [P, 4, G], F32R) for s in range(2)]
        ev = sb("ev", [P, 4, T])
        grow = sb("gain_row", [P, D])
        mask = sb("causal_mask", [P, T])
        ident = sb("ident", [P, P])
        gcol = sb("gain_cols", [P, 4, KT])
        modc = sb("mod_cols", [P, 48])
        ocol = sb("out_norm_col", [P, 1])
        lbc = sb("lb_cols", [P, 6, KT])
        stat = sb("stat", [P, 64])
        stat2 = sb("stat2", [P, 32])
        bfc = sb("b_f_col", [P, 1])
        sel = sb("head_select", [P, 16])
        m8 = sb("max8", [P, 8])
        zero, one = sb("zero", [P, 1]), sb("one", [P, 1])

        perm = slot["D"][:, 3072:3200]
        rope = [slot["D"][:, 2048:2560], slot["D"][:, 2560:3072]]
        rope_t = slot["D"][:, 3200:3264].rearrange("p (a t f) -> p a t f", a=2, t=TT)
        wsm = slot["D"][:, 0:576].rearrange("p (k n) -> p k n", k=KT)
        wsm_h = nc.alloc_sbuf_tensor_at("w_small_hi", [P, KT, 72], F32R, offset=d_at + 4 * 576)
        wsm_l = nc.alloc_sbuf_tensor_at("w_small_lo", [P, KT, 72], F32R, offset=d_at + 4 * 1152)
        ada_w = [wk[:, 0:4, :], wk[:, 4:8, :], wl[:, 0:4, :]]
        ada_acc = [wl[:, j, :] for j in range(4, 8)] + [ev[:, j, :] for j in range(4)] + [feat["D"][:, j, :] for j in range(4, 8)]
        tok_p = slot["C"][:, 0:1024].rearrange("p (t d) -> p t d", t=TT)
        tri, ones, strict, strict_neg = (grow[:, j * P:j * P + P] for j in range(4))
        z_t = slot["A"][:, 0:2048].rearrange("p (j t) -> p j t", j=TT)
        sp_t = slot["A"][:, 2048:4096].rearrange("p (j t) -> p j t", j=TT)
        at_t = slot["B"][:, 0:2048].rearrange("p (j t) -> p j t", j=TT)
        ln_t = slot["B"][:, 2048:4096].rearrange("p (j t) -> p j t", j=TT)
        isc = slot["A"][:, 2048:3328]
        level = ev[:, 0:2, :].rearrange("p a (l s) -> p (a l) s", l=4).bitcast(I32)

        bias_q = [nc.alloc_sbuf_tensor_at(f"bias_q{j}", [P, T], F32R, offset=d_at + 2048 * j) for j in range(4)]
        bias_k = nc.alloc_sbuf_tensor_at("bias_k", [P, T], F32R, offset=d_at + 2048 * 4)
        a_q, a_k = [wk[:, j, :] for j in (0, 1)], [wk[:, j, :] for j in (2, 3)]
        a_v = [wk[:, j, :].rearrange("p (t d) -> p t d", t=TT) for j in (4, 5)]
        a_s, a_p = [wl[:, j, :] for j in (0, 1, 2)], [wl[:, j, :] for j in (3, 4, 5)]
        nmax, esum, rsum = stat[:, 16:24], stat[:, 48:56], stat[:, 56:64]
        SB, TB, OB = (0, 1, 5), (2, 3), (4, 6)

        ps = ctx.enter_context(nc.psum_tensor("banks", [P, 8, 512], F32))

        w_landed = [sem(f"w_landed{s}") for s in range(2)]
        w_split, w_ready, w_free = sem("w_split"), sem("w_ready"), sem("w_free")
        bank_full, bank_free = sem("bank_full"), sem("bank_free")
        ev_free, hi_done = sem("ev_free"), sem("hi_done")
        const_in, late_in = sem("const_in"), sem("late_in")
        dve_self, act_self = sem("dve_self"), sem("act_self")
        stored = sem("stored")
        apart = sem("apart")
        S = {}

        def sg(name):
            if name not in S:
                S[name] = sem(name)
            return S[name]

        def cols(w, c0, n=G, k0=0, kn=4):
            return w[k0 * P:(k0 + kn) * P, c0:c0 + n].rearrange("(k p) n -> p k n", p=P)

        win0, wout0 = a["att_w_in"][0], a["att_w_out"][0]
        win1, wout1 = a["rec_w_in"][0], a["rec_w_out"][0]
        win2, wout2 = a["w_in_2"][0], a["w_out_2"][0]
        wada = a["w_ada_2"][0]
        wff1, wff2 = a["w_ff1_2"][0], a["w_ff2_2"][0]

        ctx.enter_context(nc.allow_non_contiguous_dma(reason="small columns of gains"))
        block = ctx.enter_context(nc.Block())

        CONSTS = 15

        @block.sync
        def _(sp):
            for dst, src in (
                (ident[:, :], a["c_ident"]), (mask[:, :], a["c_mask"]), (sel[:, :], a["c_sel"]),
                (gcol[:, 0, :], a["norm_pre"][0].rearrange("(k p) -> p k", p=P)),
                (gcol[:, 1, :], a["norm_pre"][1].rearrange("(k p) -> p k", p=P)),
                (gcol[:, 2, :], a["g_pre_mix_2"][0].rearrange("(k p) -> p k", p=P)),
                (gcol[:, 3, :], a["g_pre_ffn_2"][0].rearrange("(k p) -> p k", p=P)),
                (modc[:, :], a["b_ada_2"][0].rearrange("(k p) -> p k", p=P)),
                (ocol[:, :], a["rec_out_norm"][0].rearrange("(p a) -> p a", a=1)),
                (lbc[:, 0:2, :], a["rec_lb"].rearrange("l (k p) -> p l k", p=P)),
                (stat[:, 32:40], a["c_2"][0].rearrange("(k p) -> p k", p=P)),
                (bfc[0:16, :], a["att_b_f"][0].rearrange("(p a) -> p a", a=1)),
                (bfc[32:48, :], a["att_b_f"][0].rearrange("(p a) -> p a", a=1)),
                (bfc[64:80, :], a["att_b_f"][0].rearrange("(p a) -> p a", a=1)),
                (bfc[96:112, :], a["att_b_f"][0].rearrange("(p a) -> p a", a=1)),
            ):
                sp.dma_start(dst, src).then_inc(const_in, 16)
            sp.dma_start(h[:, :, :], a["x"][0].rearrange("(t p) d -> p t d", p=P)).then_inc(sg("x_in"), 16)

            count = [0]

            def load(src, kn=4):
                c = count[0]
                sp.wait_ge(w_ready, c + 1)
                sp.dma_start(raw[c % 2][:, 0:kn, :], src).then_inc(w_landed[c % 2], 16)
                count[0] += 1

            for c in range(24):
                if c >= 3:
                    sp.wait_ge(sg("ada_used"), c - 2)
                sp.dma_start(ada_w[c % 3], cols(wada, c // 2 * G, k0=4 * (c % 2))).then_inc(sg(f"ada_landed{c % 3}"), 16)
                if c % 2 and count[0] < 12:
                    half = count[0] % 2
                    load(cols(win0, count[0] // 2 * G, k0=4 * half))

            def load_groups(w, n, c0=0):
                if n < 4:
                    for g in range(n):
                        load(cols(w, c0 + g * G))
                        load(cols(w, c0 + g * G, k0=4))
                    return
                first = count[0]
                with sp.Fori(0, n) as g:
                    for half in range(2):
                        sp.wait_ge(w_ready, 2 * g + (first + half + 1))
                        src = w[half * 4 * P:(half + 1) * 4 * P, bass.ds(g * G + c0, G)]
                        sp.dma_start(raw[half][:, :, :], src.rearrange("(k p) n -> p k n", p=P))\
                          .then_inc(w_landed[half], 16)
                count[0] += 2 * n

            def load_ple(l):
                for n in range(2):
                    load(cols(a["ple_w_gate"][l], n * G))
                    load(cols(a["ple_w_gate"][l], n * G, k0=4))
                    load(cols(a["ple_w_proj"][l], n * G, kn=2), kn=2)

            load_groups(win0, 2, 3 * D)
            load_groups(wout0, 2)
            load_ple(0)
            load_groups(win1, 6)
            load_groups(win1, 2, 3 * D)
            load_groups(wout1, 2)
            load_ple(1)
            load_groups(win2, 1, 6 * G)
            load_groups(win2, 3)
            load_groups(win2, 3, 3 * G)
            for n in range(2):
                for gate, up in ((3656, a["w_up_a_2"][0]), (4680, a["w_up_b_2"][0])):
                    load(cols(win2, gate + n * G))
                    load(cols(win2, gate + n * G, k0=4))
                    load(cols(up, n * G))
            load_groups(wout2, 2)
            for i in range(9):
                if i < 8:
                    load(cols(wff1, i * G))
                    load(cols(wff1, i * G, k0=4))
                if i > 0:
                    load(cols(wff2, 0, k0=4 * (i - 1)))
                    load(cols(wff2, G, k0=4 * (i - 1)))
            assert count[0] == CHUNKS, (count[0], CHUNKS)
            sp.wait_ge(sg("final"), TT)
            sp.dma_start(a["out"][0].rearrange("(t p) d -> p t d", p=P), h[:, :, :]).then_inc(stored, 16)
            sp.wait_ge(stored, 16)

        @block.gpsimd
        def _(pool):
            pool.sem_inc(w_ready, 2)
            pool.memset(zero[:, :], 0.0).then_inc(w_split, 1)
            pool.wait_ge(w_split, 1)
            nothing = zero[:, :].unsqueeze(2).broadcast_to([P, 4, G])
            with pool.Fori(0, CHUNKS // 2) as i:
                for s in range(2):
                    pool.wait_ge(w_landed[s], 16 * i + 16)
                    pool.wait_ge(w_free, 2 * i + (s + 1))
                    pool.tensor_tensor(wh[s][:, :, :], raw[s][:, :, :], nothing, ALU.add).then_inc(w_split, 1)
                    pool.wait_ge(w_split, 2 * i + (s + 2))
                    pool.tensor_tensor(wlo[s][:, :, :], raw[s][:, :, :], wh[s][:, :, :].bitcast(F32), ALU.subtract)\
                        .then_inc(w_ready, 1)

        @block.tensor
        def _(pe):
            pe.sem_inc(w_free, 2)

            def bank(n):
                return ps[:, n % 8, :]

            def three(out, s, k, act_h, act_l, ak, m, feature_major, start, stop):
                cut = slice(m * P, m * P + P)
                if feature_major:
                    w_h, w_l, x_h, x_l = wh[s][:, k, cut], wlo[s][:, k, cut], act_h[:, ak, :], act_l[:, ak, :]
                    pe.matmul(out, w_h, x_h, start=start, stop=False)
                    pe.matmul(out, w_h, x_l, start=False, stop=False)
                    return pe.matmul(out, w_l, x_h, start=False, stop=stop)
                w_h, w_l, x_h, x_l = wh[s][:, k, :], wlo[s][:, k, :], act_h[:, ak, cut], act_l[:, ak, cut]
                pe.matmul(out, x_h, w_h, start=start, stop=False)
                pe.matmul(out, x_h, w_l, start=False, stop=False)
                return pe.matmul(out, x_l, w_h, start=False, stop=stop)

            def group(n, c, feature_major, act_h=xh, act_l=xl, a0=0, chunks=2, kn=4, static=0):
                n8, c2 = static
                for ch in range(chunks):
                    pe.wait_ge(w_ready, c + (ch + 3))
                    for m in range(4):
                        if ch == 0:
                            pe.wait_ge(bank_free, n + (m + 1))
                        for k in range(kn):
                            mm = three(ps[:, (n8 + m) % 8, :], (c2 + ch) % 2, k, act_h, act_l, a0 + 4 * ch + k, m,
                                       feature_major, ch == 0 and k == 0, ch == chunks - 1 and k == kn - 1)
                        if ch == chunks - 1:
                            mm.then_inc(bank_full, 1)
                            if m == 3:
                                pe.drain().then_inc(w_free, 1)
                        elif m == 3:
                            mm.then_inc(w_free, 1)

            def groups(name, count, kinds, skip=0, **kw):
                n0, c0 = BASE[name][0] + 4 * skip, BASE[name][1] + 2 * skip
                static = (n0 % 8, c0 % 2)
                if count >= 4:
                    with pe.Fori(0, count // 2) as i:
                        for half in range(2):
                            group(8 * i + (n0 + 4 * half), 4 * i + (c0 + 2 * half), kinds,
                                  static=((n0 + 4 * half) % 8, c0 % 2), **kw)
                else:
                    for g in range(count):
                        group(n0 + 4 * g, c0 + 2 * g, kinds, static=((n0 + 4 * g) % 8, c0 % 2), **kw)

            def transposes(name, src, ready, tiles=KT, skip=0):
                n0 = BASE[name][0]
                pe.wait_ge(*ready)
                for k in range(tiles):
                    n = n0 + k
                    pe.wait_ge(bank_free, n + 1)
                    for t in range(TT):
                        tr = pe.transpose(bank(n)[:, t * P:t * P + P], src[:, t, k * P:k * P + P], ident[:, :])
                    tr.then_inc(bank_full, 1)

            def all_banks_free(name):
                pe.wait_ge(bank_free, BASE[name][0] + 8)

            def attention(x, pairs, bias):
                with pe.Fori(0, pairs // 2) as i:
                    for t in range(19):
                        if t < 16:
                            b, p, r, q = t, t // 8, t // 4 % 2, t % 4
                            hs, kw = slice(HD * r, HD * r + HD), (q + 1) * P
                            if b % 8 == 0:
                                pe.wait_ge(sg(x + "_staged"), 2 * i + (p + 1))
                            if b >= 3:
                                pe.wait_ge(sg(x + "_max"), 16 * i + (b - 2))
                            mm = pe.matmul(ps[:, SB[b % 3], 0:kw], a_q[p][hs, q * P:q * P + P], a_k[p][hs, 0:kw],
                                           start=True, stop=not bias)
                            if bias:
                                mm = pe.matmul(ps[:, SB[b % 3], 0:kw], bias_q[2 * p + r][:, q * P:q * P + P],
                                               bias_k[:, 0:kw], start=False, stop=True)
                            mm.then_inc(sg(x + "_scores"), 1)
                        if 2 <= t < 18:
                            b = t - 2
                            pe.wait_ge(sg(x + "_exp"), 16 * i + (b + 1))
                            if b >= 2:
                                pe.wait_ge(sg(x + "_evac"), 16 * i + (b - 1))
                            for j in range(b % 4 + 1):
                                mm = pe.transpose(ps[:, TB[b % 2], j * P:j * P + P], a_s[b % 3][:, j * P:j * P + P],
                                                  ident[:, :])
                            mm.then_inc(sg(x + "_turned"), 1)
                        if t >= 3:
                            b = t - 3
                            p, r, q = b // 8, b // 4 % 2, b % 4
                            pe.wait_ge(sg(x + "_evac"), 16 * i + (b + 1))
                            if b >= 2:
                                pe.wait_ge(sg(x + "_out"), 16 * i + (b - 1))
                            for j in range(q + 1):
                                mm = pe.matmul(ps[:, OB[b % 2], 0:HD], a_p[b % 3][:, j * P:j * P + P],
                                               a_v[p][:, j, HD * r:HD * r + HD], start=j == 0, stop=j == q)
                            mm.then_inc(sg(x + "_summed"), 1)
                pe.wait_ge(sg(x + "_out"), 8 * pairs)

            pe.wait_ge(const_in, 16 * CONSTS)
            transposes("norm0", tok["D"], (sg("norm0_xn"), TT))
            pe.wait_ge(ev_free, BASE["qkv0"][2] + 4)
            groups("qkv0", 4, True)
            groups("qkv0", 2, False, skip=4)
            all_banks_free("at0")
            pe.wait_ge(sg("ada_acc"), 12)
            for n in range(12):
                for c in range(4):
                    mm = pe.matmul(ps[:, 7, 4 * n + c:4 * n + c + 1], ada_acc[n][:, c * P:c * P + P],
                                   one[:, :], start=True, stop=True)
            mm.then_inc(sg("ada_sum"), 1)
            pe.wait_ge(sg("fl_split"), 1)
            for t in range(TT):
                for k in range(KT):
                    cut = slice(t * P, t * P + P)
                    pe.matmul(ps[:, 0, 16 * t:16 * t + 16], xh[:, k, cut], wsm_h[:, k, 0:16], start=k == 0, stop=False)
                    pe.matmul(ps[:, 0, 16 * t:16 * t + 16], xh[:, k, cut], wsm_l[:, k, 0:16], start=False, stop=False)
                    mm = pe.matmul(ps[:, 0, 16 * t:16 * t + 16], xl[:, k, cut], wsm_h[:, k, 0:16], start=False, stop=k == KT - 1)
            mm.then_inc(sg("fl_full"), 1)
            pe.wait_ge(sg("fl_rows"), 1)
            for t in range(TT):
                mm = pe.transpose(ps[:, 1, t * P:t * P + P], ev[:, 0, t * P:t * P + P], ident[:, :])
            mm.then_inc(sg("fl_turned"), 1)
            attention("fox", 8, True)
            transposes("at0", tok["C"], (sg("fox_out"), 64))
            groups("g0", 2, True)
            pe.wait_ge(ev_free, BASE["out0"][2] + 4)
            groups("out0", 2, False, act_h=yh, act_l=yl)

            def ple(l):
                transposes(f"ht{l}", h, (sg(f"post{l}"), TT))
                transposes(f"pt{l}", tok_p, (sg(f"p_in{l}"), 16), tiles=2)
                n0, c0, u0, _ = BASE[f"ple{l}"]
                pe.wait_ge(ev_free, u0 + 4)
                for n in range(2):
                    group(n0 + 8 * n, c0 + 3 * n, False, static=((n0 + 8 * n) % 8, (c0 + 3 * n) % 2))
                    group(n0 + 8 * n + 4, c0 + 3 * n + 2, False, act_h=yh, act_l=yl, chunks=1, kn=2,
                          static=((n0 + 8 * n + 4) % 8, (c0 + 3 * n + 2) % 2))

            ple(0)

            transposes("norm1", tok["D"], (sg("norm1_xn"), TT))
            pe.wait_ge(ev_free, BASE["qfi1"][2] + 4)
            groups("qfi1", 4, True)
            groups("qfi1", 2, False, skip=4)
            all_banks_free("on1")
            pe.sem_inc(sg("lev_used"), 2)
            pe.sem_inc(sg("rec_full"), 1)
            with pe.Fori(0, 8) as i:
                for l in range(8):
                    pe.wait_ge(sg("lev_qk"), 8 * i + (l + 1))
                    pe.wait_ge(sg("lev_kept"), 8 * i + (l + 1))
                    for j in range(TT):
                        mm = pe.matmul(ps[:, l % 2, j * P:j * P + P], wk[:, 4 + l % 2, j * P:j * P + P],
                                       wk[:, 2 + l % 2, j * P:j * P + P], start=True, stop=True)
                    mm.then_inc(sg("lev_used"), 1)
                pe.wait_ge(sg("kd_ready"), i + 1)
                for j in range(TT - 1):
                    mm = pe.transpose(ps[:, 2, j * P:j * P + P], wl[:, 1, j * P:j * P + P], ident[:, :])
                mm.then_inc(sg("kd_turned"), 1)
                pe.wait_ge(sg("lev_kept"), 8 * i + 10)
                pe.wait_ge(sg("inp_staged"), i + 1)
                pe.wait_ge(sg("kd_copied"), i + 1)
                for j in range(TT):
                    cut = slice(j * P, j * P + P)
                    if j < TT - 1:
                        pe.matmul(ps[:, 4 + j, cut], wl[:, 2, cut], wl[:, 3, cut], start=True, stop=True)\
                            .then_inc(sg("state_add"), 1)
                    mm = pe.matmul(ps[:, 3, cut], wk[:, 6, cut], wl[:, 3, cut], start=True, stop=j == 0)
                    if j > 0:
                        pe.wait_ge(sg("state"), 3 * i + j)
                        mm = pe.matmul(ps[:, 3, cut], wl[:, 0, cut], wl[:, 4, (j % 2) * P:(j % 2) * P + P],
                                       start=False, stop=True)
                mm.then_inc(sg("rec_full"), 1)
            pe.wait_ge(sg("rec_out"), 9)
            transposes("on1", tok["D"], (sg("o_normed"), 1))
            groups("g1", 2, True)
            pe.wait_ge(ev_free, BASE["out1"][2] + 4)
            groups("out1", 2, False, act_h=yh, act_l=yl)
            ple(1)

            transposes("norm2", tok["D"], (sg("norm2_xn"), TT))
            pe.wait_ge(ev_free, BASE["qi2"][2] + 4)

            def rope_group(n, c, u, static):
                group(n, c, True, static=static)
                for m in range(4):
                    pe.wait_ge(bank_free, n + (m + 9))
                    pe.matmul(ps[:, (static[0] + 4 + m) % 8, :], perm[:, :], ev[:, m, :], start=True, stop=True)\
                        .then_inc(bank_full, 1)

            n0, c0, u0, _ = BASE["qi2"]
            pe.wait_ge(sg("rope_in"), 64)
            rope_group(n0, c0, u0, (n0 % 8, c0 % 2))
            n0, c0, u0, _ = BASE["qka2"]
            for g in range(2):
                rope_group(n0 + 8 * g, c0 + 2 * g, u0 + 4 * g, (n0 % 8, c0 % 2))
            n0, c0, _, _ = BASE["va2"]
            group(n0, c0, False, static=(n0 % 8, c0 % 2))
            all_banks_free("b2")
            pe.wait_ge(sg("ki_split"), 1)
            for t in range(TT):
                for k in range(KT):
                    cut = slice(t * P, t * P + P)
                    o = ps[:, 0, 72 * t:72 * t + 72]
                    pe.matmul(o, xh[:, k, cut], wsm_h[:, k, :], start=k == 0, stop=False)
                    pe.matmul(o, xh[:, k, cut], wsm_l[:, k, :], start=False, stop=False)
                    mm = pe.matmul(o, xl[:, k, cut], wsm_h[:, k, :], start=False, stop=k == KT - 1)
            mm.then_inc(sg("ki_full"), 1)
            pe.wait_ge(sg("ki_rows"), 1)
            for t in range(TT):
                mm = pe.transpose(ps[:, 1, t * P:t * P + P], ev[:, 1, t * P:t * P + P], ident[:, :])
            mm.then_inc(sg("ki_turned"), 1)
            pe.wait_ge(sg("ki_ready"), 1)
            for q in range(TT):
                kw = (q + 1) * P
                for hh in range(8):
                    b = 8 * q + hh
                    hs = slice(HD * (hh % 2), HD * (hh % 2) + HD)
                    if b >= 2:
                        pe.wait_ge(sg("idx_relu"), b - 1)
                    pe.matmul(ps[:, 2 + b % 2, 0:kw], feat["A"][hs, hh // 2, q * P:q * P + P], ev[hs, 2, 0:kw],
                              start=True, stop=True).then_inc(sg("idx_full"), 1)
            pe.wait_ge(sg("idx_relu"), 32)
            n0, c0, _, _ = BASE["b2"]
            for g in range(3):
                group(n0 + 4 * g, c0 + 2 * g, g < 2, static=((n0 + 4 * g) % 8, c0 % 2))
            all_banks_free("at2")
            attention("top", 4, False)
            transposes("at2", tok["C"], (sg("top_out"), 32), tiles=4)
            all_banks_free("merge2")

            qs, ks, vs = ev[:, 0, :], ev[:, 1, :], ev[:, 2, :].rearrange("p (t d) -> p t d", t=TT)
            pe.wait_ge(sg("tri_in"), 16)
            with pe.Fori(0, 4) as i:
                pe.wait_ge(sg("stk_staged"), i + 1)
                for r in range(2):
                    hs = slice(HD * r, HD * r + HD)
                    for j in reversed(range(TT)):
                        pe.matmul(ps[:, j, j * P:T], ks[hs, j * P:j * P + P], qs[hs, j * P:T], start=True, stop=True)\
                            .then_inc(sg("stk_z"), 1)
                    for j in reversed(range(TT)):
                        pe.wait_ge(sg("stk_sp"), 8 * i + (4 * r + 4 - j))
                        pe.wait_ge(sg("stk_zc"), 8 * i + (4 * r + 4 - j))
                        for j2 in range(j, TT):
                            mm = pe.matmul(ps[:, j, j2 * P:T], tri if j2 == j else ones,
                                           sp_t[:, j2, j2 * P:T], start=j2 == j, stop=j2 == TT - 1)
                        mm.then_inc(sg("stk_r"), 1)
                    for j in range(TT):
                        if j == 0:
                            pe.wait_ge(sg("stk_att"), 8 * i + (4 * r + 4))
                        mm = pe.matmul(ps[hs, 4, j * P:T], vs[:, j, hs], at_t[:, j, j * P:T], start=j == 0, stop=j == TT - 1)
                    mm.then_inc(sg("stk_o"), 1)
            pe.wait_ge(sg("stk_out"), 4)

            n0, c0, _, _ = BASE["merge2"]
            for n in range(2):
                for b in range(2):
                    ni, ci = n0 + 16 * n + 8 * b, c0 + 6 * n + 3 * b
                    group(ni, ci, True, static=(ni % 8, ci % 2))
                    group(ni + 4, ci + 2, True, act_h=yh, act_l=yl, a0=4 * b, chunks=1,
                          static=((ni + 4) % 8, (ci + 2) % 2))
            pe.wait_ge(sg("merged"), KT)
            groups("out2", 2, False)

            def rows_of(name, col):
                n0 = BASE[name][0]
                for b in range(2):
                    pe.wait_ge(bank_free, n0 + b + 1)
                    for k in range(4):
                        c = modc[:, col + 4 * b + k:col + 4 * b + k + 1]
                        mm = pe.matmul(bank(n0 + b)[:, k * P:k * P + P], c.broadcast_to([P, P]), ident[:, :],
                                       start=True, stop=True)
                    mm.then_inc(bank_full, 1)

            rows_of("ga2_0", 16)
            transposes("norm3", tok["D"], (sg("norm3_xn"), TT))
            n0, c0, u0, _ = BASE["ffn"]
            pe.wait_ge(ev_free, u0 + 4)

            def ff1(n, c, st):
                group(n, c, True, static=st)

            def ff2(n, c, u, st, half):
                pe.wait_ge(ev_free, u)
                for g in range(2):
                    group(n + 4 * g, c + g, False, act_h=yh, act_l=yl, a0=4 * half, chunks=1,
                          static=((st[0] + 4 * g) % 8, (st[1] + g) % 2))

            def at(dn, dc):
                return ((n0 + dn) % 8, (c0 + dc) % 2)

            ff1(n0, c0, at(0, 0))
            with pe.Fori(0, 3) as j:
                n, c, u = 24 * j + n0, 8 * j + c0, 24 * j + u0
                ff1(n + 4, c + 2, at(4, 2))
                ff2(n + 8, c + 4, u + 8, at(8, 4), 0)
                ff1(n + 16, c + 6, at(16, 6))
                ff2(n + 20, c + 8, u + 12 + 8, at(20, 8), 1)
            n, c, u = n0 + 72, c0 + 24, u0 + 72
            ff1(n + 4, c + 2, at(4, 2))
            ff2(n + 8, c + 4, u + 8, at(8, 4), 0)
            ff2(n + 16, c + 6, u + 12, at(16, 6), 1)
            rows_of("ga2_1", 40)

        @block.scalar
        def _(act):
            A = Chain(act, act_self)
            act.sem_inc(bank_free, 8)

            def empty(n, dst, func=ACT.Copy, **kw):
                act.wait_ge(bank_full, n + 1)
                act.activation(dst, ps[:, n % 8, :], func, **kw).then_inc(bank_free, 1)

            def empty_to_ev(n, u, func=ACT.Copy, **kw):
                act.wait_ge(ev_free, u + 1)
                empty(n, ev[:, u % 4, :], func, **kw)

            def squares(name, src, junk, ready):
                for t in range(TT):
                    act.wait_ge(ready[0], ready[1][t])
                    act.activation(junk[:, t, :], src[:, t, :], ACT.Square, accum_out=stat[:, t:t + 1])\
                       .then_inc(sg(name + "_ss"), 1)
                act.wait_ge(sg(name + "_var"), 1)
                act.activation(stat[:, 8:12], stat[:, 4:8], ACT.Sqrt).then_inc(sg(name + "_sd"), 1)

            def turned_with_gain(name, gains, bias=None, tiles=KT):
                n0, _, u0, _ = BASE[name]
                for k in range(tiles):
                    if gains is None:
                        empty_to_ev(n0 + k, u0 + k)
                    else:
                        empty_to_ev(n0 + k, u0 + k, ACT.Identity, scale=gains[:, k:k + 1],
                                    bias=0.0 if bias is None else bias[:, k:k + 1])

            def empty_all(name, count, dst, skip=0, **kw):
                for m in range(count):
                    empty(BASE[name][0] + skip + m, dst(m), **kw)

            def gated(name):
                for m in range(8):
                    empty_to_ev(BASE[name][0] + m, BASE[name][2] + m, ACT.Silu)

            def token_dst(x):
                return lambda m: tok[x][:, m % 4, (m // 4) * G:(m // 4) * G + G]

            def out_and_norm(name, l, gain_src):
                empty_all(name, 8, token_dst("B"))
                act.dma_start(grow[:, :], gain_src.partition_broadcast(P)).then_inc(sg(f"grow{l}"), 16)
                n_last = BASE[name][0] + 8
                squares(f"post{l}", tok["B"], tok["D"], (bank_free, [8 + n_last] * 4))

            def ple(l):
                act.dma_start(tok_p, a["p"][l, 0].rearrange("(t p) d -> p t d", p=P)).then_inc(sg(f"p_in{l}"), 16)
                turned_with_gain(f"ht{l}", None)
                turned_with_gain(f"pt{l}", None, tiles=2)
                n0, _, u0, _ = BASE[f"ple{l}"]
                for n in range(2):
                    for t in range(TT):
                        empty(n0 + 8 * n + t, tok["A"][:, t, n * G:n * G + G], ACT.Sigmoid)
                    for t in range(TT):
                        empty_to_ev(n0 + 8 * n + 4 + t, u0 + 4 * n + t)

            def attention(x, pairs):
                with act.Fori(0, pairs // 2) as i:
                    for t in range(18):
                        if t < 16:
                            b = t
                            kw = (b % 4 + 1) * P
                            act.wait_ge(sg(x + "_max"), 16 * i + (b + 1))
                            act.activation(a_s[b % 3][:, 0:kw], a_s[b % 3][:, 0:kw], ACT.Exp, scale=-1.0,
                                           bias=nmax[:, b % 8:b % 8 + 1], accum_out=esum[:, b % 8:b % 8 + 1])\
                               .then_inc(sg(x + "_exp"), 1)
                        if t >= 2:
                            b = t - 2
                            kw = (b % 4 + 1) * P
                            act.wait_ge(sg(x + "_turned"), 16 * i + (b + 1))
                            if b >= 3:
                                act.wait_ge(sg(x + "_summed"), 16 * i + (b - 2))
                            act.activation(a_p[b % 3][:, 0:kw], ps[:, TB[b % 2], 0:kw], ACT.Copy)\
                               .then_inc(sg(x + "_evac"), 1)

            act.wait_ge(const_in, 16 * CONSTS)
            act.activation(stat[:, 40:48], stat[:, 32:40], ACT.Silu).then_inc(sg("c_silu"), 1)

            act.wait_ge(sg("x_in"), 16)
            squares("norm0", h, tok["B"], (sg("x_in"), [16] * 4))
            turned_with_gain("norm0", gcol[:, 0, :])
            act.dma_start(wsm[:, :, 0:16], cols(win0, 4 * D, 16, kn=KT)).then_inc(sg("fl_in"), 16)
            empty_all("qkv0", 8, lambda m: feat["A"][:, m, :], scale=HD ** -0.5)
            empty_all("qkv0", 8, lambda m: feat["B"][:, m, :], skip=8)
            empty_all("qkv0", 8, token_dst("C"), skip=16)
            act.wait_ge(sg("fl_x"), 1)
            A.after(act.activation(feat["D"][:, 5, :], feat["D"][:, 7, :], ACT.Abs))
            act.activation(feat["D"][:, 5, :], feat["D"][:, 5, :], ACT.Exp, scale=-1.0).then_inc(act_self, 1)
            A.n += 1
            A.wait()
            act.activation(feat["D"][:, 5, :], feat["D"][:, 5, :], ACT.Ln, bias=1.0).then_inc(sg("fl_ln"), 1)
            attention("fox", 8)
            for k in range(KT):
                empty(BASE["at0"][0] + k, feat["A"][:, k, :])
            gated("g0")
            out_and_norm("out0", 0, a["norm_post"][0])
            ple(0)

            act.wait_ge(sg("lb_sub"), 1)
            act.activation(lbc[:, 3:5, :], lbc[:, 3:5, :], ACT.Exp).then_inc(sg("lb_exp"), 1)
            squares("norm1", h, tok["B"], (sg("ple0_h"), [8] * 4))
            turned_with_gain("norm1", gcol[:, 1, :])
            empty_all("qfi1", 8, lambda m: feat["A"][:, m, :])
            for m in range(8):
                empty_to_ev(BASE["qfi1"][0] + 8 + m, BASE["qfi1"][2] + m, ACT.Sigmoid)
            empty_all("qfi1", 8, token_dst("D"), skip=16)
            LT, EB, ED, IS, KTT = wl[:, 7, :], wl[:, 5, :], wl[:, 6, :], wl[:, 3, :], wl[:, 2, :]
            act.sem_inc(sg("rec_out"), 1)
            act.wait_ge(bank_free, BASE["on1"][0] + 8)
            act.wait_ge(sg("f_ready"), KT)
            act.dma_start(ev[:, 0:2, :], a["c_levels"].rearrange("p (a s) -> p a s", a=2)).then_inc(sg("level_in"), 16)
            with act.Fori(0, 8) as i:
                act.wait_ge(sg("cum_done"), i + 1)
                act.sem_inc(apart, 1)
                act.activation(LT, feat["B"][:, i, :], ACT.Ln).then_inc(sg("logs"), 1)
                act.wait_ge(sg("rec_out"), i + 1)
                act.sem_inc(apart, 1)
                act.activation(IS.rearrange("p (t d) -> p t d", t=TT), tok["D"][:, :, bass.ds(i * P, P)], ACT.Copy)\
                   .then_inc(sg("inp_staged"), 1)
                for l in range(7):
                    act.wait_ge(sg("lev_diff"), 8 * i + (l + 1))
                    act.activation(wk[:, l % 2, :], wk[:, l % 2, :], ACT.Exp).then_inc(sg("lev_exp"), 1)
                act.wait_ge(sg("lev_diff"), 8 * i + 8)
                act.activation(ED, ED, ACT.Exp)
                act.activation(EB, wk[:, 7, :], ACT.Exp).then_inc(sg("eb_ready"), 1)
                act.wait_ge(sg("kd_turned"), i + 1)
                act.activation(KTT[:, 0:384], ps[:, 2, 0:384], ACT.Copy).then_inc(sg("kd_copied"), 1)
                act.wait_ge(sg("rec_full"), i + 2)
                for j in range(TT):
                    act.activation(LT[:, 0:P], ps[:, 3, j * P:j * P + P], ACT.Square,
                                   accum_out=stat2[:, bass.ds(i * 4 + j, 1)]).then_inc(sg("junk"), 1)
                    act.wait_ge(sg("junk"), 4 * i + (j + 1))
                act.sem_inc(apart, 1)
                act.activation(tok["D"][:, :, bass.ds(i * P, P)], ps[:, 3, :].rearrange("p (t d) -> p t d", t=TT),
                               ACT.Copy).then_inc(sg("rec_out"), 1)
            act.wait_ge(sg("o_var"), 1)
            act.activation(stat2[:, 0:32], stat2[:, 0:32], ACT.Sqrt).then_inc(sg("o_sd"), 1)
            n0 = BASE["on1"][0]
            for k in range(KT):
                empty(n0 + k, feat["A"][:, k, :], ACT.Copy, scale=ocol[:, 0:1])
            gated("g1")
            out_and_norm("out1", 1, a["norm_post"][1])
            ple(1)

            squares("norm2", h, tok["B"], (sg("ple1_h"), [8] * 4))
            act.wait_ge(sg("gains2"), 2)
            turned_with_gain("norm2", gcol[:, 2, :], modc[:, 0:8])
            act.dma_start(rope[0], a["c_cos"]).then_inc(sg("rope_in"), 16)
            act.dma_start(rope[1], a["c_sin"]).then_inc(sg("rope_in"), 16)
            act.dma_start(perm, a["c_perm"]).then_inc(sg("rope_in"), 16)
            act.dma_start(slot["D"][:, 3200:3264], a["c_rope_t"]).then_inc(sg("rope_in"), 16)
            act.dma_start(wsm, cols(win2, 7 * G, 72, kn=KT)).then_inc(sg("ki_in"), 16)

            def rope_group(n, u, dst, scale):
                for m in range(4):
                    empty_to_ev(n + m, u + m, scale=scale)
                for m in range(4):
                    empty(n + 4 + m, dst(m))

            n0, _, u0, _ = BASE["qi2"]
            rope_group(n0, u0, lambda m: feat["A"][:, m, :], 1.0)
            n0, _, u0, _ = BASE["qka2"]
            rope_group(n0, u0, lambda m: feat["B"][:, m, :], HD ** -0.5)
            rope_group(n0 + 8, u0 + 4, lambda m: feat["B"][:, 4 + m, :], 1.0)
            empty_all("va2", 4, token_dst("C"))
            rt = [ev[:, 3, :], ev[:, 0, :]]
            for q in range(TT):
                for hh in range(8):
                    b = 8 * q + hh
                    if b >= 2:
                        act.wait_ge(sg("idx_acc"), b - 1)
                    act.wait_ge(sg("idx_full"), b + 1)
                    act.activation(rt[b % 2][:, 0:(q + 1) * P], ps[:, 2 + b % 2, 0:(q + 1) * P], ACT.Relu)\
                       .then_inc(sg("idx_relu"), 1)
            empty_all("b2", 4, lambda m: feat["D"][:, m, :], scale=HD ** -0.5)
            empty_all("b2", 4, lambda m: feat["D"][:, 4 + m, :], skip=4)
            empty_all("b2", 4, lambda m: tok["C"][:, m, G:D], skip=8)
            act.dma_start(grow[:, 0:512], a["c_stick"]).then_inc(sg("tri_in"), 16)
            attention("top", 4)
            turned_with_gain("at2", None, tiles=4)
            with act.Fori(0, 4) as i:
                for r in range(2):
                    for j in reversed(range(TT)):
                        z = ps[:, j, j * P:T]
                        act.wait_ge(sg("stk_z"), 8 * i + (4 * r + 4 - j))
                        act.wait_ge(sg("stk_free"), 2 * i + (r + 1))
                        act.activation(z_t[:, j, j * P:T], z, ACT.Copy).then_inc(sg("stk_zc"), 1)
                        act.activation(ln_t[:, j, j * P:T], z, ACT.Abs).then_inc(act_self, 1)
                        act.wait_ge(act_self, A.n + 16 * i + (8 * r + 2 * (TT - 1 - j) + 1))
                        act.activation(ln_t[:, j, j * P:T], ln_t[:, j, j * P:T], ACT.Exp, scale=-1.0).then_inc(act_self, 1)
                        act.wait_ge(act_self, A.n + 16 * i + (8 * r + 2 * (TT - 1 - j) + 2))
                        act.activation(ln_t[:, j, j * P:T], ln_t[:, j, j * P:T], ACT.Ln, bias=1.0).then_inc(sg("stk_ln"), 1)
                    for j in reversed(range(TT)):
                        act.wait_ge(sg("stk_arg"), 8 * i + (4 * r + 4 - j))
                        act.activation(at_t[:, j, j * P:T], z_t[:, j, j * P:T], ACT.Exp).then_inc(sg("stk_att"), 1)
            A.n += 64

            n0, _, u0, _ = BASE["merge2"]
            for n in range(2):
                for b in range(2):
                    gates = feat["BC"[b]]
                    for m in range(4):
                        empty(n0 + 16 * n + 8 * b + m, gates[:, 4 * n + m, :], ACT.Sigmoid)
                    for m in range(4):
                        empty_to_ev(n0 + 16 * n + 8 * b + 4 + m, u0 + 8 * n + 4 * b + m)

            def rows_of(name, l):
                for b in range(2):
                    empty(BASE[name][0] + b, slot["C"][:, b * G:b * G + G])

            out_and_norm("out2", 2, a["g_post_mix_2"][0])
            rows_of("ga2_0", 2)
            squares("norm3", h, tok["B"], (sg("post2"), [1, 2, 3, 4]))
            turned_with_gain("norm3", gcol[:, 3, :], modc[:, 24:32])
            n0, _, u0, _ = BASE["ffn"]
            n, u = n0, u0
            for i in range(9):
                if i < 8:
                    for m in range(4):
                        empty_to_ev(n + m, u + m, ACT.Relu)
                    n, u = n + 4, u + 4
                if i > 0:
                    for m in range(8):
                        empty_to_ev(n + m, u + m)
                    n, u = n + 8, u + 8
            act.dma_start(grow[:, :], a["g_post_ffn_2"][0].partition_broadcast(P)).then_inc(sg("grow3"), 16)
            squares("post3", tok["B"], tok["D"], (ev_free, [4 + u] * 4))
            rows_of("ga2_1", 3)

        @block.vector
        def _(dve):
            V = Chain(dve, dve_self)
            dve.sem_inc(ev_free, 4)
            X = (xh, xl)
            Y = (yh, yl)

            def split(n, u, s, dst, k):
                dve.wait_ge(bank_free, n + 9)
                split_tile(ev[:, u % 4, :], s, dst, k).then_inc(ev_free, 1)

            def split_tile(src, s, dst, k):
                dve.tensor_copy(dst[0][:, k, :], src).then_inc(hi_done, 1)
                dve.wait_ge(hi_done, s + 1)
                return dve.tensor_tensor(dst[1][:, k, :], src, dst[0][:, k, :].bitcast(F32), ALU.subtract)

            def split_all(name, dst, tiles=KT):
                n0, _, u0, s0 = BASE[name]
                for k in range(tiles):
                    split(n0 + k, u0 + k, s0 + k, dst, k)

            def rstd(name):
                dve.wait_ge(sg(name + "_ss"), TT)
                dve.tensor_scalar(stat[:, 4:8], stat[:, 0:4], 1.0 / D, EPS, ALU.mult, ALU.add).then_inc(sg(name + "_var"), 1)
                dve.wait_ge(sg(name + "_sd"), 1)
                V.after(dve.reciprocal(stat[:, 12:16], stat[:, 8:12]))

            def norm(name):
                rstd(name)
                for t in range(TT):
                    dve.tensor_scalar(tok["D"][:, t, :], h[:, t, :], stat[:, 12 + t:13 + t], None, ALU.mult)\
                       .then_inc(sg(name + "_xn"), 1)

            def post(l, last=None):
                rstd(f"post{l}")
                dve.wait_ge(sg(f"grow{l}"), 16)
                if l >= 2:
                    dve.wait_ge(bank_free, BASE[f"ga2_{l - 2}"][0] + 10)
                    V.after(dve.tensor_tensor(grow[:, :], grow[:, :], slot["C"][:, 0:D], ALU.mult))
                for t in range(TT):
                    y = tok["B"][:, t, :]
                    V.after(dve.scalar_tensor_tensor(out=y, in0=y, scalar=stat[:, 12 + t:13 + t], in1=grow[:, :],
                                                     op0=ALU.mult, op1=ALU.mult))
                    dve.tensor_tensor(h[:, t, :], h[:, t, :], y, ALU.add).then_inc(last or sg(f"post{l}"), 1)

            def gated(name):
                n0, _, u0, s0 = BASE[name]
                for m in range(8):
                    dve.wait_ge(bank_free, n0 + m + 9)
                    e = ev[:, (u0 + m) % 4, :]
                    V.after(dve.tensor_tensor(e, e, feat["A"][:, m, :], ALU.mult))
                    split_tile(e, s0 + m, Y, m).then_inc(ev_free, 1)

            def ple(l):
                dve.wait_ge(sg(f"post{l}"), TT)
                split_all(f"ht{l}", X)
                split_all(f"pt{l}", Y, tiles=2)
                n0, _, u0, _ = BASE[f"ple{l}"]
                for n in range(2):
                    for t in range(TT):
                        dve.wait_ge(bank_free, n0 + 8 * n + 4 + t + 9)
                        e = ev[:, (u0 + 4 * n + t) % 4, :]
                        hh = h[:, t, n * G:n * G + G]
                        V.after(dve.tensor_tensor(e, e, tok["A"][:, t, n * G:n * G + G], ALU.mult))
                        V.after(dve.tensor_tensor(hh, hh, e, ALU.add))
                        dve.sem_inc(ev_free, 1)
                        dve.sem_inc(sg(f"ple{l}_h"), 1)

            def attention(x, pairs, src, strip, bias):
                per_turn = 16
                with dve.Fori(0, pairs // 2) as i:
                    V.enter(i, per_turn)

                    def stage(p):
                        if p == 0:
                            dve.sem_inc(apart, 1)
                        dve.tensor_copy(a_q[p], src[0][:, 2 * i + p, :])
                        dve.tensor_copy(a_k[p], src[1][:, 2 * i + p, :])
                        if bias:
                            for r in range(2):
                                dve.tensor_scalar(bias_q[2 * p + r][:, :], feat["D"][:, 7, :],
                                                  sel[:, bass.ds(4 * i + (2 * p + r), 1)], None, ALU.mult)
                        dve.tensor_copy(a_v[p], src[2][:, :, bass.ds(i * 2 * P + p * P, P)]).then_inc(sg(x + "_staged"), 1)

                    stage(0)
                    for t in range(20):
                        if t < 16:
                            b = t
                            kw = (b % 4 + 1) * P
                            dve.wait_ge(sg(x + "_scores"), 16 * i + (b + 1))
                            if b >= 3:
                                dve.wait_ge(sg(x + "_turned"), 16 * i + (b - 2))
                            dve.sem_inc(apart, 1)
                            dve.tensor_tensor_reduce(a_s[b % 3][:, 0:kw], ps[:, SB[b % 3], 0:kw], strip(b % 4), -1.0,
                                                     -NEG, ALU.add, ALU.min, nmax[:, b % 8:b % 8 + 1])\
                               .then_inc(sg(x + "_max"), 1)
                        if t == 3:
                            stage(1)
                        if t >= 4:
                            b = t - 4
                            q, o = b % 4, b % 8
                            dve.wait_ge(sg(x + "_exp"), 16 * i + (b + 1))
                            V.after(dve.reciprocal(rsum[:, o:o + 1], esum[:, o:o + 1]))
                            dve.wait_ge(sg(x + "_summed"), 16 * i + (b + 1))
                            dve.tensor_scalar(tok["C"][:, q, bass.ds(i * 2 * P + b // 4 * HD, HD)], ps[:, OB[b % 2], 0:HD],
                                              rsum[:, o:o + 1], None, ALU.mult).then_inc(sg(x + "_out"), 1)
                V.leave(pairs // 2)

            def modulation():
                dve.memset(one[:, :], 1.0)
                dve.wait_ge(sg("c_silu"), 1)
                for n in range(12):
                    acc = ada_acc[n]
                    for c in (2 * n, 2 * n + 1):
                        dve.wait_ge(sg(f"ada_landed{c % 3}"), 16 * (c // 3 + 1))
                        for k in range(4):
                            w = ada_w[c % 3][:, k, :]
                            s = stat[:, 40 + 4 * (c % 2) + k:41 + 4 * (c % 2) + k]
                            if c % 2 == 0 and k == 0:
                                V.after(dve.tensor_scalar(acc, w, s, None, ALU.mult))
                            else:
                                V.after(dve.scalar_tensor_tensor(out=acc, in0=w, scalar=s, in1=acc, op0=ALU.mult, op1=ALU.add))
                        dve.sem_inc(sg("ada_used"), 1)
                    dve.sem_inc(sg("ada_acc"), 1)
                dve.wait_ge(sg("ada_sum"), 1)
                V.after(dve.tensor_tensor(modc[:, :], modc[:, :], ps[:, 7, 0:48], ALU.add))
                for g, c in ((2, 8), (3, 32)):
                    dve.scalar_tensor_tensor(out=gcol[:, g, :], in0=modc[:, c:c + 8], scalar=1.0, in1=gcol[:, g, :],
                                             op0=ALU.add, op1=ALU.mult).then_inc(sg("gains2"), 1)

            dve.wait_ge(const_in, 16 * CONSTS)
            V.after(dve.tensor_tensor(lbc[:, 2, :], lbc[:, 0, :], lbc[:, 1, :], ALU.max))
            dve.tensor_tensor(lbc[:, 3, :], lbc[:, 0, :], lbc[:, 2, :], ALU.subtract)
            dve.tensor_tensor(lbc[:, 4, :], lbc[:, 1, :], lbc[:, 2, :], ALU.subtract).then_inc(sg("lb_sub"), 1)

            norm("norm0")
            split_all("norm0", X)
            modulation()
            dve.wait_ge(sg("fl_in"), 16)
            V.after(dve.tensor_copy(wsm_h[:, :, 0:16], wsm[:, :, 0:16]))
            V.after(dve.tensor_tensor(wsm_l[:, :, 0:16], wsm[:, :, 0:16], wsm_h[:, :, 0:16].bitcast(F32), ALU.subtract))
            dve.sem_inc(sg("fl_split"), 1)
            fr = ev[:, 0, :].rearrange("p (t c) -> p t c", t=TT)
            V.after(dve.memset(ev[:, 0, :], 0.0))
            dve.wait_ge(sg("fl_full"), 1)
            fp = ps[:, 0, 0:64].rearrange("p (t c) -> p t c", t=TT)
            for r in (0, 32, 64, 96):
                V.after(dve.tensor_copy(fr[:, :, r:r + 16], fp))
            dve.sem_inc(sg("fl_rows"), 1)
            dve.wait_ge(sg("fl_turned"), 1)
            C5, C6, C7 = (feat["D"][:, k, :] for k in (5, 6, 7))
            V.after(dve.memset(stat[:, 24:25], 0.0))
            for r in (0, 32, 64, 96):
                V.after(dve.tensor_copy(stat[r:r + 16, 24:25], bfc[r:r + 16, :]))
            V.after(dve.tensor_scalar(C7, ps[:, 1, :], stat[:, 24:25], None, ALU.add))
            dve.sem_inc(sg("fl_x"), 1)
            dve.wait_ge(sg("fl_ln"), 1)
            V.after(dve.tensor_scalar(C7, C7, 0.0, None, ALU.min))
            V.after(dve.tensor_tensor(C7, C7, C5, ALU.subtract))
            V.after(dve.tensor_tensor_scan(C6, C7, C7, 0.0, ALU.add, ALU.bypass))
            V.after(dve.tensor_copy(bias_k[:, :], C6))
            V.after(dve.tensor_tensor(C5, C6, bias_k[:, :].bitcast(F32), ALU.subtract))
            V.after(dve.tensor_copy(C7[0:32, :], bias_k[0:32, :].bitcast(F32)))
            V.after(dve.tensor_copy(C7[32:64, :], C5[32:64, :]))
            V.after(dve.memset(C7[64:128, :], -1.0))
            V.after(dve.tensor_copy(bias_k[96:128, :], C5[96:128, :]))
            V.after(dve.tensor_scalar(bias_k[0:64, :], C5[0:64, :], 0.0, 1.0, ALU.mult, ALU.add))
            attention("fox", 8, (feat["A"], feat["B"], tok["C"]), lambda q: mask[:, 384 - q * P:512], True)
            gated("g0")
            post(0)
            ple(0)

            dve.wait_ge(sg("lb_exp"), 1)
            V.after(dve.tensor_tensor(lbc[:, 0, :], lbc[:, 3, :], lbc[:, 4, :], ALU.add))
            V.after(dve.reciprocal(lbc[:, 1, :], lbc[:, 0, :]))
            V.after(dve.tensor_tensor(lbc[:, 3, :], lbc[:, 3, :], lbc[:, 1, :], ALU.mult))
            V.after(dve.tensor_tensor(lbc[:, 4, :], lbc[:, 4, :], lbc[:, 1, :], ALU.mult))
            V.after(dve.tensor_tensor(lbc[:, 1, :], lbc[:, 3, :], lbc[:, 4, :], ALU.add))
            V.after(dve.tensor_tensor(lbc[:, 1, :], lbc[:, 1, :], lbc[:, 3, :], ALU.subtract))
            V.after(dve.tensor_scalar(lbc[:, 0, :], lbc[:, 1, :], -1.0, 1.0, ALU.mult, ALU.add))
            V.after(dve.tensor_scalar(lbc[:, 5, :], lbc[:, 0, :], -1.0, None, ALU.mult))
            dve.wait_ge(sg("ple0_h"), 8)
            norm("norm1")
            split_all("norm1", X)
            n0, _, u0, _ = BASE["qfi1"]
            for m in range(8):
                dve.wait_ge(bank_free, n0 + 8 + m + 9)
                e = ev[:, (u0 + m) % 4, :]
                V.after(dve.tensor_scalar(feat["B"][:, m, :], e, lbc[:, 0, m:m + 1], lbc[:, 1, m:m + 1], ALU.mult, ALU.add))
                V.after(dve.tensor_scalar(feat["B"][:, m, :], feat["B"][:, m, :], 2.0 ** -63, None, ALU.max))
                V.after(dve.tensor_scalar(feat["C"][:, m, :], e, lbc[:, 5, m:m + 1], lbc[:, 0, m:m + 1], ALU.mult, ALU.add))
                dve.sem_inc(ev_free, 1)
                dve.sem_inc(sg("f_ready"), 1)
            dve.wait_ge(sg("level_in"), 16)
            LT, EB, ED, BT, SC = wl[:, 7, :], wl[:, 5, :], wl[:, 6, :], wk[:, 7, :], wk[:, 6, :]
            ST = [wl[:, 4, 0:P], wl[:, 4, P:2 * P]]
            V.after(dve.memset(wk[:, 2:7, :], 0.0))
            dve.sem_inc(sg("cum_done"), 1)
            dve.sem_inc(sg("lev_kept"), 2)
            with dve.Fori(0, 8) as i:
                V.enter(i, 4 + 2 * 8 + 2 * 8 + 8 + 3 + 3)
                dve.wait_ge(sg("logs"), i + 1)
                for j in range(TT):
                    cut = slice(j * P, j * P + P)
                    V.mark(dve.tensor_tensor_scan(BT[:, cut], LT[:, cut], LT[:, cut], 0.0, ALU.add, ALU.bypass))
                V.wait()
                dve.sem_inc(sg("cum_done"), 1)

                def diff(l):
                    if l == 7:
                        bl = BT.rearrange("p (n c) -> p n c", c=P)
                        V.mark(dve.tensor_tensor(ED.rearrange("p (n c) -> p n c", c=P),
                                                 bl[:, :, P - 1:P].broadcast_to([P, TT, P]), bl, ALU.subtract))
                        V.mark(dve.tensor_copy(m8[:, 0:1], BT[:, 0:1]))
                    else:
                        half = 64 >> l
                        b3 = BT.rearrange("p (n c) -> p n c", c=2 * half)
                        e3 = wk[:, l % 2, :].rearrange("p (n c) -> p n c", c=2 * half)
                        mid = b3[:, :, half - 1:half].broadcast_to([P, T // (2 * half), half])
                        V.mark(dve.tensor_tensor(e3[:, :, 0:half], mid, b3[:, :, 0:half], ALU.subtract))
                        V.mark(dve.tensor_tensor(e3[:, :, half:2 * half], b3[:, :, half:2 * half], mid, ALU.subtract))
                    V.wait()
                    dve.sem_inc(sg("lev_diff"), 1)

                def decay(l):
                    o = l % 2
                    dve.wait_ge(sg("lev_used"), 8 * i + (l + 1))
                    if l == 7:
                        dve.sem_inc(apart, 1)
                        V.mark(dve.tensor_copy(wk[:, 2 + o, :], feat["A"][:, i, :]))
                        V.mark(dve.tensor_copy(wk[:, 4 + o, :], feat["C"][:, i, :]))
                    else:
                        half = 64 >> l
                        dve.wait_ge(sg("lev_exp"), 7 * i + (l + 1))
                        v = [x.rearrange("p (n c) -> p n c", c=2 * half) for x in
                             (wk[:, 2 + o, :], wk[:, 4 + o, :], wk[:, o, :], feat["A"][:, i, :], feat["C"][:, i, :])]
                        hi, lo = slice(half, 2 * half), slice(0, half)
                        V.mark(dve.tensor_tensor(v[0][:, :, hi], v[3][:, :, hi], v[2][:, :, hi], ALU.mult))
                        V.mark(dve.tensor_tensor(v[1][:, :, lo], v[4][:, :, lo], v[2][:, :, lo], ALU.mult))
                    V.wait()
                    dve.sem_inc(sg("lev_qk"), 1)

                def keep(l):
                    dve.wait_ge(sg("lev_used"), 8 * i + (l + 3))
                    if l == 0:
                        dve.wait_ge(sg("rec_full"), i + 1)
                    mk = level[:, l:l + 1, :].broadcast_to([P, TT, P])
                    dve.sem_inc(apart, 1)
                    V.after(dve.copy_predicated(SC.rearrange("p (n c) -> p n c", c=P), mk,
                                                ps[:, l % 2, :].rearrange("p (n c) -> p n c", c=P)))
                    dve.sem_inc(sg("lev_kept"), 1)

                diff(0)
                for l in range(8):
                    if l < 7:
                        diff(l + 1)
                    decay(l)
                    if l > 0:
                        keep(l - 1)
                dve.wait_ge(sg("eb_ready"), i + 1)
                V.mark(dve.tensor_tensor(wl[:, 0, :], feat["A"][:, i, :], EB, ALU.mult))
                V.mark(dve.tensor_tensor(wl[:, 1, :], feat["C"][:, i, :], ED, ALU.mult))
                V.wait()
                dve.sem_inc(sg("kd_ready"), 1)
                keep(7)
                V.mark(dve.tensor_copy(m8[:, 0:1], BT[:, 0:1]))
                for j in range(TT - 1):
                    dve.wait_ge(sg("state_add"), 3 * i + (j + 1))
                    u = ps[:, 4 + j, j * P:j * P + P]
                    if j == 0:
                        ins = dve.tensor_copy(ST[1], u)
                    else:
                        ins = dve.scalar_tensor_tensor(out=ST[(j + 1) % 2], in0=ST[j % 2],
                                                       scalar=EB[:, j * P + P - 1:j * P + P], in1=u,
                                                       op0=ALU.mult, op1=ALU.add)
                    V.after(ins)
                    dve.sem_inc(sg("state"), 1)
                V.wait()
            V.leave(8)
            dve.wait_ge(sg("rec_out"), 9)
            V.after(dve.tensor_scalar(stat2[:, 0:32], stat2[:, 0:32], 1.0 / P, EPS, ALU.mult, ALU.add))
            dve.sem_inc(sg("o_var"), 1)
            dve.wait_ge(sg("o_sd"), 1)
            V.after(dve.reciprocal(stat2[:, 0:32], stat2[:, 0:32]))
            o4 = slot["D"][:, :].rearrange("p (t h d) -> p t h d", t=TT, h=8)
            r4 = stat2[:, 0:32].rearrange("p (h t) -> p t h", t=TT)
            for t in range(TT):
                V.after(dve.tensor_tensor(o4[:, t], o4[:, t], r4[:, t, :].unsqueeze(2).broadcast_to([P, 8, P]), ALU.mult))
            dve.sem_inc(sg("o_normed"), 1)
            gated("g1")
            post(1)
            ple(1)

            dve.wait_ge(sg("ple1_h"), 8)
            norm("norm2")
            split_all("norm2", X)
            dve.wait_ge(sg("ki_in"), 16)
            V.after(dve.tensor_copy(wsm_h[:, :, :], wsm))
            V.after(dve.tensor_tensor(wsm_l[:, :, :], wsm, wsm_h[:, :, :].bitcast(F32), ALU.subtract))
            dve.sem_inc(sg("ki_split"), 1)
            dve.wait_ge(sg("rope_in"), 64)

            def rope_group(n, u, dst):
                for m in range(4):
                    dve.wait_ge(bank_free, n + 4 + m + 9)
                    e = ev[:, (u + m) % 4, :]
                    V.mark(dve.tensor_tensor(dst(m), dst(m), rope[1], ALU.mult))
                    V.mark(dve.tensor_tensor(e, e, rope[0], ALU.mult))
                    V.wait()
                    V.after(dve.tensor_tensor(dst(m), dst(m), e, ALU.add))
                    dve.sem_inc(ev_free, 1)

            n0, _, u0, _ = BASE["qi2"]
            rope_group(n0, u0, lambda m: feat["A"][:, m, :])
            n0, _, u0, _ = BASE["qka2"]
            rope_group(n0, u0, lambda m: feat["B"][:, m, :])
            rope_group(n0 + 8, u0 + 4, lambda m: feat["B"][:, 4 + m, :])
            dve.wait_ge(sg("ki_full"), 1)
            smv = ev[:, 0, 0:288].rearrange("p (t c) -> p t c", t=TT)
            kr = ev[:, 1, :].rearrange("p (t c) -> p t c", t=TT)
            tmp = ev[:, 0, 288:352].rearrange("p (a t f) -> p a t f", a=2, t=TT)
            V.after(dve.tensor_copy(smv, ps[:, 0, 0:288].rearrange("p (t c) -> p t c", t=TT)))
            V.mark(dve.tensor_scalar(stat2[:, 0:32].rearrange("p (t h) -> p t h", t=TT), smv[:, :, 64:72], ISCALE, None, ALU.mult))
            V.mark(dve.tensor_copy(kr[:, :, 0:64], smv[:, :, 0:64]))
            x1, x2, cs, sn = smv[:, :, 0:8], smv[:, :, 8:16], rope_t[:, 0], rope_t[:, 1]
            V.mark(dve.tensor_tensor(tmp[:, 0], x2, sn, ALU.mult))
            V.mark(dve.tensor_tensor(tmp[:, 1], x1, sn, ALU.mult))
            V.wait()
            V.mark(dve.tensor_tensor(kr[:, :, 0:8], x1, cs, ALU.mult))
            V.mark(dve.tensor_tensor(kr[:, :, 8:16], x2, cs, ALU.mult))
            V.wait()
            V.mark(dve.tensor_tensor(kr[:, :, 0:8], kr[:, :, 0:8], tmp[:, 0], ALU.subtract))
            V.mark(dve.tensor_tensor(kr[:, :, 8:16], kr[:, :, 8:16], tmp[:, 1], ALU.add))
            V.wait()
            V.after(dve.tensor_copy(kr[:, :, 64:128], kr[:, :, 0:64]))
            dve.sem_inc(sg("ki_rows"), 1)
            dve.wait_ge(sg("ki_turned"), 1)
            V.after(dve.tensor_copy(ev[:, 2, :], ps[:, 1, :]))
            dve.sem_inc(sg("ki_ready"), 1)
            rt = [ev[:, 3, :], ev[:, 0, :]]
            for q in range(TT):
                kw = (q + 1) * P
                strip = isc[:, KOFF[q]:KOFF[q] + kw]
                for hh in range(8):
                    b = 8 * q + hh
                    dve.wait_ge(sg("idx_relu"), b + 1)
                    V.after(dve.scalar_tensor_tensor(out=strip, in0=rt[b % 2][:, 0:kw],
                                                     scalar=stat2[:, 8 * q + hh:8 * q + hh + 1],
                                                     in1=mask[:, 384 - q * P:512] if hh == 0 else strip,
                                                     op0=ALU.mult, op1=ALU.add))
                    dve.sem_inc(sg("idx_acc"), 1)
            dve.wait_ge(sg("idx_relu"), 32)
            tw, eq = slot["A"][:, 0:512], slot["A"][:, 512:1024]
            V.after(dve.tensor_copy(isc[:, 0:P], mask[:, 384:512]))
            for q in range(1, TT):
                kw = (q + 1) * P
                strip, w, e = isc[:, KOFF[q]:KOFF[q] + kw], tw[:, 0:kw], eq[:, 0:kw]
                V.after(dve.tensor_copy(w, strip))
                for r in range(TOPK // 8):
                    V.after(dve.max(m8[:, :], w))
                    if r < TOPK // 8 - 1:
                        V.after(dve.match_replace(w, m8[:, :], w, NEG))
                V.after(dve.tensor_scalar(e, strip, m8[:, 7:8], None, ALU.is_equal))
                V.after(dve.tensor_scalar(w, strip, m8[:, 7:8], None, ALU.is_gt))
                V.after(dve.tensor_reduce(stat[:, 24:25], w, AX.X, ALU.add))
                V.after(dve.tensor_scalar(stat[:, 25:26], stat[:, 24:25], -1.0, float(TOPK), ALU.mult, ALU.add))
                V.after(dve.tensor_tensor_scan(strip, e, e, 0.0, ALU.add, ALU.bypass))
                V.after(dve.scalar_tensor_tensor(out=e, in0=strip, scalar=stat[:, 25:26], in1=e, op0=ALU.is_le, op1=ALU.mult))
                V.after(dve.tensor_tensor(w, w, e, ALU.add))
                V.after(dve.tensor_scalar(strip, w, 1.0, -NEG, ALU.subtract, ALU.mult))
            dve.wait_ge(bank_free, BASE["at2"][0] + 8)

            attention("top", 4, (feat["B"], feat["B"][:, 4:8, :], tok["C"]), lambda q: isc[:, KOFF[q]:KOFF[q] + (q + 1) * P],
                      False)
            split_all("at2", Y, tiles=4)

            dve.wait_ge(sg("tri_in"), 16)
            dve.sem_inc(sg("stk_free"), 1)
            with dve.Fori(0, 4) as i:
                V.enter(i, 2 * (4 * 2 + 4 * 2) + 2)
                dve.tensor_copy(ev[:, 0, :], feat["D"][:, i, :])
                dve.tensor_copy(ev[:, 1, :], feat["D"][:, i + 4, :])
                dve.tensor_copy(ev[:, 2, :].rearrange("p (t d) -> p t d", t=TT), tok["C"][:, :, bass.ds(i * P + G, P)])\
                   .then_inc(sg("stk_staged"), 1)
                for r in range(2):
                    for j in reversed(range(TT)):
                        dve.wait_ge(sg("stk_ln"), 8 * i + (4 * r + 4 - j))
                        V.after(dve.scalar_tensor_tensor(out=sp_t[:, j, j * P:T], in0=z_t[:, j, j * P:T], scalar=0.0,
                                                         in1=ln_t[:, j, j * P:T], op0=ALU.max, op1=ALU.add))
                        dg = sp_t[:, j, j * P:j * P + P]
                        V.after(dve.tensor_tensor(dg, dg, strict, ALU.mult))
                        dve.sem_inc(sg("stk_sp"), 1)
                    for j in reversed(range(TT)):
                        dve.wait_ge(sg("stk_r"), 8 * i + (4 * r + 4 - j))
                        V.after(dve.tensor_tensor(z_t[:, j, j * P:T], z_t[:, j, j * P:T], ps[:, j, j * P:T], ALU.subtract))
                        dg = z_t[:, j, j * P:j * P + P]
                        V.after(dve.tensor_tensor(dg, dg, strict_neg, ALU.add))
                        dve.sem_inc(sg("stk_arg"), 1)
                    dve.wait_ge(sg("stk_o"), 2 * i + (r + 1))
                    dve.sem_inc(sg("stk_free"), 1)
                o = ev[:, 3, :]
                V.after(dve.tensor_copy(o, ps[:, 4, :]))
                V.after(dve.tensor_copy(yh[:, i + 4, :], o))
                dve.tensor_tensor(yl[:, i + 4, :], o, yh[:, i + 4, :].bitcast(F32), ALU.subtract).then_inc(sg("stk_out"), 1)
            V.leave(4)

            n0, _, u0, s0 = BASE["merge2"]
            for n in range(2):
                for b in range(2):
                    for m in range(4):
                        dve.wait_ge(bank_free, n0 + 16 * n + 8 * b + 4 + m + 9)
                        e, am = ev[:, (u0 + 8 * n + 4 * b + m) % 4, :], feat["A"][:, 4 * n + m, :]
                        gate = feat["BC"[b]][:, 4 * n + m, :]
                        if b == 0:
                            V.after(dve.tensor_tensor(am, e, gate, ALU.mult))
                        else:
                            V.after(dve.tensor_tensor(e, e, gate, ALU.mult))
                            V.after(dve.tensor_tensor(am, am, e, ALU.add))
                        dve.sem_inc(ev_free, 1)
            for k in range(KT):
                split_tile(feat["A"][:, k, :], s0 + k, X, k).then_inc(sg("merged"), 1)
            post(2)
            dve.wait_ge(sg("post2"), TT)
            norm("norm3")
            split_all("norm3", X)
            n0, _, u0, s0 = BASE["ffn"]
            n, u, s = n0, u0, s0
            for i in range(9):
                if i < 8:
                    for m in range(4):
                        dve.wait_ge(bank_free, n + m + 9)
                        e = ev[:, (u + m) % 4, :]
                        V.after(dve.tensor_tensor(e, e, e, ALU.mult))
                        split_tile(e, s + m, Y, 4 * (i % 2) + m).then_inc(ev_free, 1)
                    n, u, s = n + 4, u + 4, s + 4
                if i > 0:
                    for m in range(8):
                        dve.wait_ge(bank_free, n + m + 9)
                        e = ev[:, (u + m) % 4, :]
                        y = tok["B"][:, m % 4, (m // 4) * G:(m // 4) * G + G]
                        if i == 1:
                            V.after(dve.tensor_copy(y, e))
                        else:
                            V.after(dve.tensor_tensor(y, y, e, ALU.add))
                        dve.sem_inc(ev_free, 1)
                    n, u = n + 8, u + 8
            post(3, last=sg("final"))


def constants():
    i = np.arange(P)
    causal = np.zeros((P, T), np.float32)
    causal[:, 384:] = np.where(i[None, :] > i[:, None], NEG, 0.0)
    sel = np.zeros((P, 16), np.float32)
    for x in range(16):
        sel[x::32, x] = 1.0
    s, t = i[:, None], i[None, :]
    levels = np.zeros((P, 8, P), np.float32)
    for l in range(7):
        half = 64 >> l
        levels[:, l] = (s // (2 * half) == t // (2 * half)) & (s % (2 * half) < half) & (t % (2 * half) >= half)
    levels[:, 7] = s == t
    stick = np.concatenate([(s >= t).astype(np.float32), np.ones((P, P), np.float32), (s < t).astype(np.float32),
                            np.where(s < t, 0.0, NEG).astype(np.float32)], axis=1)
    pos = np.arange(T, dtype=np.float32)
    freq = np.float32(500000.0) ** (-np.arange(0, 16, 2, dtype=np.float32) / np.float32(16))
    ang = pos[:, None] * freq[None, :].astype(np.float32)
    cos, sin = np.cos(ang).astype(np.float32), np.sin(ang).astype(np.float32)
    fcos, fsin, perm = np.ones((P, T), np.float32), np.zeros((P, T), np.float32), np.zeros((P, P), np.float32)
    for base in (0, 64):
        for f in range(8):
            fcos[base + f] = fcos[base + 8 + f] = cos[:, f]
            fsin[base + f], fsin[base + 8 + f] = -sin[:, f], sin[:, f]
            perm[base + 8 + f, base + f] = perm[base + f, base + 8 + f] = 1.0
    rope_t = np.stack([x.reshape(TT, P, 8).transpose(1, 0, 2) for x in (cos, sin)], axis=1).reshape(P, 64)
    return {
        "c_ident": np.eye(P, dtype=np.float32), "c_mask": causal, "c_sel": sel, "c_levels": levels.reshape(P, 8 * P),
        "c_stick": stick, "c_cos": fcos, "c_sin": fsin, "c_perm": perm, "c_rope_t": np.ascontiguousarray(rope_t),
    }


INPUTS = ["x", "p", "norm_pre", "norm_post", "att_w_in", "att_b_f", "att_w_out", "rec_w_in", "rec_lb", "rec_out_norm",
          "rec_w_out", "ple_w_proj", "ple_w_gate", "c_2", "w_ada_2", "b_ada_2", "g_pre_mix_2", "w_in_2", "w_up_a_2",
          "w_up_b_2", "w_out_2", "g_post_mix_2", "g_pre_ffn_2", "w_ff1_2", "w_ff2_2", "g_post_ffn_2"]


def kernel(**inputs):
    import concourse.bacc as bacc
    from concourse.bass_utils import run_bass_kernel_spmd

    nc = bacc.Bacc("TRN2", target_bir_lowering=False, num_devices=1)
    arrays = {name: np.ascontiguousarray(inputs[name]) for name in INPUTS}
    arrays.update(constants())
    aps = {name: nc.dram_tensor(name + "_dram", x.shape, mybir.dt.from_np(x.dtype), kind="ExternalInput").ap()
           for name, x in arrays.items()}
    aps["out"] = nc.dram_tensor("out_dram", (1, T, D), F32, kind="ExternalOutput").ap()
    build(nc, aps)
    r = run_bass_kernel_spmd(nc, [{name + "_dram": x for name, x in arrays.items()}], core_ids=[0])
    return r.results[0]["out_dram"]
```

```python
from contextlib import ExitStack

import numpy as np

import concourse.bass as bass
from concourse import mybir

P = 128
T = 512
TT = T // P
D = 1024
KT = D // P
G = 512
HD = 64
NEG = -3.0e38
EPS = 1e-6
TOPK = min(256, T // 4)
ISCALE = (64 ** -0.5) * (8 ** -0.5)
STK_UNIT = [(0, 0), (1, 0), (2, 0), (2, 256)]
STK_COLS = [512, 384, 384]
GATE_A = [0, 1, 4, 5, 2, 3, 6, 7]
GATE_B = [0, 4, 1, 5, 2, 6, 3, 7]
TREE = {4: 0, 8: 128, 16: 192, 32: 224, 64: 240, 128: 248}
KOFF = [0, 128, 384, 768]
F32 = mybir.dt.float32
F32R = mybir.dt.float32r
I32 = mybir.dt.int32
ALU = mybir.AluOpType
ACT = mybir.ActivationFunctionType
AX = mybir.AxisListType

STAGES = [
    ("norm0", 8, 0, 8, 8), ("qkv0", 24, 12, 0, 0), ("g0", 0, 8, 0, 0), ("at0", 8, 0, 8, 8),
    ("outa0", 4, 2, 0, 0), ("pt0", 2, 0, 2, 2), ("outb0", 4, 2, 0, 0), ("pj0", 8, 2, 0, 0), ("ht0", 8, 0, 8, 8),
    ("pg0", 8, 4, 8, 0),
    ("norm1", 8, 0, 8, 8), ("qfi1", 24, 12, 8, 0), ("g1", 0, 8, 0, 0), ("at1", 8, 0, 8, 8),
    ("outa1", 4, 2, 0, 0), ("pt1", 2, 0, 2, 2), ("outb1", 4, 2, 0, 0), ("pj1", 8, 2, 0, 0), ("ht1", 8, 0, 8, 8),
    ("pg1", 8, 4, 8, 0),
    ("norm2", 8, 0, 8, 8), ("qi2", 8, 2, 4, 0), ("qka2", 16, 4, 8, 0), ("va2", 4, 2, 0, 0),
    ("b2", 12, 6, 0, 0), ("ga2", 0, 4, 0, 0), ("at2", 4, 0, 4, 4), ("gb2", 0, 8, 0, 0), ("merge2", 16, 4, 16, 8), ("out2", 8, 4, 0, 0), ("ga2_0", 2, 0, 0, 0),
    ("norm3", 8, 0, 8, 8), ("ffn", 96, 32, 96, 32), ("ga2_1", 2, 0, 0, 0),
]
BASE, _at = {}, [0, 0, 0, 0]
for _name, *_use in STAGES:
    BASE[_name] = tuple(_at)
    _at = [a + b for a, b in zip(_at, _use)]
CHUNKS = _at[1]


class Chain:

    def __init__(self, eng, sem):
        self.eng, self.sem, self.n, self.turn = eng, sem, 0, None

    def mark(self, ins):
        self.n += 1
        ins.then_inc(self.sem, 1)

    def wait(self):
        self.eng.wait_ge(self.sem, self.n if self.turn is None else self.turn + self.n)

    def after(self, ins):
        self.mark(ins)
        self.wait()

    def enter(self, i, per):
        self.start, self.per, self.turn = self.n, per, i * per

    def leave(self, turns):
        assert self.n == self.start + self.per, (self.n - self.start, self.per)
        self.n, self.turn = self.start + self.per * turns, None


def build(nc, a):
    ctx = ExitStack()
    with ctx:
        def sb(name, shape, dt=F32):
            return ctx.enter_context(nc.sbuf_tensor(name, shape, dt))

        def sem(name):
            return ctx.enter_context(nc.semaphore(name))

        h = sb("h", [P, TT, D])
        slot = {x: sb(f"slot_{x}", [P, 4096]) for x in "ABC"}
        d_at = nc.sbuf_base
        slot["D"] = sb("slot_D", [P, 4096])
        feat = {x: slot[x][:, :].rearrange("p (k t) -> p k t", k=KT) for x in "ABCD"}
        tok = {x: slot[x][:, :].rearrange("p (t d) -> p t d", t=TT) for x in "ABCD"}
        xh, xl = sb("xh", [P, KT, T], F32R), sb("xl", [P, KT, T], F32R)
        y_at = nc.sbuf_base
        yh = sb("yh", [P, KT, T], F32R)
        yl_at = nc.sbuf_base
        yl = sb("yl", [P, KT, T], F32R)
        wk = nc.alloc_sbuf_tensor_at("work_hi", [P, KT, T], F32, offset=y_at)
        wl = nc.alloc_sbuf_tensor_at("work_lo", [P, KT, T], F32, offset=yl_at)
        raw = [sb(f"w_raw{s}", [P, 4, G]) for s in range(2)]
        wh = [sb(f"w_hi{s}", [P, 4, G], F32R) for s in range(2)]
        wlo = [sb(f"w_lo{s}", [P, 4, G], F32R) for s in range(2)]
        ev = sb("ev", [P, 4, T])
        grow = sb("gain_row", [P, D])
        mask = sb("causal_mask", [P, T])
        ident = sb("ident", [P, P])
        gcol = sb("gain_cols", [P, 4, KT])
        modc = sb("mod_cols", [P, 48])
        ocol = sb("out_norm_col", [P, 1])
        lbc = sb("lb_cols", [P, 6, KT])
        stat = sb("stat", [P, 64])
        stat2 = sb("stat2", [P, 32])
        bfc = sb("b_f_col", [P, 1])
        sel = sb("head_select", [P, 16])
        m8 = sb("max8", [P, 8])
        zero, one = sb("zero", [P, 1]), sb("one", [P, 1])

        perm = slot["D"][:, 3072:3200]
        rope = [slot["D"][:, 2048:2560], slot["D"][:, 2560:3072]]
        rope_t = slot["D"][:, 3200:3264].rearrange("p (a t f) -> p a t f", a=2, t=TT)
        wsm = slot["D"][:, 0:576].rearrange("p (k n) -> p k n", k=KT)
        wsm_h = nc.alloc_sbuf_tensor_at("w_small_hi", [P, KT, 72], F32R, offset=d_at + 4 * 576)
        wsm_l = nc.alloc_sbuf_tensor_at("w_small_lo", [P, KT, 72], F32R, offset=d_at + 4 * 1152)
        ada_w = [wk[:, 0:4, :], wk[:, 4:8, :], wl[:, 0:4, :]]
        ada_acc = [wl[:, j, :] for j in range(4, 8)] + [ev[:, j, :] for j in range(4)] + [feat["D"][:, j, :] for j in range(4, 8)]
        tok_p = slot["C"][:, 0:1024].rearrange("p (t d) -> p t d", t=TT)
        tri, ones, strict, strict_neg = (grow[:, j * P:j * P + P] for j in range(4))
        stk_sp = [[feat["A"][:, 3 * e + u, :] for u in range(3)] for e in range(2)]
        stk_at = [[feat["A"][:, 6, :], feat["A"][:, 7, :], slot["C"][:, 0:G]],
                  [slot["C"][:, j * D:j * D + G] for j in (1, 2, 3)]]
        isc = slot["A"][:, 2048:3328]
        level = ev[:, 0:2, :].rearrange("p a (l s) -> p (a l) s", l=4).bitcast(I32)

        r_q, r_k, r_sc, r_in = ([wk[:, 2 * j + e, :] for e in range(2)] for j in range(4))
        r_tree = wl[:, 0:4, :].rearrange("p a (b c) -> p (a b) c", b=2)
        r_f2 = [ev[:, 3, 0:256], ev[:, 3, 256:512]]
        r_kt = [wl[:, 4 + e, 0:384] for e in range(2)]
        r_st = [[wl[:, 4 + e, 384:512]] + [wl[:, 6, (2 * e + j) * P:(2 * e + j + 1) * P] for j in range(2)] for e in range(2)]
        r_junk = wl[:, 7, 0:2 * P]

        bias_q = [nc.alloc_sbuf_tensor_at(f"bias_q{j}", [P, T], F32R, offset=d_at + 2048 * j) for j in range(4)]
        bias_k = nc.alloc_sbuf_tensor_at("bias_k", [P, T], F32R, offset=d_at + 2048 * 4)
        a_q, a_k = [wk[:, j, :] for j in (0, 1)], [wk[:, j, :] for j in (2, 3)]
        a_v = [wk[:, j, :].rearrange("p (t d) -> p t d", t=TT) for j in (4, 5)]
        a_s, a_p = [wl[:, j, :] for j in (0, 1, 2)], [wl[:, j, :] for j in (3, 4, 5)]
        nmax, esum, rsum = stat[:, 16:24], stat[:, 48:56], stat[:, 56:64]
        SB, TB, OB = (0, 1, 5), (2, 3), (4, 6)

        ps = ctx.enter_context(nc.psum_tensor("banks", [P, 8, 512], F32))

        w_landed = [sem(f"w_landed{s}") for s in range(2)]
        w_split, w_ready, w_free = sem("w_split"), sem("w_ready"), sem("w_free")
        bank_full, bank_free = sem("bank_full"), sem("bank_free")
        ev_free, hi_done = sem("ev_free"), sem("hi_done")
        const_in, late_in = sem("const_in"), sem("late_in")
        dve_self, act_self = sem("dve_self"), sem("act_self")
        stored = sem("stored")
        apart = sem("apart")
        S = {}

        def sg(name):
            if name not in S:
                S[name] = sem(name)
            return S[name]

        def cols(w, c0, n=G, k0=0, kn=4):
            return w[k0 * P:(k0 + kn) * P, c0:c0 + n].rearrange("(k p) n -> p k n", p=P)

        win0, wout0 = a["att_w_in"][0], a["att_w_out"][0]
        win1, wout1 = a["rec_w_in"][0], a["rec_w_out"][0]
        win2, wout2 = a["w_in_2"][0], a["w_out_2"][0]
        wada = a["w_ada_2"][0]
        wff1, wff2 = a["w_ff1_2"][0], a["w_ff2_2"][0]

        ctx.enter_context(nc.allow_non_contiguous_dma(reason="small columns of gains"))
        block = ctx.enter_context(nc.Block())

        CONSTS = 15

        @block.sync
        def _(sp):
            for dst, src in (
                (ident[:, :], a["c_ident"]), (mask[:, :], a["c_mask"]), (sel[:, :], a["c_sel"]),
                (gcol[:, 0, :], a["norm_pre"][0].rearrange("(k p) -> p k", p=P)),
                (gcol[:, 1, :], a["norm_pre"][1].rearrange("(k p) -> p k", p=P)),
                (gcol[:, 2, :], a["g_pre_mix_2"][0].rearrange("(k p) -> p k", p=P)),
                (gcol[:, 3, :], a["g_pre_ffn_2"][0].rearrange("(k p) -> p k", p=P)),
                (modc[:, :], a["b_ada_2"][0].rearrange("(k p) -> p k", p=P)),
                (ocol[:, :], a["rec_out_norm"][0].rearrange("(p a) -> p a", a=1)),
                (lbc[:, 0:2, :], a["rec_lb"].rearrange("l (k p) -> p l k", p=P)),
                (stat[:, 32:40], a["c_2"][0].rearrange("(k p) -> p k", p=P)),
                (bfc[0:16, :], a["att_b_f"][0].rearrange("(p a) -> p a", a=1)),
                (bfc[32:48, :], a["att_b_f"][0].rearrange("(p a) -> p a", a=1)),
                (bfc[64:80, :], a["att_b_f"][0].rearrange("(p a) -> p a", a=1)),
                (bfc[96:112, :], a["att_b_f"][0].rearrange("(p a) -> p a", a=1)),
            ):
                sp.dma_start(dst, src).then_inc(const_in, 16)
            sp.dma_start(h[:, :, :], a["x"][0].rearrange("(t p) d -> p t d", p=P)).then_inc(sg("x_in"), 16)

            count = [0]

            def load(src, kn=4, n=G):
                c = count[0]
                sp.wait_ge(w_ready, c + 1)
                sp.dma_start(raw[c % 2][:, 0:kn, 0:n], src).then_inc(w_landed[c % 2], 16)
                count[0] += 1

            for c in range(24):
                if c >= 3:
                    sp.wait_ge(sg("ada_used"), c - 2)
                sp.dma_start(ada_w[c % 3], cols(wada, c // 2 * G, k0=4 * (c % 2))).then_inc(sg(f"ada_landed{c % 3}"), 16)
                if c % 2 and count[0] < 12:
                    half = count[0] % 2
                    load(cols(win0, count[0] // 2 * G, k0=4 * half))

            def load_groups(w, n, c0=0):
                if n < 4:
                    for g in range(n):
                        load(cols(w, c0 + g * G))
                        load(cols(w, c0 + g * G, k0=4))
                    return
                first = count[0]
                with sp.Fori(0, n) as g:
                    for half in range(2):
                        sp.wait_ge(w_ready, 2 * g + (first + half + 1))
                        src = w[half * 4 * P:(half + 1) * 4 * P, bass.ds(g * G + c0, G)]
                        sp.dma_start(raw[half][:, :, :], src.rearrange("(k p) n -> p k n", p=P))\
                          .then_inc(w_landed[half], 16)
                count[0] += 2 * n

            def load_beside(w, c0):
                for t in range(4):
                    for half in range(2):
                        load(cols(w, c0 + t * 256, 256, k0=4 * half), n=256)

            def load_ple(l):
                for n in range(2):
                    load(cols(a["ple_w_proj"][l], n * G, kn=2), kn=2)
                load_groups(a["ple_w_gate"][l], 2)

            load_beside(win0, 3 * D)
            load_groups(wout0, 2)
            load_ple(0)
            load_groups(win1, 6)
            load_beside(win1, 3 * D)
            load_groups(wout1, 2)
            load_ple(1)
            load_groups(win2, 1, 6 * G)
            load_groups(win2, 3)
            load_groups(win2, 3, 3 * G)
            load_groups(win2, 2, 3656)
            load_beside(win2, 4680)
            for n in range(2):
                load(cols(a["w_up_a_2"][0], n * G))
                load(cols(a["w_up_b_2"][0], n * G))
            load_groups(wout2, 2)
            for i in range(9):
                if i < 8:
                    load(cols(wff1, i * G))
                    load(cols(wff1, i * G, k0=4))
                if i > 0:
                    load(cols(wff2, 0, k0=4 * (i - 1)))
                    load(cols(wff2, G, k0=4 * (i - 1)))
            assert count[0] == CHUNKS, (count[0], CHUNKS)
            sp.wait_ge(sg("final"), TT)
            sp.dma_start(a["out"][0].rearrange("(t p) d -> p t d", p=P), h[:, :, :]).then_inc(stored, 16)
            sp.wait_ge(stored, 16)

        @block.gpsimd
        def _(pool):
            pool.sem_inc(w_ready, 2)
            pool.memset(zero[:, :], 0.0).then_inc(w_split, 1)
            pool.wait_ge(w_split, 1)
            nothing = zero[:, :].unsqueeze(2).broadcast_to([P, 4, G])
            with pool.Fori(0, CHUNKS // 2) as i:
                for s in range(2):
                    pool.wait_ge(w_landed[s], 16 * i + 16)
                    pool.wait_ge(w_free, 2 * i + (s + 1))
                    pool.tensor_tensor(wh[s][:, :, :], raw[s][:, :, :], nothing, ALU.add).then_inc(w_split, 1)
                    pool.wait_ge(w_split, 2 * i + (s + 2))
                    pool.tensor_tensor(wlo[s][:, :, :], raw[s][:, :, :], wh[s][:, :, :].bitcast(F32), ALU.subtract)\
                        .then_inc(w_ready, 1)

        @block.tensor
        def _(pe):
            pe.sem_inc(w_free, 2)

            def bank(n):
                return ps[:, n % 8, :]

            def three(out, s, k, act_h, act_l, ak, m, feature_major, start, stop):
                cut = slice(m * P, m * P + P)
                if feature_major:
                    w_h, w_l, x_h, x_l = wh[s][:, k, cut], wlo[s][:, k, cut], act_h[:, ak, :], act_l[:, ak, :]
                    pe.matmul(out, w_h, x_h, start=start, stop=False)
                    pe.matmul(out, w_h, x_l, start=False, stop=False)
                    return pe.matmul(out, w_l, x_h, start=False, stop=stop)
                w_h, w_l, x_h, x_l = wh[s][:, k, :], wlo[s][:, k, :], act_h[:, ak, cut], act_l[:, ak, cut]
                pe.matmul(out, x_h, w_h, start=start, stop=False)
                pe.matmul(out, x_h, w_l, start=False, stop=False)
                return pe.matmul(out, x_l, w_h, start=False, stop=stop)

            def group(n, c, feature_major, act_h=xh, act_l=xl, a0=0, chunks=2, kn=4, static=0, ready=None):
                n8, c2 = static
                for ch in range(chunks):
                    pe.wait_ge(w_ready, c + (ch + 3))
                    for m in range(4):
                        if ch == 0:
                            pe.wait_ge(bank_free, n + (m + 1))
                        for k in range(kn):
                            if ready and m == 0:
                                pe.wait_ge(ready[0], ready[1] + 4 * ch + k + 1)
                            mm = three(ps[:, (n8 + m) % 8, :], (c2 + ch) % 2, k, act_h, act_l, a0 + 4 * ch + k, m,
                                       feature_major, ch == 0 and k == 0, ch == chunks - 1 and k == kn - 1)
                        if ch == chunks - 1:
                            mm.then_inc(bank_full, 1)
                            if m == 3:
                                pe.drain().then_inc(w_free, 1)
                        elif m == 3:
                            mm.then_inc(w_free, 1)

            def groups(name, count, kinds, skip=0, **kw):
                n0, c0 = BASE[name][0] + 4 * skip, BASE[name][1] + 2 * skip
                static = (n0 % 8, c0 % 2)
                if count >= 4:
                    with pe.Fori(0, count // 2) as i:
                        for half in range(2):
                            group(8 * i + (n0 + 4 * half), 4 * i + (c0 + 2 * half), kinds,
                                  static=((n0 + 4 * half) % 8, c0 % 2), **kw)
                else:
                    for g in range(count):
                        group(n0 + 4 * g, c0 + 2 * g, kinds, static=((n0 + 4 * g) % 8, c0 % 2), **kw)

            def transposes(name, src, ready, tiles=KT, skip=0):
                n0 = BASE[name][0]
                pe.wait_ge(*ready)
                for k in range(tiles):
                    n = n0 + k
                    pe.wait_ge(bank_free, n + 1)
                    for t in range(TT):
                        tr = pe.transpose(bank(n)[:, t * P:t * P + P], src[:, t, k * P:k * P + P], ident[:, :])
                    tr.then_inc(bank_full, 1)

            def split_of(name):
                return ev_free, BASE[name][2] + 4

            def beside(x, i, unit, tiles=2):
                (m, k), c0 = divmod(unit, 8), BASE[x][1]
                if k == 0:
                    pe.wait_ge(sg(x + "_free"), tiles * i + (m + 1))
                if m == 0 and k % 4 == 0:
                    pe.wait_ge(w_ready, 2 * i + (c0 + k // 4 + 3))
                mm = three(ps[:, 7, :], k // 4, k % 4, xh, xl, k, m, True, k == 0, k == 7)
                if k == 7:
                    mm.then_inc(sg(x + "_full"), 1)
                    if m == tiles - 1:
                        pe.drain().then_inc(w_free, 1)
                elif m == tiles - 1 and k == 3:
                    mm.then_inc(w_free, 1)

            def all_banks_free(name):
                pe.wait_ge(bank_free, BASE[name][0] + 8)

            def attention(x, pairs, bias, side, tiles):
                with pe.Fori(0, pairs // 2) as i:
                    for t in range(19):
                        if t < 16:
                            b, p, r, q = t, t // 8, t // 4 % 2, t % 4
                            hs, kw = slice(HD * r, HD * r + HD), (q + 1) * P
                            if b % 8 == 0:
                                pe.wait_ge(sg(x + "_staged"), 2 * i + (p + 1))
                            if b >= 3:
                                pe.wait_ge(sg(x + "_max"), 16 * i + (b - 2))
                            mm = pe.matmul(ps[:, SB[b % 3], 0:kw], a_q[p][hs, q * P:q * P + P], a_k[p][hs, 0:kw],
                                           start=True, stop=not bias)
                            if bias:
                                mm = pe.matmul(ps[:, SB[b % 3], 0:kw], bias_q[2 * p + r][:, q * P:q * P + P],
                                               bias_k[:, 0:kw], start=False, stop=True)
                            mm.then_inc(sg(x + "_scores"), 1)
                        if tiles == 2 and t < 17 and t != 8:
                            beside(side, i, t - (t > 8))
                        if tiles == 4 and t < 16:
                            beside(side, i, 2 * t, 4)
                            beside(side, i, 2 * t + 1, 4)
                        if 2 <= t < 18:
                            b = t - 2
                            pe.wait_ge(sg(x + "_exp"), 16 * i + (b + 1))
                            if b >= 2:
                                pe.wait_ge(sg(x + "_evac"), 16 * i + (b - 1))
                            for j in range(b % 4 + 1):
                                mm = pe.transpose(ps[:, TB[b % 2], j * P:j * P + P], a_s[b % 3][:, j * P:j * P + P],
                                                  ident[:, :])
                            mm.then_inc(sg(x + "_turned"), 1)
                        if t >= 3:
                            b = t - 3
                            p, r, q = b // 8, b // 4 % 2, b % 4
                            pe.wait_ge(sg(x + "_evac"), 16 * i + (b + 1))
                            if b >= 2:
                                pe.wait_ge(sg(x + "_out"), 16 * i + (b - 1))
                            for j in range(q + 1):
                                mm = pe.matmul(ps[:, OB[b % 2], 0:HD], a_p[b % 3][:, j * P:j * P + P],
                                               a_v[p][:, j, HD * r:HD * r + HD], start=j == 0, stop=j == q)
                            mm.then_inc(sg(x + "_summed"), 1)
                pe.wait_ge(sg(x + "_out"), 8 * pairs)
                pe.wait_ge(sg(side + "_free"), tiles * pairs // 2 + 1)

            pe.wait_ge(const_in, 16 * CONSTS)
            transposes("norm0", tok["D"], (sg("norm0_xn"), TT))
            groups("qkv0", 4, True, ready=split_of("norm0"))
            groups("qkv0", 2, False, skip=4)
            all_banks_free("at0")
            pe.wait_ge(sg("ada_acc"), 12)
            for n in range(12):
                for c in range(4):
                    mm = pe.matmul(ps[:, 7, 4 * n + c:4 * n + c + 1], ada_acc[n][:, c * P:c * P + P],
                                   one[:, :], start=True, stop=True)
            mm.then_inc(sg("ada_sum"), 1)
            pe.wait_ge(sg("fl_split"), 1)
            for t in range(TT):
                for k in range(KT):
                    cut = slice(t * P, t * P + P)
                    pe.matmul(ps[:, 0, 16 * t:16 * t + 16], xh[:, k, cut], wsm_h[:, k, 0:16], start=k == 0, stop=False)
                    pe.matmul(ps[:, 0, 16 * t:16 * t + 16], xh[:, k, cut], wsm_l[:, k, 0:16], start=False, stop=False)
                    mm = pe.matmul(ps[:, 0, 16 * t:16 * t + 16], xl[:, k, cut], wsm_h[:, k, 0:16], start=False, stop=k == KT - 1)
            mm.then_inc(sg("fl_full"), 1)
            pe.wait_ge(sg("fl_rows"), 1)
            for t in range(TT):
                mm = pe.transpose(ps[:, 1, t * P:t * P + P], ev[:, 0, t * P:t * P + P], ident[:, :])
            mm.then_inc(sg("fl_turned"), 1)
            attention("fox", 8, True, "g0", 2)
            transposes("at0", tok["C"], (sg("fox_out"), 64))

            def out_and_ple(l):
                groups(f"outa{l}", 1, False, act_h=yh, act_l=yl, ready=split_of(f"at{l}"))
                transposes(f"pt{l}", tok_p, (sg(f"p_in{l}"), 16), tiles=2)
                groups(f"outb{l}", 1, False, act_h=yh, act_l=yl)
                n0, c0, _, _ = BASE[f"pj{l}"]
                pe.wait_ge(ev_free, BASE[f"pt{l}"][2] + 6)
                for n in range(2):
                    group(n0 + 4 * n, c0 + n, False, a0=6, chunks=1, kn=2, static=((n0 + 4 * n) % 8, (c0 + n) % 2))
                transposes(f"ht{l}", h, (sg(f"post{l}"), TT))
                groups(f"pg{l}", 2, False, ready=split_of(f"ht{l}"))

            out_and_ple(0)

            transposes("norm1", tok["D"], (sg("norm1_xn"), TT))
            groups("qfi1", 4, True, ready=split_of("norm1"))
            groups("qfi1", 2, False, skip=4)
            all_banks_free("at1")
            pe.sem_inc(sg("rec_full"), 2)
            with pe.Fori(0, 4) as i:
                for s in range(8):
                    for e in range(2):
                        if s == 0:
                            pe.wait_ge(sg("rec_staged"), 2 * i + (e + 1))
                        else:
                            pe.wait_ge(sg("lev_qk"), 14 * i + (2 * s + e - 1))
                        pe.wait_ge(sg("lev_kept"), 16 * i + (2 * s + e + 1))
                        for j in range(TT):
                            cut = slice(j * P, j * P + P)
                            mm = pe.matmul(ps[:, e, cut], r_k[e][:, cut], r_q[e][:, cut], start=True, stop=True)
                        mm.then_inc(sg("lev_used"), 1)
                        u = 2 * s + e
                        for unit in [u] if u < 8 else [] if u == 8 else [u - 1] if u < 15 else [14, 15]:
                            beside("g1", i, unit)
                for e in range(2):
                    pe.wait_ge(sg("kd_ready"), 2 * i + (e + 1))
                    for j in range(TT - 1):
                        mm = pe.transpose(ps[:, 3 + e, j * P:j * P + P], r_k[e][:, j * P:j * P + P], ident[:, :])
                    mm.then_inc(sg("kd_turned"), 1)
                for e in range(2):
                    pe.wait_ge(sg("kd_copied"), 2 * i + (e + 1))
                    for j in range(TT - 1):
                        cut = slice(j * P, j * P + P)
                        mm = pe.matmul(ps[:, 5 + e, cut], r_kt[e][:, cut], r_in[e][:, cut], start=True, stop=True)
                    mm.then_inc(sg("state_add"), 1)
                for e in range(2):
                    pe.wait_ge(sg("lev_kept"), 16 * i + (e + 17))
                    for j in range(TT):
                        cut = slice(j * P, j * P + P)
                        mm = pe.matmul(ps[:, 3 + e, cut], r_sc[e][:, cut], r_in[e][:, cut], start=True, stop=j == 0)
                        if j > 0:
                            pe.wait_ge(sg("state"), 6 * i + (3 * e + j))
                            mm = pe.matmul(ps[:, 3 + e, cut], r_q[e][:, cut], r_st[e][j - 1], start=False, stop=True)
                    mm.then_inc(sg("rec_full"), 1)
            pe.wait_ge(sg("g1_free"), 9)
            transposes("at1", tok["D"], (sg("o_normed"), 1))
            out_and_ple(1)

            transposes("norm2", tok["D"], (sg("norm2_xn"), TT))

            def rope_group(n, c, u, static, **kw):
                group(n, c, True, static=static, **kw)
                for m in range(4):
                    pe.wait_ge(bank_free, n + (m + 9))
                    pe.matmul(ps[:, (static[0] + 4 + m) % 8, :], perm[:, :], ev[:, m, :], start=True, stop=True)\
                        .then_inc(bank_full, 1)

            n0, c0, u0, _ = BASE["qi2"]
            pe.wait_ge(sg("rope_in"), 64)
            rope_group(n0, c0, u0, (n0 % 8, c0 % 2), ready=split_of("norm2"))
            n0, c0, u0, _ = BASE["qka2"]
            for g in range(2):
                rope_group(n0 + 8 * g, c0 + 2 * g, u0 + 4 * g, (n0 % 8, c0 % 2))
            n0, c0, _, _ = BASE["va2"]
            group(n0, c0, False, static=(n0 % 8, c0 % 2))
            all_banks_free("b2")
            pe.wait_ge(sg("ki_split"), 1)
            for t in range(TT):
                for k in range(KT):
                    cut = slice(t * P, t * P + P)
                    o = ps[:, 0, 72 * t:72 * t + 72]
                    pe.matmul(o, xh[:, k, cut], wsm_h[:, k, :], start=k == 0, stop=False)
                    pe.matmul(o, xh[:, k, cut], wsm_l[:, k, :], start=False, stop=False)
                    mm = pe.matmul(o, xl[:, k, cut], wsm_h[:, k, :], start=False, stop=k == KT - 1)
            mm.then_inc(sg("ki_full"), 1)
            pe.wait_ge(sg("ki_rows"), 1)
            for t in range(TT):
                mm = pe.transpose(ps[:, 1, t * P:t * P + P], ev[:, 1, t * P:t * P + P], ident[:, :])
            mm.then_inc(sg("ki_turned"), 1)
            pe.wait_ge(sg("ki_ready"), 1)
            for q in range(TT):
                kw = (q + 1) * P
                for hh in range(8):
                    b = 8 * q + hh
                    hs = slice(HD * (hh % 2), HD * (hh % 2) + HD)
                    if b >= 2:
                        pe.wait_ge(sg("idx_relu"), b - 1)
                    pe.matmul(ps[:, 2 + b % 2, 0:kw], feat["A"][hs, hh // 2, q * P:q * P + P], ev[hs, 2, 0:kw],
                              start=True, stop=True).then_inc(sg("idx_full"), 1)
            pe.wait_ge(sg("idx_relu"), 32)
            n0, c0, _, _ = BASE["b2"]
            for g in range(3):
                group(n0 + 4 * g, c0 + 2 * g, g < 2, static=((n0 + 4 * g) % 8, c0 % 2))
            all_banks_free("at2")
            attention("top", 4, False, "ga2", 4)
            transposes("at2", tok["C"], (sg("top_out"), 32), tiles=4)
            all_banks_free("merge2")

            qs, ks, vs = ev[:, 0, :], ev[:, 1, :], ev[:, 2, :].rearrange("p (t d) -> p t d", t=TT)

            def unit_bank(e, j, t0):
                u, o = STK_UNIT[j]
                return ps[:, 3 * e + u, o + (t0 - j) * P:o + (TT - j) * P]

            pe.wait_ge(sg("tri_in"), 16)
            with pe.Fori(0, 4) as i:
                for unit in range(4):
                    beside("gb2", i, unit)
                pe.wait_ge(sg("stk_staged"), i + 1)
                for e in range(2):
                    hs = slice(HD * e, HD * e + HD)
                    for j in reversed(range(TT)):
                        mm = pe.matmul(unit_bank(e, j, j), ks[hs, j * P:j * P + P], qs[hs, j * P:T],
                                       start=True, stop=True)
                        if j < 3:
                            mm.then_inc(sg("stk_z"), 1)
                for unit in range(4, 11):
                    beside("gb2", i, unit)
                for e in range(2):
                    hs = slice(HD * e, HD * e + HD)
                    for j in reversed(range(TT)):
                        pe.wait_ge(sg("stk_sp"), 6 * i + (3 * e + 3 - STK_UNIT[j][0]))
                        pe.matmul(unit_bank(e, j, j), ks[hs, j * P:j * P + P], qs[hs, j * P:T], start=True, stop=False)
                        for j2 in range(j, TT):
                            u, o = STK_UNIT[j2]
                            mm = pe.matmul(unit_bank(e, j, j2), tri if j2 == j else ones,
                                           stk_sp[e][u][:, o:o + (TT - j2) * P], start=False, stop=j2 == TT - 1)
                        if j < 3:
                            mm.then_inc(sg("stk_r"), 1)
                for unit in range(11, 16):
                    beside("gb2", i, unit)
                for e in range(2):
                    hs = slice(HD * e, HD * e + HD)
                    pe.wait_ge(sg("stk_att"), 6 * i + (3 * e + 3))
                    for j in range(TT):
                        u, o = STK_UNIT[j]
                        mm = pe.matmul(ps[hs, 6, j * P:T], vs[:, j, hs], stk_at[e][u][:, o:o + (TT - j) * P],
                                       start=j == 0, stop=j == TT - 1)
                    mm.then_inc(sg("stk_o"), 1)
            pe.wait_ge(sg("stk_out"), 4)
            pe.wait_ge(sg("gb2_free"), 9)

            n0, c0, _, _ = BASE["merge2"]
            for g in range(4):
                group(n0 + 4 * g, c0 + g, True, act_h=yh, act_l=yl, a0=4 * (g % 2), chunks=1,
                      static=((n0 + 4 * g) % 8, (c0 + g) % 2))
            groups("out2", 2, False, ready=(sg("merged"), 0))

            def rows_of(name, col):
                n0 = BASE[name][0]
                for b in range(2):
                    pe.wait_ge(bank_free, n0 + b + 1)
                    for k in range(4):
                        c = modc[:, col + 4 * b + k:col + 4 * b + k + 1]
                        mm = pe.matmul(bank(n0 + b)[:, k * P:k * P + P], c.broadcast_to([P, P]), ident[:, :],
                                       start=True, stop=True)
                    mm.then_inc(bank_full, 1)

            rows_of("ga2_0", 16)
            transposes("norm3", tok["D"], (sg("norm3_xn"), TT))
            n0, c0, u0, _ = BASE["ffn"]

            def ff1(n, c, st):
                group(n, c, True, static=st, ready=split_of("norm3"))

            def ff2(n, c, u, st, half):
                pe.wait_ge(ev_free, u)
                for g in range(2):
                    group(n + 4 * g, c + g, False, act_h=yh, act_l=yl, a0=4 * half, chunks=1,
                          static=((st[0] + 4 * g) % 8, (st[1] + g) % 2))

            def at(dn, dc):
                return ((n0 + dn) % 8, (c0 + dc) % 2)

            ff1(n0, c0, at(0, 0))
            with pe.Fori(0, 3) as j:
                n, c, u = 24 * j + n0, 8 * j + c0, 24 * j + u0
                ff1(n + 4, c + 2, at(4, 2))
                ff2(n + 8, c + 4, u + 8, at(8, 4), 0)
                ff1(n + 16, c + 6, at(16, 6))
                ff2(n + 20, c + 8, u + 12 + 8, at(20, 8), 1)
            n, c, u = n0 + 72, c0 + 24, u0 + 72
            ff1(n + 4, c + 2, at(4, 2))
            ff2(n + 8, c + 4, u + 8, at(8, 4), 0)
            ff2(n + 16, c + 6, u + 12, at(16, 6), 1)
            rows_of("ga2_1", 40)

        @block.scalar
        def _(act):
            A = Chain(act, act_self)
            act.sem_inc(bank_free, 8)

            def empty(n, dst, func=ACT.Copy, **kw):
                act.wait_ge(bank_full, n + 1)
                act.activation(dst, ps[:, n % 8, :], func, **kw).then_inc(bank_free, 1)

            def empty_to_ev(n, u, func=ACT.Copy, **kw):
                act.wait_ge(ev_free, u + 1)
                empty(n, ev[:, u % 4, :], func, **kw)

            def square(name, t, src, junk, sem_, value):
                act.wait_ge(sem_, value)
                act.activation(junk[:, t, :], src[:, t, :], ACT.Square, accum_out=stat[:, t:t + 1])\
                   .then_inc(sg(name + "_ss"), 1)

            def root(name):
                act.wait_ge(sg(name + "_var"), 1)
                act.activation(stat[:, 8:12], stat[:, 4:8], ACT.Sqrt).then_inc(sg(name + "_sd"), 1)

            def turned_with_gain(name, gains, bias=None, tiles=KT):
                n0, _, u0, _ = BASE[name]
                for k in range(tiles):
                    if gains is None:
                        empty_to_ev(n0 + k, u0 + k)
                    else:
                        empty_to_ev(n0 + k, u0 + k, ACT.Identity, scale=gains[:, k:k + 1],
                                    bias=0.0 if bias is None else bias[:, k:k + 1])

            def empty_all(name, count, dst, skip=0, **kw):
                for m in range(count):
                    empty(BASE[name][0] + skip + m, dst(m), **kw)

            def gated(name, **gain):
                n0, _, u0, _ = BASE[name]
                for m in range(8):
                    act.activation(feat["A"][:, m, :], feat["A"][:, m, :], ACT.Silu).then_inc(sg(name + "_silu"), 1)
                    empty_to_ev(n0 + m, u0 + m, **gain)

            def token_dst(x, g=0):
                return lambda m: tok[x][:, m % 4, (m // 4 + g) * G:(m // 4 + g) * G + G]

            def emptied_with_squares(l, n0):
                for t in range(TT):
                    empty(n0 + t, token_dst("B", 1)(t))
                    square(f"post{l}", t, tok["B"], tok["D"], bank_free, n0 + t + 9)

            def out_and_ple(l):
                act.dma_start(tok_p, a["p"][l, 0].rearrange("(t p) d -> p t d", p=P)).then_inc(sg(f"p_in{l}"), 16)
                act.dma_start(grow[:, :], a["norm_post"][l].partition_broadcast(P)).then_inc(sg(f"grow{l}"), 16)
                empty_all(f"outa{l}", 4, token_dst("B"))
                turned_with_gain(f"pt{l}", None, tiles=2)
                emptied_with_squares(l, BASE[f"outb{l}"][0])
                root(f"post{l}")
                empty_all(f"pj{l}", 8, token_dst("A"))
                turned_with_gain(f"ht{l}", None)
                n0, _, u0, _ = BASE[f"pg{l}"]
                for m in range(8):
                    empty_to_ev(n0 + m, u0 + m, ACT.Sigmoid)
                    if m > 4:
                        square(f"norm{l + 1}", m - 5, h, tok["B"], sg(f"pg{l}_h"), m)
                square(f"norm{l + 1}", 3, h, tok["B"], sg(f"pg{l}_h"), 8)
                root(f"norm{l + 1}")

            def beside(x, i, m, tiles, dst):
                act.wait_ge(sg(x + "_full"), tiles * i + (m + 1))
                act.sem_inc(apart, 1)
                act.activation(dst, ps[:, 7, :], ACT.Copy).then_inc(sg(x + "_free"), 1)

            def attention(x, pairs, side, tiles, dst):
                with act.Fori(0, pairs // 2) as i:
                    for t in range(18):
                        if t in (8, 4, 12)[:tiles - 1]:
                            beside(side, i, t * tiles // 16 - 1, tiles, dst(i, t * tiles // 16 - 1))
                        if t < 16:
                            b = t
                            kw = (b % 4 + 1) * P
                            act.wait_ge(sg(x + "_max"), 16 * i + (b + 1))
                            act.activation(a_s[b % 3][:, 0:kw], a_s[b % 3][:, 0:kw], ACT.Exp, scale=-1.0,
                                           bias=nmax[:, b % 8:b % 8 + 1], accum_out=esum[:, b % 8:b % 8 + 1])\
                               .then_inc(sg(x + "_exp"), 1)
                        if t >= 2:
                            b = t - 2
                            kw = (b % 4 + 1) * P
                            act.wait_ge(sg(x + "_turned"), 16 * i + (b + 1))
                            if b >= 3:
                                act.wait_ge(sg(x + "_summed"), 16 * i + (b - 2))
                            act.activation(a_p[b % 3][:, 0:kw], ps[:, TB[b % 2], 0:kw], ACT.Copy)\
                               .then_inc(sg(x + "_evac"), 1)
                    beside(side, i, tiles - 1, tiles, dst(i, tiles - 1))

            act.wait_ge(const_in, 16 * CONSTS)
            act.activation(stat[:, 40:48], stat[:, 32:40], ACT.Silu).then_inc(sg("c_silu"), 1)

            act.wait_ge(sg("x_in"), 16)
            for t in range(TT):
                square("norm0", t, h, tok["B"], sg("x_in"), 16)
            root("norm0")
            turned_with_gain("norm0", gcol[:, 0, :])
            act.dma_start(wsm[:, :, 0:16], cols(win0, 4 * D, 16, kn=KT)).then_inc(sg("fl_in"), 16)
            empty_all("qkv0", 8, lambda m: feat["A"][:, m, :], scale=HD ** -0.5)
            empty_all("qkv0", 8, lambda m: feat["B"][:, m, :], skip=8)
            empty_all("qkv0", 8, token_dst("C"), skip=16)
            act.wait_ge(sg("fl_x"), 1)
            A.after(act.activation(feat["D"][:, 5, :], feat["D"][:, 7, :], ACT.Abs))
            act.activation(feat["D"][:, 5, :], feat["D"][:, 5, :], ACT.Exp, scale=-1.0).then_inc(act_self, 1)
            A.n += 1
            A.wait()
            act.activation(feat["D"][:, 5, :], feat["D"][:, 5, :], ACT.Ln, bias=1.0).then_inc(sg("fl_ln"), 1)
            act.sem_inc(sg("g0_free"), 1)
            attention("fox", 8, "g0", 2, lambda i, m: feat["A"][:, 2 * i + m, :])
            gated("at0")
            act.wait_ge(sg("lb_sub"), 1)
            act.activation(lbc[:, 3:5, :], lbc[:, 3:5, :], ACT.Exp).then_inc(sg("lb_exp"), 1)
            out_and_ple(0)

            turned_with_gain("norm1", gcol[:, 1, :])
            empty_all("qfi1", 8, lambda m: feat["A"][:, m, :])
            for m in range(8):
                empty_to_ev(BASE["qfi1"][0] + 8 + m, BASE["qfi1"][2] + m, ACT.Sigmoid)
            empty_all("qfi1", 8, token_dst("D"), skip=16)
            act.sem_inc(sg("g1_free"), 1)
            act.wait_ge(bank_free, BASE["at1"][0] + 8)
            act.wait_ge(sg("f_ready"), KT)
            act.dma_start(ev[:, 0:2, :], a["c_levels"].rearrange("p (a s) -> p a s", a=2)).then_inc(sg("level_in"), 16)
            with act.Fori(0, 4) as i:
                for e in range(2):
                    act.wait_ge(sg("rec_full"), 2 * i + (e + 1))
                    act.sem_inc(apart, 1)
                    act.activation(r_q[e], feat["A"][:, 2 * i + e, :], ACT.Copy)
                    act.activation(r_k[e], feat["C"][:, 2 * i + e, :], ACT.Copy)
                    act.activation(r_in[e].rearrange("p (t d) -> p t d", t=TT), tok["D"][:, :, bass.ds(i * 2 * P + e * P, P)],
                                   ACT.Copy).then_inc(sg("rec_staged"), 1)
                for m in range(2):
                    beside("g1", i, m, 2, feat["A"][:, 2 * i + m, :])
                for e in range(2):
                    act.wait_ge(sg("kd_turned"), 2 * i + (e + 1))
                    act.activation(r_kt[e], ps[:, 3 + e, 0:384], ACT.Copy).then_inc(sg("kd_copied"), 1)
                for e in range(2):
                    act.wait_ge(sg("rec_full"), 2 * i + (e + 3))
                    for j in range(TT):
                        act.sem_inc(apart, 1)
                        act.activation(r_junk[:, (4 * e + j) % 2 * P:(4 * e + j) % 2 * P + P], ps[:, 3 + e, j * P:j * P + P],
                                       ACT.Square, accum_out=stat2[:, bass.ds(i * 8 + 4 * e + j, 1)]).then_inc(sg("junk"), 1)
                        act.wait_ge(sg("junk"), 8 * i + (4 * e + j + 1))
                    act.sem_inc(apart, 1)
                    act.activation(tok["D"][:, :, bass.ds(i * 2 * P + e * P, P)],
                                   ps[:, 3 + e, :].rearrange("p (t d) -> p t d", t=TT), ACT.Copy).then_inc(sg("rec_out"), 1)
            act.wait_ge(sg("o_var"), 1)
            act.activation(stat2[:, 0:32], stat2[:, 0:32], ACT.Sqrt).then_inc(sg("o_sd"), 1)
            gated("at1", scale=ocol[:, 0:1])
            out_and_ple(1)

            act.wait_ge(sg("gains2"), 2)
            turned_with_gain("norm2", gcol[:, 2, :], modc[:, 0:8])
            act.dma_start(rope[0], a["c_cos"]).then_inc(sg("rope_in"), 16)
            act.dma_start(rope[1], a["c_sin"]).then_inc(sg("rope_in"), 16)
            act.dma_start(perm, a["c_perm"]).then_inc(sg("rope_in"), 16)
            act.dma_start(slot["D"][:, 3200:3264], a["c_rope_t"]).then_inc(sg("rope_in"), 16)
            act.dma_start(wsm, cols(win2, 7 * G, 72, kn=KT)).then_inc(sg("ki_in"), 16)

            def rope_group(n, u, dst, scale):
                for m in range(4):
                    empty_to_ev(n + m, u + m, scale=scale)
                for m in range(4):
                    empty(n + 4 + m, dst(m))

            n0, _, u0, _ = BASE["qi2"]
            rope_group(n0, u0, lambda m: feat["A"][:, m, :], 1.0)
            n0, _, u0, _ = BASE["qka2"]
            rope_group(n0, u0, lambda m: feat["B"][:, m, :], HD ** -0.5)
            rope_group(n0 + 8, u0 + 4, lambda m: feat["B"][:, 4 + m, :], 1.0)
            empty_all("va2", 4, token_dst("C"))
            rt = [ev[:, 3, :], ev[:, 0, :]]
            for q in range(TT):
                for hh in range(8):
                    b = 8 * q + hh
                    if b >= 2:
                        act.wait_ge(sg("idx_acc"), b - 1)
                    act.wait_ge(sg("idx_full"), b + 1)
                    act.activation(rt[b % 2][:, 0:(q + 1) * P], ps[:, 2 + b % 2, 0:(q + 1) * P], ACT.Relu)\
                       .then_inc(sg("idx_relu"), 1)
            empty_all("b2", 4, lambda m: feat["D"][:, m, :], scale=HD ** -0.5)
            empty_all("b2", 4, lambda m: feat["D"][:, 4 + m, :], skip=4)
            empty_all("b2", 4, lambda m: tok["C"][:, m, G:D], skip=8)
            act.dma_start(grow[:, 0:512], a["c_stick"]).then_inc(sg("tri_in"), 16)
            act.sem_inc(sg("ga2_free"), 1)
            attention("top", 4, "ga2", 4, lambda i, m: feat["B"][:, 2 * i + GATE_A[m], :])
            turned_with_gain("at2", None, tiles=4)
            for k in range(KT):
                act.activation(feat["B"][:, k, :], feat["B"][:, k, :], ACT.Sigmoid).then_inc(sg("gates"), 1)
            with act.Fori(0, 4) as i:
                for e in range(2):
                    for u in (2, 1, 0):
                        act.wait_ge(sg("stk_z"), 6 * i + (3 * e + 3 - u))
                        w = STK_COLS[u]
                        act.activation(stk_sp[e][u][:, 0:w], ps[:, 3 * e + u, 0:w], ACT.Abs).then_inc(sg("stk_abs"), 1)
                    for u in (2, 1, 0):
                        act.wait_ge(sg("stk_abs"), 6 * i + (3 * e + 3 - u))
                        x = stk_sp[e][u][:, 0:STK_COLS[u]]
                        act.activation(x, x, ACT.Exp, scale=-1.0).then_inc(sg("stk_exp"), 1)
                for e in range(2):
                    for u in (2, 1, 0):
                        act.wait_ge(sg("stk_exp"), 6 * i + (3 * e + 3 - u))
                        x = stk_sp[e][u][:, 0:STK_COLS[u]]
                        act.activation(x, x, ACT.Ln, bias=1.0).then_inc(sg("stk_ln"), 1)
                for e in range(2):
                    for u in (2, 1, 0):
                        act.wait_ge(sg("stk_arg"), 6 * i + (3 * e + 3 - u))
                        w = STK_COLS[u]
                        act.activation(stk_at[e][u][:, 0:w], ps[:, 3 * e + u, 0:w], ACT.Exp).then_inc(sg("stk_att"), 1)

            n0, _, u0, _ = BASE["merge2"]
            for g in range(4):
                for m in range(4):
                    if g % 2:
                        act.wait_ge(sg("gb2_free"), 9)
                        x = feat["D"][:, GATE_B[4 * (g // 2) + m], :]
                        act.activation(x, x, ACT.Sigmoid).then_inc(sg("gates"), 1)
                    empty_to_ev(n0 + 4 * g + m, u0 + 4 * g + m)

            def rows_of(name, l):
                for b in range(2):
                    empty(BASE[name][0] + b, slot["C"][:, b * G:b * G + G])

            act.dma_start(grow[:, :], a["g_post_mix_2"][0].partition_broadcast(P)).then_inc(sg("grow2"), 16)
            empty_all("out2", 4, token_dst("B"))
            emptied_with_squares(2, BASE["out2"][0] + 4)
            root("post2")
            rows_of("ga2_0", 2)
            for t in range(TT):
                square("norm3", t, h, tok["B"], sg("post2"), t + 1)
            root("norm3")
            turned_with_gain("norm3", gcol[:, 3, :], modc[:, 24:32])
            n0, _, u0, _ = BASE["ffn"]
            n, u = n0, u0
            for i in range(9):
                if i < 8:
                    for m in range(4):
                        empty_to_ev(n + m, u + m, ACT.Relu)
                    n, u = n + 4, u + 4
                if i > 0:
                    for m in range(8):
                        empty_to_ev(n + m, u + m)
                        if i == 8 and m > 4:
                            square("post3", m - 5, tok["B"], tok["D"], ev_free, u + m + 4)
                    n, u = n + 8, u + 8
                if i == 0:
                    act.dma_start(grow[:, :], a["g_post_ffn_2"][0].partition_broadcast(P)).then_inc(sg("grow3"), 16)
            square("post3", 3, tok["B"], tok["D"], ev_free, u + 4)
            root("post3")
            rows_of("ga2_1", 3)

        @block.vector
        def _(dve):
            V = Chain(dve, dve_self)
            dve.sem_inc(ev_free, 4)
            X = (xh, xl)
            Y = (yh, yl)

            def split(n, u, s, dst, k):
                dve.wait_ge(bank_free, n + 9)
                split_tile(ev[:, u % 4, :], s, dst, k).then_inc(ev_free, 1)

            def split_tile(src, s, dst, k):
                dve.tensor_copy(dst[0][:, k, :], src).then_inc(hi_done, 1)
                dve.wait_ge(hi_done, s + 1)
                return dve.tensor_tensor(dst[1][:, k, :], src, dst[0][:, k, :].bitcast(F32), ALU.subtract)

            def split_all(name, dst, tiles=KT, first=0):
                n0, _, u0, s0 = BASE[name]
                for k in range(tiles):
                    split(n0 + k, u0 + k, s0 + k, dst, first + k)

            def rstd(name):
                dve.wait_ge(sg(name + "_ss"), TT)
                dve.tensor_scalar(stat[:, 4:8], stat[:, 0:4], 1.0 / D, EPS, ALU.mult, ALU.add).then_inc(sg(name + "_var"), 1)
                dve.wait_ge(sg(name + "_sd"), 1)
                V.after(dve.reciprocal(stat[:, 12:16], stat[:, 8:12]))

            def norm(name):
                rstd(name)
                for t in range(TT):
                    dve.tensor_scalar(tok["D"][:, t, :], h[:, t, :], stat[:, 12 + t:13 + t], None, ALU.mult)\
                       .then_inc(sg(name + "_xn"), 1)

            def post(l, last=None):
                rstd(f"post{l}")
                dve.wait_ge(sg(f"grow{l}"), 16)
                if l >= 2:
                    dve.wait_ge(bank_free, BASE[f"ga2_{l - 2}"][0] + 10)
                    V.after(dve.tensor_tensor(grow[:, :], grow[:, :], slot["C"][:, 0:D], ALU.mult))
                for t in range(TT):
                    y = tok["B"][:, t, :]
                    V.after(dve.scalar_tensor_tensor(out=y, in0=y, scalar=stat[:, 12 + t:13 + t], in1=grow[:, :],
                                                     op0=ALU.mult, op1=ALU.mult))
                    dve.tensor_tensor(h[:, t, :], h[:, t, :], y, ALU.add).then_inc(last or sg(f"post{l}"), 1)

            def gated(name):
                n0, _, u0, s0 = BASE[name]
                for m in range(8):
                    dve.wait_ge(sg(name + "_silu"), m + 1)
                    dve.wait_ge(bank_free, n0 + m + 9)
                    e = ev[:, (u0 + m) % 4, :]
                    V.after(dve.tensor_tensor(e, e, feat["A"][:, m, :], ALU.mult))
                    split_tile(e, s0 + m, Y, m).then_inc(ev_free, 1)

            def out_and_ple(l):
                split_all(f"pt{l}", X, tiles=2, first=6)
                post(l)
                dve.wait_ge(sg(f"post{l}"), TT)
                split_all(f"ht{l}", X)
                n0, _, u0, _ = BASE[f"pg{l}"]
                for m in range(8):
                    n, t = divmod(m, 4)
                    dve.wait_ge(bank_free, n0 + m + 9)
                    e = ev[:, (u0 + m) % 4, :]
                    hh = h[:, t, n * G:n * G + G]
                    V.after(dve.tensor_tensor(e, e, tok["A"][:, t, n * G:n * G + G], ALU.mult))
                    V.after(dve.tensor_tensor(hh, hh, e, ALU.add))
                    dve.sem_inc(ev_free, 1)
                    dve.sem_inc(sg(f"pg{l}_h"), 1)

            def attention(x, pairs, src, strip, bias):
                per_turn = 16
                with dve.Fori(0, pairs // 2) as i:
                    V.enter(i, per_turn)

                    def stage(p):
                        if p == 0:
                            dve.sem_inc(apart, 1)
                        dve.tensor_copy(a_q[p], src[0][:, 2 * i + p, :])
                        dve.tensor_copy(a_k[p], src[1][:, 2 * i + p, :])
                        if bias:
                            for r in range(2):
                                dve.tensor_scalar(bias_q[2 * p + r][:, :], feat["D"][:, 7, :],
                                                  sel[:, bass.ds(4 * i + (2 * p + r), 1)], None, ALU.mult)
                        dve.tensor_copy(a_v[p], src[2][:, :, bass.ds(i * 2 * P + p * P, P)]).then_inc(sg(x + "_staged"), 1)

                    stage(0)
                    for t in range(20):
                        if t < 16:
                            b = t
                            kw = (b % 4 + 1) * P
                            dve.wait_ge(sg(x + "_scores"), 16 * i + (b + 1))
                            if b >= 3:
                                dve.wait_ge(sg(x + "_turned"), 16 * i + (b - 2))
                            dve.sem_inc(apart, 1)
                            dve.tensor_tensor_reduce(a_s[b % 3][:, 0:kw], ps[:, SB[b % 3], 0:kw], strip(b % 4), -1.0,
                                                     -NEG, ALU.add, ALU.min, nmax[:, b % 8:b % 8 + 1])\
                               .then_inc(sg(x + "_max"), 1)
                        if t == 3:
                            stage(1)
                        if t >= 4:
                            b = t - 4
                            q, o = b % 4, b % 8
                            dve.wait_ge(sg(x + "_exp"), 16 * i + (b + 1))
                            V.after(dve.reciprocal(rsum[:, o:o + 1], esum[:, o:o + 1]))
                            dve.wait_ge(sg(x + "_summed"), 16 * i + (b + 1))
                            dve.tensor_scalar(tok["C"][:, q, bass.ds(i * 2 * P + b // 4 * HD, HD)], ps[:, OB[b % 2], 0:HD],
                                              rsum[:, o:o + 1], None, ALU.mult).then_inc(sg(x + "_out"), 1)
                V.leave(pairs // 2)

            def modulation():
                dve.memset(one[:, :], 1.0)
                dve.wait_ge(sg("c_silu"), 1)
                for n in range(12):
                    acc = ada_acc[n]
                    for c in (2 * n, 2 * n + 1):
                        dve.wait_ge(sg(f"ada_landed{c % 3}"), 16 * (c // 3 + 1))
                        for k in range(4):
                            w = ada_w[c % 3][:, k, :]
                            s = stat[:, 40 + 4 * (c % 2) + k:41 + 4 * (c % 2) + k]
                            if c % 2 == 0 and k == 0:
                                V.after(dve.tensor_scalar(acc, w, s, None, ALU.mult))
                            else:
                                V.after(dve.scalar_tensor_tensor(out=acc, in0=w, scalar=s, in1=acc, op0=ALU.mult, op1=ALU.add))
                        dve.sem_inc(sg("ada_used"), 1)
                    dve.sem_inc(sg("ada_acc"), 1)
                dve.wait_ge(sg("ada_sum"), 1)
                V.after(dve.tensor_tensor(modc[:, :], modc[:, :], ps[:, 7, 0:48], ALU.add))
                for g, c in ((2, 8), (3, 32)):
                    dve.scalar_tensor_tensor(out=gcol[:, g, :], in0=modc[:, c:c + 8], scalar=1.0, in1=gcol[:, g, :],
                                             op0=ALU.add, op1=ALU.mult).then_inc(sg("gains2"), 1)

            dve.wait_ge(const_in, 16 * CONSTS)
            V.after(dve.tensor_tensor(lbc[:, 2, :], lbc[:, 0, :], lbc[:, 1, :], ALU.max))
            dve.tensor_tensor(lbc[:, 3, :], lbc[:, 0, :], lbc[:, 2, :], ALU.subtract)
            dve.tensor_tensor(lbc[:, 4, :], lbc[:, 1, :], lbc[:, 2, :], ALU.subtract).then_inc(sg("lb_sub"), 1)

            norm("norm0")
            split_all("norm0", X)
            modulation()
            dve.wait_ge(sg("fl_in"), 16)
            V.after(dve.tensor_copy(wsm_h[:, :, 0:16], wsm[:, :, 0:16]))
            V.after(dve.tensor_tensor(wsm_l[:, :, 0:16], wsm[:, :, 0:16], wsm_h[:, :, 0:16].bitcast(F32), ALU.subtract))
            dve.sem_inc(sg("fl_split"), 1)
            fr = ev[:, 0, :].rearrange("p (t c) -> p t c", t=TT)
            V.after(dve.memset(ev[:, 0, :], 0.0))
            dve.wait_ge(sg("fl_full"), 1)
            fp = ps[:, 0, 0:64].rearrange("p (t c) -> p t c", t=TT)
            for r in (0, 32, 64, 96):
                V.after(dve.tensor_copy(fr[:, :, r:r + 16], fp))
            dve.sem_inc(sg("fl_rows"), 1)
            dve.wait_ge(sg("fl_turned"), 1)
            C5, C6, C7 = (feat["D"][:, k, :] for k in (5, 6, 7))
            V.after(dve.memset(stat[:, 24:25], 0.0))
            for r in (0, 32, 64, 96):
                V.after(dve.tensor_copy(stat[r:r + 16, 24:25], bfc[r:r + 16, :]))
            V.after(dve.tensor_scalar(C7, ps[:, 1, :], stat[:, 24:25], None, ALU.add))
            dve.sem_inc(sg("fl_x"), 1)
            dve.wait_ge(sg("fl_ln"), 1)
            V.after(dve.tensor_scalar(C7, C7, 0.0, None, ALU.min))
            V.after(dve.tensor_tensor(C7, C7, C5, ALU.subtract))
            V.after(dve.tensor_tensor_scan(C6, C7, C7, 0.0, ALU.add, ALU.bypass))
            V.after(dve.tensor_copy(bias_k[:, :], C6))
            V.after(dve.tensor_tensor(C5, C6, bias_k[:, :].bitcast(F32), ALU.subtract))
            V.after(dve.tensor_copy(C7[0:32, :], bias_k[0:32, :].bitcast(F32)))
            V.after(dve.tensor_copy(C7[32:64, :], C5[32:64, :]))
            V.after(dve.memset(C7[64:128, :], -1.0))
            V.after(dve.tensor_copy(bias_k[96:128, :], C5[96:128, :]))
            V.after(dve.tensor_scalar(bias_k[0:64, :], C5[0:64, :], 0.0, 1.0, ALU.mult, ALU.add))
            attention("fox", 8, (feat["A"], feat["B"], tok["C"]), lambda q: mask[:, 384 - q * P:512], True)
            gated("at0")
            out_and_ple(0)

            dve.wait_ge(sg("lb_exp"), 1)
            V.after(dve.tensor_tensor(lbc[:, 0, :], lbc[:, 3, :], lbc[:, 4, :], ALU.add))
            V.after(dve.reciprocal(lbc[:, 1, :], lbc[:, 0, :]))
            V.after(dve.tensor_tensor(lbc[:, 3, :], lbc[:, 3, :], lbc[:, 1, :], ALU.mult))
            V.after(dve.tensor_tensor(lbc[:, 4, :], lbc[:, 4, :], lbc[:, 1, :], ALU.mult))
            V.after(dve.tensor_tensor(lbc[:, 1, :], lbc[:, 3, :], lbc[:, 4, :], ALU.add))
            V.after(dve.tensor_tensor(lbc[:, 1, :], lbc[:, 1, :], lbc[:, 3, :], ALU.subtract))
            V.after(dve.tensor_scalar(lbc[:, 0, :], lbc[:, 1, :], -1.0, 1.0, ALU.mult, ALU.add))
            V.after(dve.tensor_scalar(lbc[:, 5, :], lbc[:, 0, :], -1.0, None, ALU.mult))
            dve.wait_ge(sg("pg0_h"), 8)
            norm("norm1")
            split_all("norm1", X)
            n0, _, u0, _ = BASE["qfi1"]
            for m in range(8):
                dve.wait_ge(bank_free, n0 + 8 + m + 9)
                e = ev[:, (u0 + m) % 4, :]
                V.mark(dve.tensor_scalar(feat["B"][:, m, :], e, lbc[:, 0, m:m + 1], lbc[:, 1, m:m + 1], ALU.mult, ALU.add))
                V.after(dve.tensor_scalar(feat["C"][:, m, :], e, lbc[:, 5, m:m + 1], lbc[:, 0, m:m + 1], ALU.mult, ALU.add))
                dve.sem_inc(ev_free, 1)
                below = feat["B"][:, m, :]
                for w in (2, 4, 8, 16, 32, 64, 128):
                    pairs_ = below.rearrange("p (n c) -> p n c", c=2)
                    out = r_q[0][:, 0:256] if w == 2 else r_tree[:, m, TREE[w]:TREE[w] + T // w]
                    V.after(dve.tensor_tensor(out.unsqueeze(2), pairs_[:, :, 0:1], pairs_[:, :, 1:2], ALU.mult))
                    below = out
                dve.sem_inc(sg("f_ready"), 1)
            dve.wait_ge(sg("level_in"), 16)
            V.mark(dve.memset(r_sc[0], 0.0))
            V.after(dve.memset(r_sc[1], 0.0))
            dve.sem_inc(sg("lev_kept"), 2)
            with dve.Fori(0, 4) as i:
                V.enter(i, 2 + 2 * (1 + 7 * 2) + 16 + 6)

                def decay(e, s):
                    dve.wait_ge(sg("lev_used"), 16 * i + (2 * s + e - 1))
                    dve.sem_inc(apart, 1)
                    if s == 1:
                        V.after(dve.tensor_tensor(r_q[e], r_q[e], feat["B"][:, 2 * i + e, :], ALU.mult))
                        dve.sem_inc(sg("lev_qk"), 1)
                        return
                    half = 1 << (s - 2)
                    f = (feat["B"][:, 2 * i + e, :] if half == 1 else r_f2[e] if half == 2 else
                         r_tree[:, 2 * i + e, TREE[half]:TREE[half] + T // half])
                    f = f.rearrange("p (n c) -> p n c", c=2)
                    q, k = (x[e].rearrange("p (n c) -> p n c", c=2 * half) for x in (r_q, r_k))
                    lo, hi, shape = slice(0, half), slice(half, 2 * half), [P, T // (2 * half), half]
                    V.mark(dve.tensor_tensor(q[:, :, hi], q[:, :, hi], f[:, :, 0:1].broadcast_to(shape), ALU.mult))
                    V.after(dve.tensor_tensor(k[:, :, lo], k[:, :, lo], f[:, :, 1:2].broadcast_to(shape), ALU.mult))
                    dve.sem_inc(sg("lev_qk" if s < 8 else "kd_ready"), 1)

                def keep(e, s):
                    dve.wait_ge(sg("lev_used"), 16 * i + (2 * s + e + 1))
                    if s == 0:
                        dve.wait_ge(sg("rec_full"), 2 * i + (e + 1))
                    dve.sem_inc(apart, 1)
                    V.after(dve.copy_predicated(r_sc[e].rearrange("p (n c) -> p n c", c=P),
                                                level[:, s:s + 1, :].broadcast_to([P, TT, P]),
                                                ps[:, e, :].rearrange("p (n c) -> p n c", c=P)))
                    dve.sem_inc(sg("lev_kept"), 1)

                for e in range(2):
                    dve.sem_inc(apart, 1)
                    pairs_ = feat["B"][:, 2 * i + e, :].rearrange("p (n c) -> p n c", c=2)
                    V.after(dve.tensor_tensor(r_f2[e].unsqueeze(2), pairs_[:, :, 0:1], pairs_[:, :, 1:2], ALU.mult))
                for s in range(1, 9):
                    for e in range(2):
                        decay(e, s)
                        keep(e, s - 1)
                for e in range(2):
                    dve.wait_ge(sg("state_add"), 2 * i + (e + 1))
                    for j in range(TT - 1):
                        u = ps[:, 5 + e, j * P:j * P + P]
                        if j == 0:
                            V.after(dve.tensor_copy(r_st[e][0], u))
                        else:
                            V.after(dve.scalar_tensor_tensor(out=r_st[e][j], in0=r_st[e][j - 1],
                                                             scalar=r_tree[:, 2 * i + e, TREE[128] + j:TREE[128] + j + 1],
                                                             in1=u, op0=ALU.mult, op1=ALU.add))
                        dve.sem_inc(sg("state"), 1)
            V.leave(4)
            dve.wait_ge(sg("rec_out"), 8)
            V.after(dve.tensor_scalar(stat2[:, 0:32], stat2[:, 0:32], 1.0 / P, EPS, ALU.mult, ALU.add))
            dve.sem_inc(sg("o_var"), 1)
            dve.wait_ge(sg("o_sd"), 1)
            V.after(dve.reciprocal(stat2[:, 0:32], stat2[:, 0:32]))
            o4 = slot["D"][:, :].rearrange("p (t h d) -> p t h d", t=TT, h=8)
            r4 = stat2[:, 0:32].rearrange("p (h t) -> p t h", t=TT)
            for t in range(TT):
                V.after(dve.tensor_tensor(o4[:, t], o4[:, t], r4[:, t, :].unsqueeze(2).broadcast_to([P, 8, P]), ALU.mult))
            dve.sem_inc(sg("o_normed"), 1)
            gated("at1")
            out_and_ple(1)

            dve.wait_ge(sg("pg1_h"), 8)
            norm("norm2")
            split_all("norm2", X)
            dve.wait_ge(sg("ki_in"), 16)
            V.after(dve.tensor_copy(wsm_h[:, :, :], wsm))
            V.after(dve.tensor_tensor(wsm_l[:, :, :], wsm, wsm_h[:, :, :].bitcast(F32), ALU.subtract))
            dve.sem_inc(sg("ki_split"), 1)
            dve.wait_ge(sg("rope_in"), 64)

            def rope_group(n, u, dst):
                for m in range(4):
                    dve.wait_ge(bank_free, n + 4 + m + 9)
                    e = ev[:, (u + m) % 4, :]
                    V.mark(dve.tensor_tensor(dst(m), dst(m), rope[1], ALU.mult))
                    V.mark(dve.tensor_tensor(e, e, rope[0], ALU.mult))
                    V.wait()
                    V.after(dve.tensor_tensor(dst(m), dst(m), e, ALU.add))
                    dve.sem_inc(ev_free, 1)

            n0, _, u0, _ = BASE["qi2"]
            rope_group(n0, u0, lambda m: feat["A"][:, m, :])
            n0, _, u0, _ = BASE["qka2"]
            rope_group(n0, u0, lambda m: feat["B"][:, m, :])
            rope_group(n0 + 8, u0 + 4, lambda m: feat["B"][:, 4 + m, :])
            dve.wait_ge(sg("ki_full"), 1)
            smv = ev[:, 0, 0:288].rearrange("p (t c) -> p t c", t=TT)
            kr = ev[:, 1, :].rearrange("p (t c) -> p t c", t=TT)
            tmp = ev[:, 0, 288:352].rearrange("p (a t f) -> p a t f", a=2, t=TT)
            V.after(dve.tensor_copy(smv, ps[:, 0, 0:288].rearrange("p (t c) -> p t c", t=TT)))
            V.mark(dve.tensor_scalar(stat2[:, 0:32].rearrange("p (t h) -> p t h", t=TT), smv[:, :, 64:72], ISCALE, None, ALU.mult))
            V.mark(dve.tensor_copy(kr[:, :, 0:64], smv[:, :, 0:64]))
            x1, x2, cs, sn = smv[:, :, 0:8], smv[:, :, 8:16], rope_t[:, 0], rope_t[:, 1]
            V.mark(dve.tensor_tensor(tmp[:, 0], x2, sn, ALU.mult))
            V.mark(dve.tensor_tensor(tmp[:, 1], x1, sn, ALU.mult))
            V.wait()
            V.mark(dve.tensor_tensor(kr[:, :, 0:8], x1, cs, ALU.mult))
            V.mark(dve.tensor_tensor(kr[:, :, 8:16], x2, cs, ALU.mult))
            V.wait()
            V.mark(dve.tensor_tensor(kr[:, :, 0:8], kr[:, :, 0:8], tmp[:, 0], ALU.subtract))
            V.mark(dve.tensor_tensor(kr[:, :, 8:16], kr[:, :, 8:16], tmp[:, 1], ALU.add))
            V.wait()
            V.after(dve.tensor_copy(kr[:, :, 64:128], kr[:, :, 0:64]))
            dve.sem_inc(sg("ki_rows"), 1)
            dve.wait_ge(sg("ki_turned"), 1)
            V.after(dve.tensor_copy(ev[:, 2, :], ps[:, 1, :]))
            dve.sem_inc(sg("ki_ready"), 1)
            rt = [ev[:, 3, :], ev[:, 0, :]]
            for q in range(TT):
                kw = (q + 1) * P
                strip = isc[:, KOFF[q]:KOFF[q] + kw]
                for hh in range(8):
                    b = 8 * q + hh
                    dve.wait_ge(sg("idx_relu"), b + 1)
                    V.after(dve.scalar_tensor_tensor(out=strip, in0=rt[b % 2][:, 0:kw],
                                                     scalar=stat2[:, 8 * q + hh:8 * q + hh + 1],
                                                     in1=mask[:, 384 - q * P:512] if hh == 0 else strip,
                                                     op0=ALU.mult, op1=ALU.add))
                    dve.sem_inc(sg("idx_acc"), 1)
            dve.wait_ge(sg("idx_relu"), 32)
            tw, eq = slot["A"][:, 0:512], slot["A"][:, 512:1024]
            V.after(dve.tensor_copy(isc[:, 0:P], mask[:, 384:512]))
            for q in range(1, TT):
                kw = (q + 1) * P
                strip, w, e = isc[:, KOFF[q]:KOFF[q] + kw], tw[:, 0:kw], eq[:, 0:kw]
                V.after(dve.tensor_copy(w, strip))
                for r in range(TOPK // 8):
                    V.after(dve.max(m8[:, :], w))
                    if r < TOPK // 8 - 1:
                        V.after(dve.match_replace(w, m8[:, :], w, NEG))
                V.after(dve.tensor_scalar(e, strip, m8[:, 7:8], None, ALU.is_equal))
                V.after(dve.tensor_scalar(w, strip, m8[:, 7:8], None, ALU.is_gt))
                V.after(dve.tensor_reduce(stat[:, 24:25], w, AX.X, ALU.add))
                V.after(dve.tensor_scalar(stat[:, 25:26], stat[:, 24:25], -1.0, float(TOPK), ALU.mult, ALU.add))
                V.after(dve.tensor_tensor_scan(strip, e, e, 0.0, ALU.add, ALU.bypass))
                V.after(dve.scalar_tensor_tensor(out=e, in0=strip, scalar=stat[:, 25:26], in1=e, op0=ALU.is_le, op1=ALU.mult))
                V.after(dve.tensor_tensor(w, w, e, ALU.add))
                V.after(dve.tensor_scalar(strip, w, 1.0, -NEG, ALU.subtract, ALU.mult))
            dve.wait_ge(bank_free, BASE["at2"][0] + 8)

            attention("top", 4, (feat["B"], feat["B"][:, 4:8, :], tok["C"]), lambda q: isc[:, KOFF[q]:KOFF[q] + (q + 1) * P],
                      False)
            split_all("at2", Y, tiles=4)

            dve.wait_ge(sg("tri_in"), 16)
            dve.sem_inc(sg("gb2_free"), 1)

            qs, ks, vs = ev[:, 0, :], ev[:, 1, :], ev[:, 2, :].rearrange("p (t d) -> p t d", t=TT)

            def diagonals(x, u):
                return x.rearrange("p (a c) -> p a c", a=2)[:, :, 0:P] if u == 2 else x[:, 0:P].unsqueeze(1)

            def each(mask_, u):
                return mask_.unsqueeze(1).broadcast_to([P, 2 if u == 2 else 1, P])

            with dve.Fori(0, 4) as i:
                V.enter(i, 13)
                dve.sem_inc(apart, 1)
                dve.tensor_copy(qs, feat["D"][:, i, :])
                dve.tensor_copy(ks, feat["D"][:, i + 4, :])
                dve.tensor_copy(vs, tok["C"][:, :, bass.ds(i * P + G, P)]).then_inc(sg("stk_staged"), 1)
                dve.wait_ge(sg("gb2_full"), 2 * i + 1)
                dve.sem_inc(apart, 1)
                dve.tensor_copy(feat["D"][:, i, :], ps[:, 7, :]).then_inc(sg("gb2_free"), 1)
                for e in range(2):
                    for u in (2, 1, 0):
                        dve.wait_ge(sg("stk_ln"), 6 * i + (3 * e + 3 - u))
                        x, w = stk_sp[e][u], STK_COLS[u]
                        V.after(dve.scalar_tensor_tensor(out=x[:, 0:w], in0=ps[:, 3 * e + u, 0:w], scalar=0.0,
                                                         in1=x[:, 0:w], op0=ALU.max, op1=ALU.add))
                        V.after(dve.tensor_tensor(diagonals(x, u), diagonals(x, u), each(strict, u), ALU.mult))
                        dve.sem_inc(sg("stk_sp"), 1)
                for e in range(2):
                    for u in (2, 1, 0):
                        dve.wait_ge(sg("stk_r"), 6 * i + (3 * e + 3 - u))
                        x = diagonals(ps[:, 3 * e + u, :], u)
                        dve.tensor_tensor(x, x, each(strict_neg, u), ALU.add).then_inc(sg("stk_arg"), 1)
                dve.wait_ge(sg("gb2_full"), 2 * i + 2)
                dve.sem_inc(apart, 1)
                dve.tensor_copy(feat["D"][:, i + 4, :], ps[:, 7, :]).then_inc(sg("gb2_free"), 1)
                dve.wait_ge(sg("stk_o"), 2 * i + 2)
                dve.sem_inc(apart, 1)
                V.after(dve.tensor_copy(yh[:, i + 4, :], ps[:, 6, :]))
                dve.sem_inc(apart, 1)
                dve.tensor_tensor(yl[:, i + 4, :], ps[:, 6, :], yh[:, i + 4, :].bitcast(F32), ALU.subtract)\
                   .then_inc(sg("stk_out"), 1)
            V.leave(4)

            n0, _, u0, s0 = BASE["merge2"]
            for g in range(4):
                for m in range(4):
                    k = 4 * (g // 2) + m
                    dve.wait_ge(bank_free, n0 + 4 * g + m + 9)
                    dve.wait_ge(sg("gates"), KT + (k + 1 if g % 2 else 4 * (g // 2)))
                    e, ya = ev[:, (u0 + 4 * g + m) % 4, :], feat["B"][:, GATE_A[k], :]
                    if g % 2 == 0:
                        V.after(dve.tensor_tensor(ya, e, ya, ALU.mult))
                    else:
                        V.after(dve.tensor_tensor(e, e, feat["D"][:, GATE_B[k], :], ALU.mult))
                        V.after(dve.tensor_tensor(e, ya, e, ALU.add))
                        split_tile(e, s0 + k, X, k).then_inc(sg("merged"), 1)
                        dve.wait_ge(sg("merged"), k + 1)
                    dve.sem_inc(ev_free, 1)
            post(2)
            dve.wait_ge(sg("post2"), TT)
            norm("norm3")
            split_all("norm3", X)
            n0, _, u0, s0 = BASE["ffn"]
            n, u, s = n0, u0, s0
            for i in range(9):
                if i < 8:
                    for m in range(4):
                        dve.wait_ge(bank_free, n + m + 9)
                        e = ev[:, (u + m) % 4, :]
                        V.after(dve.tensor_tensor(e, e, e, ALU.mult))
                        split_tile(e, s + m, Y, 4 * (i % 2) + m).then_inc(ev_free, 1)
                    n, u, s = n + 4, u + 4, s + 4
                if i > 0:
                    for m in range(8):
                        dve.wait_ge(bank_free, n + m + 9)
                        e = ev[:, (u + m) % 4, :]
                        y = tok["B"][:, m % 4, (m // 4) * G:(m // 4) * G + G]
                        if i == 1:
                            V.after(dve.tensor_copy(y, e))
                        else:
                            V.after(dve.tensor_tensor(y, y, e, ALU.add))
                        dve.sem_inc(ev_free, 1)
                    n, u = n + 8, u + 8
            post(3, last=sg("final"))


def constants():
    i = np.arange(P)
    causal = np.zeros((P, T), np.float32)
    causal[:, 384:] = np.where(i[None, :] > i[:, None], NEG, 0.0)
    sel = np.zeros((P, 16), np.float32)
    for x in range(16):
        sel[x::32, x] = 1.0
    s, t = i[:, None], i[None, :]
    levels = np.zeros((P, 8, P), np.float32)
    for l in range(1, 8):
        half = 1 << (l - 1)
        levels[:, l] = (s // (2 * half) == t // (2 * half)) & (s % (2 * half) < half) & (t % (2 * half) >= half)
    levels[:, 0] = s == t
    stick = np.concatenate([-(s >= t).astype(np.float32), -np.ones((P, P), np.float32), (s < t).astype(np.float32),
                            np.where(s < t, 0.0, NEG).astype(np.float32)], axis=1)
    pos = np.arange(T, dtype=np.float32)
    freq = np.float32(500000.0) ** (-np.arange(0, 16, 2, dtype=np.float32) / np.float32(16))
    ang = pos[:, None] * freq[None, :].astype(np.float32)
    cos, sin = np.cos(ang).astype(np.float32), np.sin(ang).astype(np.float32)
    fcos, fsin, perm = np.ones((P, T), np.float32), np.zeros((P, T), np.float32), np.zeros((P, P), np.float32)
    for base in (0, 64):
        for f in range(8):
            fcos[base + f] = fcos[base + 8 + f] = cos[:, f]
            fsin[base + f], fsin[base + 8 + f] = -sin[:, f], sin[:, f]
            perm[base + 8 + f, base + f] = perm[base + f, base + 8 + f] = 1.0
    rope_t = np.stack([x.reshape(TT, P, 8).transpose(1, 0, 2) for x in (cos, sin)], axis=1).reshape(P, 64)
    return {
        "c_ident": np.eye(P, dtype=np.float32), "c_mask": causal, "c_sel": sel, "c_levels": levels.reshape(P, 8 * P),
        "c_stick": stick, "c_cos": fcos, "c_sin": fsin, "c_perm": perm, "c_rope_t": np.ascontiguousarray(rope_t),
    }


INPUTS = ["x", "p", "norm_pre", "norm_post", "att_w_in", "att_b_f", "att_w_out", "rec_w_in", "rec_lb", "rec_out_norm",
          "rec_w_out", "ple_w_proj", "ple_w_gate", "c_2", "w_ada_2", "b_ada_2", "g_pre_mix_2", "w_in_2", "w_up_a_2",
          "w_up_b_2", "w_out_2", "g_post_mix_2", "g_pre_ffn_2", "w_ff1_2", "w_ff2_2", "g_post_ffn_2"]


def kernel(**inputs):
    import concourse.bacc as bacc
    from concourse.bass_utils import run_bass_kernel_spmd

    nc = bacc.Bacc("TRN2", target_bir_lowering=False, num_devices=1)
    arrays = {name: np.ascontiguousarray(inputs[name]) for name in INPUTS}
    arrays.update(constants())
    aps = {name: nc.dram_tensor(name + "_dram", x.shape, mybir.dt.from_np(x.dtype), kind="ExternalInput").ap()
           for name, x in arrays.items()}
    aps["out"] = nc.dram_tensor("out_dram", (1, T, D), F32, kind="ExternalOutput").ap()
    build(nc, aps)
    r = run_bass_kernel_spmd(nc, [{name + "_dram": x for name, x in arrays.items()}], core_ids=[0])
    return r.results[0]["out_dram"]
```
